# Optimizing a Trainium2 kernel written in Bass

```python
import jax, jax.numpy as jnp
from jax import lax
import numpy as np

D_MODEL = 1024
BATCH = 1
SEQ = 1024
DEPTH = 1

NSA_HEADS = 8
NSA_KV_GROUPS = 2
NSA_HEAD_DIM = 64
NSA_WIDTH = NSA_HEADS * NSA_HEAD_DIM
NSA_KV_DIM = NSA_KV_GROUPS * NSA_HEAD_DIM
CMP_LEN = 32
CMP_STRIDE = 16
CMP_HIDDEN = 64
SEL_BLOCK = 64
SEL_TOPK = 16
WINDOW = 512
Q_BLOCK = 128
FORCE_BONUS = 1.0e4
MLSTM_HEADS = 4
MLSTM_HEAD_DIM = 128
MLSTM_WIDTH = MLSTM_HEADS * MLSTM_HEAD_DIM
MLSTM_CONV = 4
MLSTM_CHUNK = 64
IN_SIZES = (NSA_WIDTH, NSA_KV_DIM, NSA_KV_DIM, NSA_KV_DIM, NSA_KV_DIM, NSA_KV_DIM, NSA_KV_DIM, NSA_HEADS * 3,
            MLSTM_WIDTH, MLSTM_WIDTH, MLSTM_WIDTH, MLSTM_WIDTH, MLSTM_HEADS, MLSTM_HEADS)
D_IN = 3360
MIX_WIDTH = NSA_WIDTH + MLSTM_WIDTH
MEM_LEN = 256
MEM_HEADS = 4
MEM_HEAD_DIM = D_MODEL // MEM_HEADS
D_FF = 2816
FFN_CONV = 3
EPS = 1e-6

kernel_name = 'hymba_nsa_mlstm_convffn_block'

def rmsnorm(x, g):
    xf = x.astype(jnp.float32)
    y = xf * lax.rsqrt(jnp.mean(xf * xf, axis=-1, keepdims=True) + EPS)
    return (y * g.astype(jnp.float32)).astype(x.dtype)

def head_rmsnorm(x, g):
    B, S, NH, dh = x.shape
    return rmsnorm(x, g.reshape(NH, dh)).reshape(B, S, NH * dh)

def causal_dwconv(x, w):
    K, C = w.shape
    return lax.conv_general_dilated(x, w[:, None, :].astype(x.dtype), window_strides=(1,), padding=[(K - 1, 0)],
                                    dimension_numbers=('NWC', 'WIO', 'NWC'), feature_group_count=C)

def split_cols(a, sizes):
    return jnp.split(a, np.cumsum(np.array(sizes))[:-1].tolist(), axis=-1)

def masked_softmax(s, mask):
    s = jnp.where(mask, s.astype(jnp.float32), -1e30)
    return jax.nn.softmax(s, axis=-1) * mask

def compress_blocks(kv, pos, w1, w2):
    S, G, dh = kv.shape
    n_cmp = (S - CMP_LEN) // CMP_STRIDE + 1
    idx = jnp.arange(n_cmp)[:, None] * CMP_STRIDE + jnp.arange(CMP_LEN)[None, :]
    blocks = kv[idx] + pos[None, :, None, :]
    flat = blocks.transpose(0, 2, 1, 3).reshape(n_cmp, G, CMP_LEN * dh)
    return jax.nn.gelu(flat @ w1, approximate=False) @ w2

def nsa_mixer(q, k_cmp, v_cmp, k_sel, v_sel, k_win, v_win, gates, pos_k, w1_k, w2_k, pos_v, w1_v, w2_v):
    S = q.shape[0]
    G, HPG, dh = NSA_KV_GROUPS, NSA_HEADS // NSA_KV_GROUPS, NSA_HEAD_DIM
    scale = dh ** -0.5
    kc = compress_blocks(k_cmp, pos_k, w1_k, w2_k)
    vc = compress_blocks(v_cmp, pos_v, w1_v, w2_v)
    n_cmp = kc.shape[0]
    cmp_start = jnp.arange(n_cmp) * CMP_STRIDE
    cmp_end = cmp_start + (CMP_LEN - 1)
    n_sel = S // SEL_BLOCK
    top_k = min(SEL_TOPK, n_sel)
    sel_start = jnp.arange(n_sel) * SEL_BLOCK
    overlap = ((cmp_start[:, None] < sel_start[None, :] + SEL_BLOCK) &
               (cmp_start[:, None] + CMP_LEN > sel_start[None, :])).astype(jnp.float32)
    ks_blocks = k_sel.reshape(n_sel, SEL_BLOCK, G, dh).transpose(2, 0, 1, 3)
    vs_blocks = v_sel.reshape(n_sel, SEL_BLOCK, G, dh).transpose(2, 0, 1, 3)
    kw_pad = jnp.pad(k_win, ((WINDOW, 0), (0, 0), (0, 0)))
    vw_pad = jnp.pad(v_win, ((WINDOW, 0), (0, 0), (0, 0)))
    g_idx = jnp.arange(G)[None, :, None]
    blk_ids = jnp.arange(n_sel)[None, None, :]
    tok_off = jnp.arange(SEL_BLOCK)
    win_off = jnp.arange(Q_BLOCK + WINDOW) - WINDOW

    def block(qb):
        t0 = qb * Q_BLOCK
        tpos = t0 + jnp.arange(Q_BLOCK)
        qg = lax.dynamic_slice_in_dim(q, t0, Q_BLOCK, 0).reshape(Q_BLOCK, G, HPG, dh) * scale
        gb = lax.dynamic_slice_in_dim(gates, t0, Q_BLOCK, 0).reshape(Q_BLOCK, G, HPG, 3)
        mask_c = (cmp_end[None, :] <= tpos[:, None])[:, None, None, :]
        p_c = masked_softmax(jnp.einsum('tghd,cgd->tghc', qg, kc), mask_c)
        o_c = jnp.einsum('tghc,cgd->tghd', p_c.astype(vc.dtype), vc)
        imp = jnp.einsum('tghc,cb->tgb', p_c, overlap)
        cur = (tpos // SEL_BLOCK)[:, None, None]
        forced = (blk_ids == 0) | (blk_ids == cur) | (blk_ids == cur - 1)
        score = jnp.where(blk_ids <= cur, imp + jnp.where(forced, FORCE_BONUS, 0.0), -FORCE_BONUS)
        _, sel = lax.top_k(score, top_k)
        kg = ks_blocks[g_idx, sel]
        vg = vs_blocks[g_idx, sel]
        tok = sel[..., None] * SEL_BLOCK + tok_off
        mask_s = (tok <= tpos[:, None, None, None]).reshape(Q_BLOCK, G, 1, top_k * SEL_BLOCK)
        s_s = jnp.einsum('tghd,tgkpd->tghkp', qg, kg).reshape(Q_BLOCK, G, HPG, top_k * SEL_BLOCK)
        p_s = masked_softmax(s_s, mask_s).reshape(Q_BLOCK, G, HPG, top_k, SEL_BLOCK)
        o_s = jnp.einsum('tghkp,tgkpd->tghd', p_s.astype(vg.dtype), vg)
        kw = lax.dynamic_slice_in_dim(kw_pad, t0, Q_BLOCK + WINDOW, 0)
        vw = lax.dynamic_slice_in_dim(vw_pad, t0, Q_BLOCK + WINDOW, 0)
        kpos = t0 + win_off
        mask_w = ((kpos[None, :] <= tpos[:, None]) & (kpos[None, :] > tpos[:, None] - WINDOW) &
                  (kpos[None, :] >= 0))[:, None, None, :]
        p_w = masked_softmax(jnp.einsum('tghd,wgd->tghw', qg, kw), mask_w)
        o_w = jnp.einsum('tghw,wgd->tghd', p_w.astype(vw.dtype), vw)
        o = gb[..., 0:1] * o_c + gb[..., 1:2] * o_s + gb[..., 2:3] * o_w
        return o.reshape(Q_BLOCK, NSA_HEADS, dh)

    out = lax.map(block, jnp.arange(S // Q_BLOCK))
    return out.reshape(S, NSA_HEADS, dh)

def mlstm_chunkwise(q, k, v, i_pre, f_pre):
    B, S, NH, dh = q.shape
    L = MLSTM_CHUNK
    nc = S // L
    f32 = jnp.float32
    to_c = lambda a: a.astype(f32).reshape(B, nc, L, NH, -1).transpose(1, 0, 3, 2, 4)
    to_cg = lambda a: a.astype(f32).reshape(B, nc, L, NH).transpose(1, 0, 3, 2)
    qc, kc, vc = to_c(q * dh ** -0.5), to_c(k), to_c(v)
    ic, lfc = to_cg(i_pre), to_cg(jax.nn.log_sigmoid(f_pre.astype(f32)))
    causal = jnp.tril(jnp.ones((L, L), dtype=bool))

    def step(carry, inp):
        C, n, m = carry
        qq, kk, vv, ii, lf = inp
        b = jnp.cumsum(lf, axis=-1)
        D = jnp.where(causal, b[..., :, None] - b[..., None, :] + ii[..., None, :], -jnp.inf)
        m_inter = b + m[..., None]
        m_t = jnp.maximum(jnp.max(D, axis=-1), m_inter)
        a_inter = jnp.exp(m_inter - m_t)
        sc = jnp.einsum('bhtd,bhsd->bhts', qq, kk) * jnp.exp(D - m_t[..., None])
        num = a_inter[..., None] * jnp.einsum('bhtd,bhde->bhte', qq, C) + jnp.einsum('bhts,bhse->bhte', sc, vv)
        den = a_inter * jnp.einsum('bhtd,bhd->bht', qq, n) + jnp.sum(sc, axis=-1)
        h = num / jnp.maximum(jnp.abs(den), jnp.exp(-m_t))[..., None]
        bL = b[..., -1]
        g_s = bL[..., None] - b + ii
        m_new = jnp.maximum(bL + m, jnp.max(g_s, axis=-1))
        w_s = jnp.exp(g_s - m_new[..., None])
        decay = jnp.exp(bL + m - m_new)
        C_new = decay[..., None, None] * C + jnp.einsum('bhs,bhsd,bhse->bhde', w_s, kk, vv)
        n_new = decay[..., None] * n + jnp.einsum('bhs,bhsd->bhd', w_s, kk)
        return (C_new, n_new, m_new), h

    init = (jnp.zeros((B, NH, dh, dh), f32), jnp.zeros((B, NH, dh), f32), jnp.zeros((B, NH), f32))
    _, h = lax.scan(step, init, (qc, kc, vc, ic, lfc))
    return h.transpose(1, 0, 3, 2, 4).reshape(B, S, NH, dh).astype(q.dtype)

def setup_inputs(seed: int = 0) -> dict:
    key = jax.random.key(seed)
    ks = jax.random.split(key, 32)
    f32 = jnp.float32
    nrm = lambda k, shape, s: jax.random.normal(k, shape, f32) * s
    gain = lambda k, shape: 1.0 + 0.02 * jax.random.normal(k, shape, f32)
    L = DEPTH
    return {
        'x': nrm(ks[0], (BATCH, SEQ, D_MODEL), 1.0),
        'mem': nrm(ks[1], (BATCH, MEM_LEN, D_MODEL), 1.0),
        'g_mix': gain(ks[2], (L, D_MODEL)),
        'w_in': nrm(ks[3], (L, D_MODEL, D_IN), D_MODEL ** -0.5),
        'cmp_pos_k': nrm(ks[4], (L, CMP_LEN, NSA_HEAD_DIM), 0.02),
        'cmp_w1_k': nrm(ks[5], (L, CMP_LEN * NSA_HEAD_DIM, CMP_HIDDEN), (CMP_LEN * NSA_HEAD_DIM) ** -0.5),
        'cmp_w2_k': nrm(ks[6], (L, CMP_HIDDEN, NSA_HEAD_DIM), CMP_HIDDEN ** -0.5),
        'cmp_pos_v': nrm(ks[7], (L, CMP_LEN, NSA_HEAD_DIM), 0.02),
        'cmp_w1_v': nrm(ks[8], (L, CMP_LEN * NSA_HEAD_DIM, CMP_HIDDEN), (CMP_LEN * NSA_HEAD_DIM) ** -0.5),
        'cmp_w2_v': nrm(ks[9], (L, CMP_HIDDEN, NSA_HEAD_DIM), CMP_HIDDEN ** -0.5),
        'mlstm_conv_w': nrm(ks[10], (L, MLSTM_CONV, 2 * MLSTM_WIDTH), MLSTM_CONV ** -0.5),
        'mlstm_b_i': nrm(ks[11], (L, MLSTM_HEADS), 0.1),
        'mlstm_b_f': jnp.linspace(3.0, 6.0, MLSTM_HEADS, dtype=f32)[None, :] + nrm(ks[12], (L, MLSTM_HEADS), 0.1),
        'g_head_nsa': gain(ks[13], (L, NSA_WIDTH)),
        'g_head_mlstm': gain(ks[14], (L, MLSTM_WIDTH)),
        'w_out': nrm(ks[15], (L, MIX_WIDTH, D_MODEL), MIX_WIDTH ** -0.5),
        'g_mem_q': gain(ks[16], (L, D_MODEL)),
        'g_mem_kv': gain(ks[17], (L, D_MODEL)),
        'w_mem_q': nrm(ks[18], (L, D_MODEL, D_MODEL), D_MODEL ** -0.5),
        'w_mem_k': nrm(ks[19], (L, D_MODEL, D_MODEL), D_MODEL ** -0.5),
        'w_mem_v': nrm(ks[20], (L, D_MODEL, D_MODEL), D_MODEL ** -0.5),
        'w_mem_o': nrm(ks[21], (L, D_MODEL, D_MODEL), D_MODEL ** -0.5),
        'g_ffn': gain(ks[22], (L, D_MODEL)),
        'w_up': nrm(ks[23], (L, D_MODEL, 2 * D_FF), D_MODEL ** -0.5),
        'ffn_conv_w': nrm(ks[24], (L, FFN_CONV, 2 * D_FF), FFN_CONV ** -0.5),
        'w_down': nrm(ks[25], (L, D_FF, D_MODEL), D_FF ** -0.5),
        'g_final': gain(ks[26], (D_MODEL,)),
    }

def reference(x, mem, g_mix, w_in, cmp_pos_k, cmp_w1_k, cmp_w2_k, cmp_pos_v, cmp_w1_v, cmp_w2_v,
              mlstm_conv_w, mlstm_b_i, mlstm_b_f, g_head_nsa, g_head_mlstm, w_out,
              g_mem_q, g_mem_kv, w_mem_q, w_mem_k, w_mem_v, w_mem_o,
              g_ffn, w_up, ffn_conv_w, w_down, g_final):
    B, S, _ = x.shape
    M = mem.shape[1]
    nsa_batched = jax.vmap(nsa_mixer, in_axes=(0,) * 8 + (None,) * 6)
    for l in range(DEPTH):
        h = rmsnorm(x, g_mix[l])
        (nq, nkc, nvc, nks, nvs, nkw, nvw, ngt, mq, mk, mv, mo, mi, mf) = split_cols(h @ w_in[l], IN_SIZES)
        kv4 = lambda a: a.reshape(B, S, NSA_KV_GROUPS, NSA_HEAD_DIM)
        o_nsa = nsa_batched(nq.reshape(B, S, NSA_HEADS, NSA_HEAD_DIM), kv4(nkc), kv4(nvc), kv4(nks), kv4(nvs),
                            kv4(nkw), kv4(nvw), jax.nn.sigmoid(ngt).reshape(B, S, NSA_HEADS, 3),
                            cmp_pos_k[l], cmp_w1_k[l], cmp_w2_k[l], cmp_pos_v[l], cmp_w1_v[l], cmp_w2_v[l])
        qk = jax.nn.silu(causal_dwconv(jnp.concatenate([mq, mk], axis=-1), mlstm_conv_w[l]))
        mq, mk = jnp.split(qk, 2, axis=-1)
        hd4 = lambda a: a.reshape(B, S, MLSTM_HEADS, MLSTM_HEAD_DIM)
        h_m = mlstm_chunkwise(hd4(mq), hd4(mk), hd4(mv), mi + mlstm_b_i[l], mf + mlstm_b_f[l])
        mixed = jnp.concatenate([head_rmsnorm(o_nsa, g_head_nsa[l]),
                                 jax.nn.sigmoid(mo) * head_rmsnorm(h_m, g_head_mlstm[l])], axis=-1)
        x = x + mixed @ w_out[l]
        hq = rmsnorm(x, g_mem_q[l])
        hm = rmsnorm(mem, g_mem_kv[l])
        q = (hq @ w_mem_q[l]).reshape(B, S, MEM_HEADS, MEM_HEAD_DIM)
        k = (hm @ w_mem_k[l]).reshape(B, M, MEM_HEADS, MEM_HEAD_DIM)
        v = (hm @ w_mem_v[l]).reshape(B, M, MEM_HEADS, MEM_HEAD_DIM)
        s = jnp.einsum('bshd,bmhd->bhsm', q, k).astype(jnp.float32) * (MEM_HEAD_DIM ** -0.5)
        p = jax.nn.softmax(s, axis=-1).astype(v.dtype)
        x = x + jnp.einsum('bhsm,bmhd->bshd', p, v).reshape(B, S, D_MODEL) @ w_mem_o[l]
        hf = rmsnorm(x, g_ffn[l])
        u = causal_dwconv(hf @ w_up[l], ffn_conv_w[l])
        a, b = jnp.split(u, 2, axis=-1)
        x = x + (jax.nn.gelu(a, approximate=False) * b) @ w_down[l]
    return rmsnorm(x, g_final)


_drawn_inputs = setup_inputs


def setup_inputs(seed=0):
    import zlib

    import numpy as np

    out = dict(_drawn_inputs(seed))
    spreads = {}
    factors = {'g_mix': 3.262,
     'cmp_pos_k': 8.0,
     'cmp_pos_v': 3.237,
     'mlstm_b_i': 8.0,
     'g_head_nsa': 4.421,
     'g_head_mlstm': 8.0,
     'g_mem_q': 8.0,
     'g_mem_kv': 8.0,
     'g_ffn': 4.22,
     'g_final': 2.829}
    for name, (base, spread) in spreads.items():
        noise = np.random.default_rng([zlib.crc32(name.encode()), seed]).standard_normal(out[name].shape)
        drawn = base * np.exp(spread * noise) if base else spread * noise
        out[name] = __import__('jax').numpy.asarray(drawn.astype(out[name].dtype))
    for name, factor in factors.items():
        out[name] = (out[name] * factor).astype(out[name].dtype)
    return out
```

```python
from contextlib import ExitStack, contextmanager

import concourse.bass as bass
from concourse import mybir

FP32 = mybir.dt.float32
FP32R = mybir.dt.float32r
ACT = mybir.ActivationFunctionType
ALU = mybir.AluOpType
AX = mybir.AxisListType

P = 128
D = 1024
SEQ = 1024
KT = D // P
TT = SEQ // P
HALF = 512
NH, G, DH = 8, 2, 64
CMP_LEN, CMP_STRIDE, CMP_HID = 32, 16, 64
NCMP = (SEQ - CMP_LEN) // CMP_STRIDE + 1
WT = 512 // P
MH, MDH, TAPS = 4, 128, 4
MEMT = 256 // P
MEM = 256
XH, XDH = 4, 256
FF = 2816
FT = FF // P
FTAPS = 3
EPS = 1e-6
NEG = -1e30
C_Q, C_KC, C_VC, C_KS, C_VS, C_KW, C_VW, C_GT = 0, 512, 640, 768, 896, 1024, 1152, 1280
C_MQ, C_MK, C_MV, C_MO, C_MI, C_MF = 1304, 1816, 2328, 2840, 3352, 3356
R_I, R_F = 32, 64


PARAM_LOADS = 18
JOBS = 2 * 2 * TT


def job_of(j):
    return j // (2 * TT), (j // 2) % TT, j % 2


def has_second(j):
    _, i, br = job_of(j)
    return br == 1 or i >= 4


X_ORDER = [("s", 0), ("s", 1), ("s", 2), ("s", 3), ("t", 0), ("s", 4), ("s", 5), ("t", 2),
           ("s", 6), ("s", 7), ("t", 4), ("t", 6)]
JOBS_1 = sum(has_second(j) for j in range(JOBS))


class Tally:

    def __init__(self, sem, step=1):
        self.sem, self.step, self.n, self.loops = sem, step, 0, []

    def add(self, k=1):
        self.n += k

    def value(self, behind=0):
        v = (self.n - behind) * self.step
        assert v > 0
        for i, per in self.loops:
            v = i * (per * self.step) + v
        return v

    def past(self, k):
        return bool(self.loops) or self.n > k

    def next(self):
        self.n += 1
        return self.value()

    def up(self, k=1):
        self.n += k
        return self.step * k


@contextmanager
def engine_loop(eng, turns, per_turn):
    with eng.Fori(0, turns) as i:
        began = {t: t.n for t, _ in per_turn}
        for t, per in per_turn:
            t.loops.append((i, per))
        yield i
        off = [(t.sem, t.n - began[t], per) for t, per in per_turn if t.n - began[t] != per]
        assert not off, off
        for t, per in per_turn:
            t.loops.pop()
            t.n = began[t] + per * turns


def build(nc, x, mem, g_mix, w_in, cmp_pos_k, cmp_w1_k, cmp_w2_k, cmp_pos_v, cmp_w1_v, cmp_w2_v,
          mlstm_conv_w, mlstm_b_i, mlstm_b_f, g_head_nsa, g_head_mlstm, w_out, g_mem_q, g_mem_kv,
          w_mem_q, w_mem_k, w_mem_v, w_mem_o, g_ffn, w_up, ffn_conv_w, w_down, g_final, out):
    ctx = ExitStack()
    with ctx:
        KB = 1024
        BASE = 16 * KB + 128
        END = 229344

        def at(name, offset, shape, dt=FP32):
            size = 4
            for s in shape[1:]:
                size *= s
            assert BASE + offset + size <= END, (name, BASE + offset + size - END)
            return nc.alloc_sbuf_tensor_at(name, shape, dt, offset=BASE + offset)

        cursor = [0]

        def keep(name, shape, dt=FP32):
            size = 4
            for s in shape[1:]:
                size *= s
            t = at(name, cursor[0], shape, dt)
            cursor[0] += (size + 31) // 32 * 32
            return t

        h_hi = keep("h_hi", [P, KT, SEQ], FP32R)
        h_lo = keep("h_lo", [P, KT, SEQ], FP32R)
        w_raw = [keep(f"w_raw{s}", [P, KT * P]) for s in range(2)]
        w_hi = [keep(f"w_hi{s}", [P, KT * P], FP32R) for s in range(2)]
        w_lo = [keep(f"w_lo{s}", [P, KT * P], FP32R) for s in range(2)]
        ident = keep("ident", [P, P])
        ones = keep("ones", [P, 1])
        N_GAIN, N_CM, N_POS, N_CF = 6 * KT, TAPS * 2 * MH, 2 * CMP_LEN, FTAPS * 2 * FT
        par = keep("par", [P, N_GAIN + N_CM + N_POS + N_CF])
        par_rows = at("par_rows", KB * 160, [P, 4, P])
        gains = par[:, 0:N_GAIN].rearrange("p (n k) -> p n k", k=KT)
        G_MIX, G_HEAD, G_MQ, G_MKV, G_FFN, G_FIN = range(6)
        conv_m = par[:, N_GAIN:N_GAIN + N_CM].rearrange("p (t k) -> p t k", t=TAPS)
        pos = par[:, N_GAIN + N_CM:N_GAIN + N_CM + N_POS].rearrange("p (a l) -> p a l", a=2)
        conv_f = par[:, N_GAIN + N_CM + N_POS:].rearrange("p (t k) -> p t k", t=FTAPS)
        PAR_TILES = [(N_GAIN + N_CM, 0), (N_POS, N_GAIN + N_CM), (2 * 2 * FT, N_GAIN + N_CM + N_POS),
                     (2 * FT, N_GAIN + N_CM + N_POS + 2 * 2 * FT)]
        bias_if = keep("bias_if", [MH, 2])
        gate_sig = keep("gate_sig", [P, TT, NH * 3])
        log_in = keep("log_in", [P, TT, MH])
        den_floor = keep("den_floor", [P, TT, MH])
        ssq = keep("ssq", [P, TT, NH + MH])
        rstd = keep("rstd", [P, TT, NH + MH])
        sums = keep("sums", [P, 8])
        shift = keep("shift", [P, 8])
        coef = keep("coef", [P, 8])
        fw = keep("fw", [P, 2, FTAPS])
        col = keep("col", [P, 4, TT])
        mmask = keep("mmask", [P, P])
        FREE = cursor[0]

        x_tok = at("x_tok", FREE, [P, TT, D])
        junk = at("junk", FREE + 32 * KB, [P, D])

        nq = at("nq", FREE, [P, NH // 2, SEQ])
        w1 = at("w1", FREE, [P, 2, CMP_LEN, CMP_HID])
        k_a = [at(f"k_a{br}", FREE + (16 + 16 * br) * KB, [P, G, SEQ], FP32R) for br in range(2)]
        k_b = [at(f"k_b{br}", FREE + (24 + 16 * br) * KB, [P, G, SEQ], FP32R) for br in range(2)]
        v_tok = at("v_tok", FREE + 48 * KB, [P, 2, TT, P])
        o_nsa = at("o_nsa", FREE + 56 * KB, [P, TT, NH * DH])
        g_rows = at("g_rows", FREE + 56 * KB, [NH * 3, SEQ])
        g_i = at("g_i", FREE + 60 * KB, [MH, SEQ])
        g_f = at("g_f", FREE + 64 * KB, [MH, SEQ])
        g_t = at("g_t", FREE + 68 * KB, [MH, SEQ])
        m_rows = at("m_rows", FREE + 72 * KB, [MH, SEQ])
        o = FREE + 76 * KB
        kc_a = at("kc_a", o, [P, G, DH], FP32R)
        kc_b = at("kc_b", o + 512, [P, G, DH], FP32R)
        vc = at("vc", o + 1024, [DH, G, DH])
        ident_r = at("ident_r", o + 1536, [P, P], FP32R)
        mask_diag = at("mask_diag", o + 2048, [P, P], FP32R)
        mask_edge = at("mask_edge", o + 2560, [P, P], FP32R)
        mask_cmp = at("mask_cmp", o + 3072, [P, TT, DH], FP32R)
        keep_cmp = at("keep_cmp", o + 5120, [P, 1])
        gate_h = at("gate_h", o + 5376, [P, 2, TT, 3])
        r = o + 5632
        kvp = at("kvp", r, [P, 2, 2, SEQ])
        mask_src = at("mask_src", r + 24 * KB, [P, TT, DH])
        mask_sq = at("mask_sq", r + 26 * KB, [P, 2, P])
        v_feat = at("v_feat", r + 16 * KB, [P, 2, SEQ])
        w2 = at("w2", r + 28 * KB + 256, [CMP_HID, 2, DH])
        hid = at("hid", r + 29 * KB, [CMP_HID, 2, G, NCMP])
        q_st = [at(f"q_st{u}", r + 4 * KB * u, [P, SEQ], FP32R) for u in range(2)]
        probs = [at(f"probs{b}", r + (8 + 4 * b) * KB, [P, SEQ]) for b in range(3)]
        probs_t = [at(f"probs_t{b}", r + (20 + 4 * b) * KB, [P, TT, P]) for b in range(2)]
        o_stage = at("o_stage", r + 28 * KB, [P, 2, TT, DH])

        o_gate = at("o_gate", FREE, [P, MH, SEQ])
        u_raw = at("u_raw", FREE + 16 * KB, [P, 4 + SEQ])
        c = FREE + 20 * KB + 32
        u_conv = at("u_conv", c, [P, SEQ])
        mq_hi = at("mq_hi", c + 4 * KB, [P, SEQ], FP32R)
        mq_lo = at("mq_lo", c + 8 * KB, [P, SEQ], FP32R)
        mk_hi = at("mk_hi", c + 12 * KB, [P, SEQ], FP32R)
        mk_lo = at("mk_lo", c + 16 * KB, [P, SEQ], FP32R)
        mv_feat = at("mv_feat", c + 20 * KB, [P, SEQ])
        m_bc = at("m_bc", c + 24 * KB, [P, SEQ])
        decay = [at(f"decay{b}", c + (28 + 2 * b) * KB, [P, HALF]) for b in range(2)]
        m_pick = at("m_pick", c + 32 * KB, [MH, P])
        head_a = at("head_a", c + 32 * KB + 512, [P, 2, TT])
        head_d = at("head_d", c + 32 * KB + 576, [P, 4, TT])
        head_w = at("head_w", c + 32 * KB + 704, [P, 2, TAPS])
        h_mls = at("h_mls", FREE + 76 * KB, [P, TT, MH * MDH])
        mv_tok = at("mv_tok", FREE + 92 * KB, [P, TT, MDH + 4])
        tri = at("tri", FREE + 96 * KB + 128, [P, TT * (TT + 1) // 2, P])

        acc = at("acc", FREE, [P, SEQ])
        r_bc = at("r_bc", FREE + 4 * KB, [P, SEQ])
        tmp = [at(f"tmp{b}", FREE + (8 + 2 * b) * KB, [P, HALF]) for b in range(4)]
        x_t = at("x_t", FREE + 16 * KB, [P, KT, SEQ])
        x_half = at("x_half", FREE + 92 * KB, [P, TT // 2, D])
        hm_hi = at("hm_hi", FREE + 48 * KB, [P, KT, MEM], FP32R)
        hm_lo = at("hm_lo", FREE + 56 * KB, [P, KT, MEM], FP32R)
        mem_tok = at("mem_tok", FREE + 64 * KB, [P, MEMT, D])
        xo = at("xo", FREE + 48 * KB, [P, KT, SEQ])
        xk = at("xk", FREE + 80 * KB, [P, KT, MEM])
        xv = at("xv", FREE + 88 * KB, [P, MEMT, D])
        xv_feat = at("xv_feat", FREE + 96 * KB, [P, KT, MEM])
        xq = at("xq", FREE + 96 * KB, [P, 2, SEQ])
        xp_t = at("xp_t", FREE + 104 * KB, [P, MEMT, SEQ])
        xv_h = at("xv_h", FREE + 112 * KB, [P, MEMT, XDH])
        xp = [at(f"xp{b}", FREE + (8 + b) * KB, [P, MEM]) for b in range(4)]
        f = FREE + 48 * KB
        gated = [at(f"gated{b}", FREE + (48 + 2 * b) * KB, [P, HALF]) for b in range(2)]
        sq = [at(f"sq{b}", FREE + (8 + 4 * b) * KB, [P, SEQ]) for b in range(2)]
        fu = [at(f"fu{s}", f + (4 * KB + 32) * s, [P, 8 + SEQ]) for s in range(2)]
        f += 2 * (4 * KB + 32)
        fc = [at(f"fc{s}", f + 4 * KB * s, [P, SEQ]) for s in range(2)]
        fg = at("fg", f + 8 * KB, [P, SEQ])
        z_hi = [at(f"z_hi{b}", f + (12 + 4 * b) * KB, [P, SEQ], FP32R) for b in range(2)]
        z_lo = [at(f"z_lo{b}", f + (20 + 4 * b) * KB, [P, SEQ], FP32R) for b in range(2)]
        y_t = at("y_t", FREE + 48 * KB, [P, KT, SEQ])
        y_tok = [at(f"y_tok{b}", FREE + (80 + 2 * b) * KB, [P, HALF]) for b in range(4)]

        ps = ctx.enter_context(nc.psum_tensor("ps", [P, 8, HALF], FP32))
        ps_flat = ps[:, :, :].rearrange("p b n -> p (b n)")

        names = {}

        for name in ("chunk_done chunk_freed tile_started weights_split w_loaded0 w_loaded1 w_hi_made gate_cols pool_chain "
                     "masks_ready vector_chain hi_ready std_ready x_scaled junk_written params_loaded w1_loaded "
                     "hid_ready khi_ready gates_ready f_abs_ready ln_step floor_ready log_rows_ready scores_ready "
                     "q_hi_ready q_ready probs_ready shift_ready pt_made0 pt_made1 pt_copied0 pt_copied1 o_ready o_taken "
                     "o_stage_taken conv_ready silu_done qk_ready pick_ready diag_ready decay_ready hm_ready hm_taken "
                     "xh_loaded gate_done ssq_ready mixed_ready split_ready mem_loaded mem_scaled sq_ready sq_used "
                     "r_col_ready tmp_ready h_ready x_shift_ready x_exp_ready xv_ready u_ready conv_done gelu_ready "
                     "z_made z_ready y_t_ready y_ready stored0 stored1 stored2 stored3").split():
            names[name] = ctx.enter_context(nc.semaphore(name))
        for i in range(TT):
            names[f"x_loaded{i}"] = ctx.enter_context(nc.semaphore(f"x_loaded{i}"))

        class View:

            def __init__(self):
                self.t = {}

            def __call__(self, name, step=1):
                if name not in self.t:
                    self.t[name] = Tally(names[name], step)
                return self.t[name]

        whole = lambda m: m[tuple([slice(None)] * len(m.shape))]
        block = ctx.enter_context(nc.Block())
        rows = lambda g, s=1: slice(DH * g, DH * g + DH)
        tri_at = lambda j, i: sum(TT - a for a in range(j)) + i - j
        pieces = [(j, a, min(a + HALF, SEQ)) for j in range(TT) for a in range(P * j, SEQ, HALF)]

        @block.sync
        def _(sp):
            t = View()
            weights_split, y_ready = t("weights_split"), t("y_ready")
            gate_cols, w_loaded0, w_loaded1 = t("gate_cols", 16), t("w_loaded0", 16), t("w_loaded1", 16)
            loaded, weights_split = [w_loaded0, w_loaded1], weights_split

            def load(weights, k_tiles=True):
                s = weights_split.n % 2
                weights_split.add(1)
                if weights_split.past(2):
                    sp.wait_ge(weights_split.sem, weights_split.value(2))
                if k_tiles:
                    sp.dma_start(w_raw[s][:, :].rearrange("p (k m) -> p k m", k=KT),
                                               weights.rearrange("(k p) m -> p k m", p=P)).then_inc(
                                                   loaded[s].sem, loaded[s].up())
                else:
                    sp.dma_start(w_raw[s][:, :], weights).then_inc(loaded[s].sem, loaded[s].up())

            def w_loop(turns, tiles):
                return engine_loop(sp, turns, [(weights_split, tiles), (loaded[0], tiles // 2), (loaded[1], tiles // 2)])

            x_v = x[0, :, :].rearrange("(t p) d -> p t d", p=P)
            for i in range(TT):
                sp.dma_start(x_tok[:, i, :], x_v[:, i, :]).then_inc(
                    t(f"x_loaded{i}", 16).sem, t(f"x_loaded{i}", 16).up())
            win = w_in[0, :, :]
            for c in (C_KC, C_VC, C_KS, C_VS, C_KW, C_VW):
                load(win[:, c:c + P])
            s = weights_split.n % 2
            weights_split.add(1)
            sp.wait_ge(weights_split.sem, weights_split.value(2))
            slot = w_raw[s][:, :].rearrange("p (k m) -> p k m", k=KT)
            for a, b, src in ((R_I, R_I + MH, C_MI), (R_I + MH, R_F, C_GT + 32), (R_F, R_F + MH, C_MF),
                              (R_F + MH, P, C_GT + 64)):
                sp.dma_start(slot[:, :, a:b], win[:, src:src + b - a].rearrange("(k p) m -> p k m", p=P)).then_inc(
                    gate_cols.sem, gate_cols.up())
            sp.wait_ge(gate_cols.sem, gate_cols.value())
            sp.dma_start(slot[:, :, 0:R_I], win[:, C_GT:C_GT + R_I].rearrange("(k p) m -> p k m", p=P)).then_inc(
                loaded[s].sem, loaded[s].up())
            for i in range(4):
                load(win[:, C_Q + P * i:C_Q + P * i + P])
            with w_loop(MH, 4) as i:
                for c in (C_MQ, C_MK, C_MV, C_MO):
                    load(win[:, bass.ds(i * P + c, P)])

            def load_all(weights):
                with w_loop(KT // 2, 2) as i:
                    for u in range(2):
                        load(weights[:, bass.ds(i * (2 * P) + u * P, P)])

            load_all(w_out[0, :, :])
            for w in (w_mem_k, w_mem_v, w_mem_q, w_mem_o):
                load_all(w[0, :, :])
            up, down = w_up[0, :, :], w_down[0, :, :]
            load(up[:, 0:P])
            load(up[:, FF:FF + P])
            with w_loop((FT - 2) // 2, 6) as i:
                for u in range(2):
                    load(up[:, bass.ds(i * (2 * P) + (1 + u) * P, P)])
                    load(up[:, bass.ds(i * (2 * P) + FF + (1 + u) * P, P)])
                    load(down[bass.ds(i * (2 * P) + u * P, P), :], k_tiles=False)
            load(up[:, FF - P:FF])
            load(up[:, 2 * FF - P:2 * FF])
            for p in (FT - 2, FT - 1):
                load(down[p * P:p * P + P, :], k_tiles=False)
            stored = [t(f"stored{b}", 16) for b in range(4)]
            for n in range(2 * TT):
                sp.wait_ge(y_ready.sem, y_ready.next())
                sp.dma_start(out[0, P * (n // 2):P * (n // 2) + P, HALF * (n % 2):HALF * (n % 2) + HALF],
                                               y_tok[n % 4][:, :]).then_inc(stored[n % 4].sem, stored[n % 4].up())
            for s in stored:
                sp.wait_ge(s.sem, s.value())

        @block.gpsimd
        def _(pool):
            t = View()
            masks_ready, pool_chain, tile_started = t("masks_ready"), t("pool_chain"), t("tile_started")
            w_hi_made, weights_split = t("w_hi_made"), t("weights_split")
            w_loaded0, w_loaded1 = t("w_loaded0", 16), t("w_loaded1", 16)
            for m, v in ((ident, 0.0), (ones, 1.0), (mask_sq, 0.0), (mask_src, 0.0), (mmask, 0.0),
                         (keep_cmp, 1.0)):
                pool.memset(whole(m), v).then_inc(pool_chain.sem, pool_chain.up())
            pool.wait_ge(pool_chain.sem, pool_chain.value())
            sel = pool.affine_select
            sel(out=ident[:, :], in_=ident[:, :], compare_op=ALU.not_equal, fill=1.0, base=0,
                          pattern=[[-1, P]], channel_multiplier=1).then_inc(pool_chain.sem, pool_chain.up())
            sel(out=mask_sq[:, 0, :], in_=mask_sq[:, 0, :], compare_op=ALU.is_ge, fill=NEG, base=0,
                          pattern=[[-1, P]], channel_multiplier=1).then_inc(pool_chain.sem, pool_chain.up())
            sel(out=mask_sq[:, 1, :], in_=mask_sq[:, 1, :], compare_op=ALU.is_gt, fill=NEG, base=0,
                          pattern=[[1, P]], channel_multiplier=-1).then_inc(pool_chain.sem, pool_chain.up())
            sel(out=mask_src[:, :, :], in_=mask_src[:, :, :], compare_op=ALU.is_ge, fill=NEG,
                          base=-(CMP_LEN - 1), pattern=[[P, TT], [-CMP_STRIDE, DH]], channel_multiplier=1).then_inc(
                              pool_chain.sem, pool_chain.up())
            sel(out=keep_cmp[:, :], in_=keep_cmp[:, :], compare_op=ALU.is_ge, fill=0.0,
                          base=-(CMP_LEN - 1), pattern=[[0, 1]], channel_multiplier=1).then_inc(
                              pool_chain.sem, pool_chain.up())
            sel(out=mmask[:, :], in_=mmask[:, :], compare_op=ALU.is_ge, fill=NEG, base=0,
                          pattern=[[1, P]], channel_multiplier=-1).then_inc(pool_chain.sem, pool_chain.up())
            pool.wait_ge(pool_chain.sem, pool_chain.value())
            pool.tensor_copy(mask_diag[:, :], mask_sq[:, 0, :]).then_inc(masks_ready.sem, masks_ready.up())
            pool.tensor_copy(mask_edge[:, :], mask_sq[:, 1, :]).then_inc(masks_ready.sem, masks_ready.up())
            pool.tensor_copy(mask_cmp[:, :, :], mask_src[:, :, :]).then_inc(masks_ready.sem, masks_ready.up())
            pool.tensor_copy(ident_r[:, :], ident[:, :]).then_inc(masks_ready.sem, masks_ready.up())

            loaded, weights_split, tile_started = [w_loaded0, w_loaded1], weights_split, tile_started
            hi_made = w_hi_made

            def split_tile(s):
                pool.wait_ge(loaded[s].sem, loaded[s].next())
                if tile_started.past(0):
                    pool.wait_ge(tile_started.sem, tile_started.value())
                pool.tensor_tensor(w_hi[s][:, :], w_raw[s][:, :],
                                                      ones[:, :].to_broadcast([P, KT * P]), ALU.mult).then_inc(
                                                          hi_made.sem, hi_made.up())
                pool.wait_ge(hi_made.sem, hi_made.value())
                pool.tensor_tensor(w_lo[s][:, :], w_raw[s][:, :], w_hi[s][:, :].bitcast(FP32), ALU.subtract).then_inc(
                    weights_split.sem, weights_split.up())
                tile_started.add(1)

            tiles = 11 + 4 * MH + 5 * KT + 3 * FT
            assert tiles % 2
            split_tile(0)
            with engine_loop(pool, tiles // 2, [(loaded[0], 1), (loaded[1], 1), (weights_split, 2), (tile_started, 2), (hi_made, 2)]):
                split_tile(1)
                split_tile(0)

        @block.tensor
        def _(pe):
            t = View()
            chunk_done, chunk_freed, h_ready = t("chunk_done"), t("chunk_freed"), t("h_ready")
            hid_ready, log_rows_ready, masks_ready = t("hid_ready"), t("log_rows_ready"), t("masks_ready")
            mem_scaled, mixed_ready, o_ready = t("mem_scaled"), t("mixed_ready"), t("o_ready")
            o_taken, pick_ready, probs_ready = t("o_taken"), t("pick_ready"), t("probs_ready")
            pt_copied0, pt_copied1, pt_made0 = t("pt_copied0"), t("pt_copied1"), t("pt_made0")
            pt_made1, q_ready, qk_ready = t("pt_made1"), t("q_ready"), t("qk_ready")
            r_col_ready, scores_ready, split_ready = t("r_col_ready"), t("scores_ready"), t("split_ready")
            sq_used, tile_started, weights_split = t("sq_used"), t("tile_started"), t("weights_split")
            x_scaled, xv_ready, y_ready = t("x_scaled"), t("xv_ready"), t("y_ready")
            y_t_ready, z_ready = t("y_t_ready"), t("z_ready")
            params_loaded, w1_loaded, xh_loaded = t("params_loaded", 16), t("w1_loaded", 16), t("xh_loaded", 16)
            mm, transpose = nc.tensor.matmul, nc.tensor.transpose

            def open_chunk(of_output=None):
                if of_output is not None and of_output >= 4:
                    pe.wait_ge(y_ready.sem, of_output - 3)
                elif chunk_done.n >= 4:
                    pe.wait_ge(chunk_freed.sem, chunk_done.value(3))
                return chunk_done.n % 4

            def freed_now():
                pe.wait_ge(chunk_freed.sem, chunk_done.value())

            def product(out_ap, slot_k, x_hi, x_lo, first, last, tag=None):
                whi, wlo = slot_k
                ins = mm(out_ap, whi, x_hi, start=first, stop=False)
                if tag:
                    ins.then_inc(tile_started.sem, tile_started.up())
                mm(out_ap, whi, x_lo, start=False, stop=False)
                return mm(out_ap, wlo, x_hi, start=False, stop=last)

            def next_weights():
                pe.wait_ge(weights_split.sem, weights_split.next())
                return (weights_split.n - 1) % 2

            def gemm_tile(x_hi, x_lo, width=SEQ, before_chunk=None):
                s = next_weights()
                for c in range(0, width, HALF):
                    n = min(HALF, width - c)
                    b = open_chunk()
                    if before_chunk:
                        before_chunk(c // HALF)
                    for k in range(KT):
                        w = (w_hi[s][:, k * P:k * P + P], w_lo[s][:, k * P:k * P + P])
                        last = product(ps[:, b, 0:n], w, x_hi[:, k, c:c + n], x_lo[:, k, c:c + n],
                                       k == 0, k == KT - 1, tag=(c == 0 and k == 0))
                    last.then_inc(chunk_done.sem, chunk_done.up())

            def gemm_loop(turns, tiles, x_hi, x_lo, width=SEQ):
                per = tiles * ((width + HALF - 1) // HALF)
                assert per % 4 == 0
                with engine_loop(pe, turns, [(weights_split, tiles), (tile_started, tiles), (chunk_done, per)]):
                    for _ in range(tiles):
                        gemm_tile(x_hi, x_lo, width)

            def transposes(parts, of_output=None):
                b = open_chunk(of_output)
                for src, n, at_col in parts:
                    m = src.shape[-1]
                    last = transpose(ps[0:m, b, at_col:at_col + n], src, ident[0:n, 0:n])
                last.then_inc(chunk_done.sem, chunk_done.up())

            masks_ready.add(4)
            pe.wait_ge(masks_ready.sem, masks_ready.value())
            params_loaded.add(PARAM_LOADS)
            pe.wait_ge(params_loaded.sem, params_loaded.value())
            for n in range(0, 4, 2):
                b = open_chunk()
                for m in (n, n + 1):
                    r_, c_ = PAR_TILES[m]
                    c_ -= PAR_TILES[n][1]
                    last = transpose(ps[:, b, c_:c_ + r_], par_rows[0:r_, m, :], ident[0:r_, 0:r_])
                last.then_inc(chunk_done.sem, chunk_done.up())
            for half in range(2):
                x_scaled.add(4)
                pe.wait_ge(x_scaled.sem, x_scaled.value())
                for k in range(KT):
                    transposes([(x_tok[:, 4 * half + j, k * P:k * P + P], P, j * P) for j in range(4)])
            freed_now()

            gemm_tile(h_hi, h_lo)
            gemm_tile(h_hi, h_lo)
            freed_now()
            w1_loaded.add(4)
            pe.wait_ge(w1_loaded.sem, w1_loaded.value())
            for kv in range(2):
                banks = []
                for g in range(G):
                    banks.append(open_chunk())
                    chunk_done.n += 1
                chunk_done.n -= G
                for l in range(CMP_LEN):
                    lo_t = l % CMP_STRIDE + (CMP_STRIDE if l >= CMP_STRIDE else 0)
                    for g in range(G):
                        src = kvp[rows(g), kv, l // CMP_STRIDE, :]
                        last = mm(ps[0:CMP_HID, banks[g], 0:NCMP], w1[rows(g), kv, l, :],
                                  src[:, lo_t:lo_t + CMP_STRIDE * (NCMP - 1) + 1:CMP_STRIDE],
                                  start=(l == 0), stop=(l == CMP_LEN - 1))
                        if l == CMP_LEN - 1:
                            last.then_inc(chunk_done.sem, chunk_done.up())
            pe.wait_ge(hid_ready.sem, hid_ready.next())
            b = open_chunk()
            for g in range(G):
                last = mm(ps[0:DH, b, DH * g:DH * g + NCMP], w2[:, 0, :], hid[:, 0, g, :], start=True, stop=True)
            last.then_inc(chunk_done.sem, chunk_done.up())
            b = open_chunk()
            for g in range(G):
                last = mm(ps[0:NCMP, b, DH * g:DH * g + DH], hid[:, 1, g, :], w2[:, 1, :], start=True, stop=True)
            last.then_inc(chunk_done.sem, chunk_done.up())
            for _ in range(5 + NH // 2):
                gemm_tile(h_hi, h_lo)
            for br in range(2):
                for q in range(2):
                    transposes([(v_feat[:, br, (4 * q + j) * P:(4 * q + j + 1) * P], P, j * P) for j in range(4)])
            transposes([(g_rows[:, j * P:j * P + P], NH * 3, j * 32) for j in range(TT)])
            pe.wait_ge(log_rows_ready.sem, log_rows_ready.next())
            b = open_chunk()
            for src, at_col in ((g_i, 0), (g_f, 64)):
                for j in range(TT):
                    last = transpose(ps[:, b, at_col + MH * j:at_col + MH * j + MH], src[:, j * P:j * P + P],
                                     ident[0:MH, 0:MH])
            last.then_inc(chunk_done.sem, chunk_done.up())
            freed_now()

            with engine_loop(pe, G, [(scores_ready, 2 * JOBS), (q_ready, 4), (probs_ready, 2 * JOBS), (pt_made0, 2 * JOBS),
                                     (pt_made1, 2 * JOBS_1), (pt_copied0, 2 * JOBS), (pt_copied1, 2 * JOBS_1), (o_ready, 2 * JOBS),
                                     (o_taken, 2 * JOBS)]) as g:
                with engine_loop(pe, 2, [(scores_ready, JOBS), (q_ready, 2), (probs_ready, JOBS), (pt_made0, JOBS), (pt_made1, JOBS_1),
                                         (pt_copied0, JOBS), (pt_copied1, JOBS_1), (o_ready, JOBS), (o_taken, JOBS)]):
                    ga = pe.snap(g * SEQ)
                    gc = pe.snap(g * DH)
                    gv = gc

                    def moving(tensor, base, off, n):
                        return tensor[:, :, :].rearrange("p g s -> p (g s)")[:, bass.ds(base + off, n)]

                    def scores(j):
                        u, i, br = job_of(j)
                        if j % TT == 0 and j % (2 * TT) == 0:
                            pe.wait_ge(q_ready.sem, q_ready.next())
                        if j >= 2:
                            pe.wait_ge(probs_ready.sem, scores_ready.value(1))
                        first = 0 if br == 0 else max(0, i - WT)
                        n = (i - first + 1) * P
                        q = q_st[u][:, i * P:i * P + P]
                        bank = 2 * (j % 2)
                        for c in range(0, n, HALF):
                            m = min(HALF, n - c)
                            o = ps[:, bank + c // HALF, 0:m]
                            at_key = first * P + c
                            masks = []
                            if c <= n - P < c + HALF:
                                masks.append((n - P - c, mask_diag))
                            if br == 1 and i >= WT and c == 0:
                                masks.append((0, mask_edge))
                            mm(o, q, moving(k_a[br], ga, at_key, m), start=True, stop=False)
                            last = mm(o, q, moving(k_b[br], ga, at_key, m), start=False, stop=not masks)
                            for z, (a, mask) in enumerate(masks):
                                last = mm(ps[:, bank + c // HALF, a:a + P], ident_r[:, :], mask[:, :],
                                          start=False, stop=z == len(masks) - 1)
                        if br == 1:
                            o = ps[:, bank + 1, P:P + DH]
                            kc_ = lambda z: z[:, :, :].rearrange("p g s -> p (g s)")[:, bass.ds(gc, DH)]
                            mm(o, q, kc_(kc_a), start=True, stop=False)
                            mm(o, q, kc_(kc_b), start=False, stop=False)
                            last = mm(o, ident_r[:, :], mask_cmp[:, i, :], start=False, stop=True)
                        last.then_inc(scores_ready.sem, scores_ready.up())

                    def turn(j):
                        u, i, br = job_of(j)
                        n = i + 1 if br == 0 else min(i, WT) + 1
                        pe.wait_ge(probs_ready.sem, probs_ready.next())
                        pr = probs[j % 3]
                        if j:
                            pe.wait_ge(pt_copied0.sem, pt_made0.value())
                        if has_second(j) and any(has_second(a) for a in range(j)):
                            pe.wait_ge(pt_copied1.sem, pt_made1.value())
                        for a in range(min(n, 4)):
                            last = transpose(ps[:, 4, a * P:a * P + P], pr[:, a * P:a * P + P], ident[:, :])
                        last.then_inc(pt_made0.sem, pt_made0.up())
                        if has_second(j):
                            for a in range(4, n):
                                last = transpose(ps[:, 5, (a - 4) * P:(a - 3) * P], pr[:, a * P:a * P + P], ident[:, :])
                            if br == 1:
                                last = transpose(ps[0:DH, 5, 3 * P:4 * P], pr[:, 5 * P:5 * P + DH], ident[:, :])
                            last.then_inc(pt_made1.sem, pt_made1.up())

                    def values(j):
                        u, i, br = job_of(j)
                        first = 0 if br == 0 else max(0, i - WT)
                        n = i + 1 - first
                        pe.wait_ge(pt_copied0.sem, pt_copied0.next())
                        if has_second(j):
                            pe.wait_ge(pt_copied1.sem, pt_copied1.next())
                        if j >= 2:
                            pe.wait_ge(o_taken.sem, o_ready.value(1))
                        v_flat = v_tok[:, br, :, :].rearrange("p t d -> p (t d)")
                        for a in range(n):
                            last = mm(ps[:, 6 + j % 2, 0:DH], probs_t[j % 2][:, a, :],
                                      v_flat[:, bass.ds(gv + (first + a) * P, DH)], start=a == 0, stop=a == n - 1)
                        if br == 1:
                            last = mm(ps[:, 6 + j % 2, DH:2 * DH], probs_t[j % 2][0:DH, TT - 1, :],
                                      vc[:, :, :].rearrange("n g d -> n (g d)")[:, bass.ds(gc, DH)],
                                      start=True, stop=True)
                        last.then_inc(o_ready.sem, o_ready.up())

                    for st in range(JOBS + 3):
                        if st < JOBS:
                            scores(st)
                        if 0 <= st - 2 < JOBS:
                            turn(st - 2)
                        if 0 <= st - 3 < JOBS:
                            values(st - 3)
                    o_taken.add(JOBS)
            pe.wait_ge(o_taken.sem, o_taken.value())

            with engine_loop(pe, MH, [(weights_split, 4), (tile_started, 4), (chunk_done, 32), (pick_ready, 1), (qk_ready, 1)]):
                for _ in range(4):
                    gemm_tile(h_hi, h_lo)
                pe.wait_ge(pick_ready.sem, pick_ready.next())
                for c in range(2):
                    b = open_chunk()
                    mm(ps[:, b, :], m_pick[:, :], m_rows[:, c * HALF:c * HALF + HALF], start=True, stop=True).then_inc(
                        chunk_done.sem, chunk_done.up())
                for q in range(2):
                    transposes([(mv_feat[:, (4 * q + j) * P:(4 * q + j + 1) * P], P, j * P) for j in range(4)])
                pe.wait_ge(qk_ready.sem, qk_ready.next())
                for j, a, e in pieces:
                    b = open_chunk()
                    product(ps[:, b, 0:e - a], (mk_hi[:, j * P:j * P + P], mk_lo[:, j * P:j * P + P]),
                                     mq_hi[:, a:e], mq_lo[:, a:e], True, True).then_inc(
                                         chunk_done.sem, chunk_done.up())
                freed_now()
                for i in range(TT):
                    b = open_chunk()
                    for j in range(i + 1):
                        last = mm(ps[:, b, 0:MDH + 1], tri[:, tri_at(j, i), :], mv_tok[:, j, 0:MDH + 1],
                                  start=j == 0, stop=j == i)
                    last.then_inc(chunk_done.sem, chunk_done.up())

            def residual_tiles(half):
                pe.wait_ge(xh_loaded.sem, xh_loaded.next())
                for k in range(KT):
                    transposes([(x_half[:, j, k * P:k * P + P], P, j * P) for j in range(4)])

            residual_tiles(0)
            pe.wait_ge(mixed_ready.sem, mixed_ready.next())
            for f in range(KT):
                src = o_nsa if f < 4 else h_mls
                for q in range(2):
                    transposes([(src[:, 4 * q + j, (f % 4) * P:(f % 4) * P + P], P, j * P) for j in range(4)])
            residual_tiles(1)
            split_ready.add(8)
            pe.wait_ge(split_ready.sem, split_ready.value())
            freed_now()
            gemm_loop(KT // 2, 2, h_hi, h_lo)

            def norm_rows():
                sq_used.add(2 + KT)
                pe.wait_ge(sq_used.sem, sq_used.value())
                for c in range(2):
                    b = open_chunk()
                    for j in range(4):
                        last = mm(ps[:, b, j:j + 1], acc[:, (4 * c + j) * P:(4 * c + j + 1) * P], ones[:, :],
                                  start=True, stop=True)
                    last.then_inc(chunk_done.sem, chunk_done.up())
                pe.wait_ge(r_col_ready.sem, r_col_ready.next())
                for c in range(2):
                    b = open_chunk()
                    for j in range(4):
                        last = mm(ps[:, b, j * P:j * P + P], col[:, 0, 4 * c + j:4 * c + j + 1].to_broadcast([P, P]),
                                  ident[:, :], start=True, stop=True)
                    last.then_inc(chunk_done.sem, chunk_done.up())

            pe.wait_ge(mem_scaled.sem, mem_scaled.next())
            for k in range(KT):
                transposes([(mem_tok[:, j, k * P:k * P + P], P, j * P) for j in range(MEMT)])
            norm_rows()
            freed_now()
            gemm_loop(KT // 4, 4, hm_hi, hm_lo, MEM)
            gemm_loop(KT // 4, 4, hm_hi, hm_lo, MEM)
            freed_now()
            for j in range(MEMT):
                for q in range(2):
                    transposes([(xv_feat[:, 4 * q + k, j * P:j * P + P], P, k * P) for k in range(4)])
            h_ready.add(2 * KT)
            pe.wait_ge(h_ready.sem, h_ready.value())
            freed_now()
            with engine_loop(pe, XH, [(weights_split, 2), (tile_started, 2), (chunk_done, 20), (xv_ready, 1)]) as hd:
                for _ in range(2):
                    gemm_tile(h_hi, h_lo)
                freed_now()
                keys = pe.snap(hd * (2 * MEM))
                xk_flat = xk[:, :, :].rearrange("p k m -> p (k m)")
                made = {}

                def x_scores(i):
                    b = open_chunk()
                    for z in range(2):
                        last = mm(ps[:, b, 0:MEM], xq[:, z, i * P:i * P + P], xk_flat[:, bass.ds(keys + z * MEM, MEM)],
                                  start=z == 0, stop=z == 1)
                    last.then_inc(chunk_done.sem, chunk_done.up())
                    made[i] = chunk_done.n

                def x_turn(i):
                    pe.wait_ge(chunk_freed.sem, chunk_done.value(chunk_done.n - made[i + 1]))
                    b = open_chunk()
                    for j in range(MEMT):
                        for d in range(2):
                            last = transpose(ps[:, b, (2 * j + d) * P:(2 * j + d + 1) * P],
                                             xp[(i + d) % 4][:, j * P:j * P + P], ident[:, :])
                    last.then_inc(chunk_done.sem, chunk_done.up())

                for what, i in X_ORDER:
                    (x_scores if what == "s" else x_turn)(i)
                pe.wait_ge(xv_ready.sem, xv_ready.next())
                freed_now()
                for z in range(2):
                    for c in range(2):
                        b = open_chunk()
                        for j in range(MEMT):
                            last = mm(ps[:, b, :], xv_h[:, j, z * P:z * P + P], xp_t[:, j, c * HALF:c * HALF + HALF],
                                      start=j == 0, stop=j == MEMT - 1)
                        last.then_inc(chunk_done.sem, chunk_done.up())
            h_ready.add(KT)
            pe.wait_ge(h_ready.sem, h_ready.value())
            gemm_loop(KT // 2, 2, h_hi, h_lo)
            norm_rows()
            freed_now()

            def up_tile(before_chunk=None):
                gemm_tile(h_hi, h_lo, before_chunk=before_chunk)

            def down(b):
                s = next_weights()
                pe.wait_ge(z_ready.sem, z_ready.next())
                for m in range(KT):
                    for c in range(2):
                        bank = open_chunk()
                        w = (w_hi[s][:, m * P:m * P + P], w_lo[s][:, m * P:m * P + P])
                        product(ps[:, bank, :], w, z_hi[b][:, c * HALF:c * HALF + HALF],
                                         z_lo[b][:, c * HALF:c * HALF + HALF], True, True, tag=(m == 0 and c == 0)).then_inc(
                                             chunk_done.sem, chunk_done.up())

            def wait_half(c):
                h_ready.add(KT)
                pe.wait_ge(h_ready.sem, h_ready.value())

            up_tile(wait_half)
            up_tile()
            with engine_loop(pe, (FT - 2) // 2, [(weights_split, 6), (tile_started, 6), (chunk_done, 40), (z_ready, 2)]):
                for u in range(2):
                    up_tile()
                    up_tile()
                    down(u)
            up_tile()
            up_tile()
            down(0)
            down(1)

            norm_rows()
            for c in range(2):
                y_t_ready.add(KT)
                pe.wait_ge(y_t_ready.sem, y_t_ready.value())
                for j in range(4):
                    for q in range(2):
                        transposes([(y_t[:, 4 * q + k, (4 * c + j) * P:(4 * c + j + 1) * P], P, k * P) for k in range(4)],
                                   of_output=8 * c + 2 * j + q)

        @block.scalar
        def _(act):
            t = View()
            chunk_done, chunk_freed, conv_done = t("chunk_done"), t("chunk_freed"), t("conv_done")
            conv_ready, decay_ready, diag_ready = t("conv_ready"), t("decay_ready"), t("diag_ready")
            f_abs_ready, floor_ready, gate_done = t("f_abs_ready"), t("floor_ready"), t("gate_done")
            gates_ready, gelu_ready, hi_ready = t("gates_ready"), t("gelu_ready"), t("hi_ready")
            hid_ready, hm_ready, hm_taken = t("hid_ready"), t("hm_ready"), t("hm_taken")
            junk_written, khi_ready, ln_step = t("junk_written"), t("khi_ready"), t("ln_step")
            o_stage_taken, o_taken, probs_ready = t("o_stage_taken"), t("o_taken"), t("probs_ready")
            pt_copied1, pt_made0, pt_made1 = t("pt_copied1"), t("pt_made0"), t("pt_made1")
            q_hi_ready, scores_ready, shift_ready = t("q_hi_ready"), t("scores_ready"), t("shift_ready")
            silu_done, sq_ready, sq_used = t("silu_done"), t("sq_ready"), t("sq_used")
            ssq_ready, std_ready, tmp_ready = t("ssq_ready"), t("std_ready"), t("tmp_ready")
            u_ready, x_exp_ready, x_shift_ready = t("u_ready"), t("x_exp_ready"), t("x_shift_ready")
            z_made = t("z_made")
            mem_loaded, params_loaded, w1_loaded = t("mem_loaded", 16), t("params_loaded", 16), t("w1_loaded", 16)
            xh_loaded = t("xh_loaded", 16)
            f = act.activation

            def chunk():
                b = chunk_done.n % 4
                act.wait_ge(chunk_done.sem, chunk_done.next())
                return b


            def load(dst, src):
                act.dma_start(dst, src).then_inc(params_loaded.sem, params_loaded.up())

            as_rows = lambda g: g.rearrange("(k p) -> k p", p=P)
            n = 0
            for g in (g_mix[0, :], g_head_nsa[0, :], g_head_mlstm[0, :], g_mem_q[0, :], g_mem_kv[0, :], g_ffn[0, :],
                      g_final):
                k = g.shape[0] // P
                load(par_rows[n:n + k, 0, :], as_rows(g))
                n += k
            load(par_rows[n:n + N_CM, 0, :], mlstm_conv_w[0, :, :].rearrange("t (k p) -> (t k) p", p=P))
            for kv, pw in enumerate((cmp_pos_k, cmp_pos_v)):
                for g in range(G):
                    load(par_rows[kv * CMP_LEN:kv * CMP_LEN + CMP_LEN, 1, DH * g:DH * g + DH], pw[0, :, :])
            load(par_rows[0:4 * FT, 2, :], ffn_conv_w[0, 0:2, :].rearrange("t (k p) -> (t k) p", p=P))
            load(par_rows[0:2 * FT, 3, :], ffn_conv_w[0, 2, :].rearrange("(k p) -> k p", p=P))
            load(w2[:, 0, :], cmp_w2_k[0, :, :])
            load(w2[:, 1, :], cmp_w2_v[0, :, :])
            load(bias_if[:, 0:1], mlstm_b_i[0, :].rearrange("(h a) -> h a", a=1))
            load(bias_if[:, 1:2], mlstm_b_f[0, :].rearrange("(h a) -> h a", a=1))

            def freed_now():
                act.wait_ge(chunk_freed.sem, chunk_done.value())

            for half in range(2):
                for i in range(4 * half, 4 * half + 4):
                    t(f"x_loaded{i}", 16).add(1)
                    act.wait_ge(t(f"x_loaded{i}", 16).sem, t(f"x_loaded{i}", 16).value())
                    f(junk[:, :], x_tok[:, i, :], ACT.Square, accum_out=ssq[:, i, 0:1]).then_inc(
                        junk_written.sem, junk_written.up())
                    act.wait_ge(junk_written.sem, junk_written.value())
                f(rstd[:, 4 * half:4 * half + 4, 0:1], ssq[:, 4 * half:4 * half + 4, 0:1], ACT.Sqrt,
                                     scale=1.0 / D, bias=EPS).then_inc(std_ready.sem, std_ready.up())
            chunk_done.add(2)
            freed_now()
            for half in range(2):
                for k in range(KT):
                    b = chunk()
                    f(h_hi[:, k, half * HALF:half * HALF + HALF], ps[:, b, :], ACT.Copy,
                                   scale=gains[:, G_MIX, k:k + 1]).then_inc(hi_ready.sem, hi_ready.up())
            act.wait_ge(chunk_done.sem, chunk_done.value())
            for kv, w1w in enumerate((cmp_w1_k, cmp_w1_v)):
                for g in range(G):
                    act.dma_start(w1[rows(g), kv, :, :],
                                                         w1w[0, :, :].rearrange("(l d) h -> d l h", d=DH)).then_inc(
                                                             w1_loaded.sem, w1_loaded.up())

            chunk_done.add(4)
            chunk_done.add(2 * G)
            freed_now()
            f(hid[:, :, :, :].rearrange("h a g n -> h (a g n)"),
                                 hid[:, :, :, :].rearrange("h a g n -> h (a g n)"), ACT.Gelu).then_inc(
                                     hid_ready.sem, hid_ready.up())
            chunk_done.add(2)
            for br in range(2):
                for c in range(2):
                    b = chunk()
                    cs = slice(c * HALF, c * HALF + HALF)
                    for g in range(G):
                        f(k_a[br][rows(g), g, cs], ps[rows(g), b, :], ACT.Copy).then_inc(
                            khi_ready.sem, khi_ready.up())
                        f(k_b[br][rows(1 - g), g, cs], ps[rows(g), b, :], ACT.Copy).then_inc(
                            khi_ready.sem, khi_ready.up())
                chunk_done.add(2)
            act.wait_ge(f_abs_ready.sem, f_abs_ready.next())
            f(g_t[:, :], g_t[:, :], ACT.Exp).then_inc(ln_step.sem, ln_step.up())
            act.wait_ge(ln_step.sem, ln_step.value())
            f(g_t[:, :], g_t[:, :], ACT.Ln, bias=1.0).then_inc(ln_step.sem, ln_step.up())
            act.wait_ge(ln_step.sem, ln_step.value())
            chunk_done.add(2 + NH)
            chunk_done.add(4)
            chunk_done.add(1)
            freed_now()
            f(gate_sig[:, :, :], gate_sig[:, :, :], ACT.Sigmoid).then_inc(gates_ready.sem, gates_ready.up())
            chunk_done.add(1)
            freed_now()
            f(den_floor[:, :, :], den_floor[:, :, :], ACT.Exp, scale=-1.0).then_inc(floor_ready.sem, floor_ready.up())

            loop = lambda eng, n, k: engine_loop(eng, n, [(q_hi_ready, 2 * k), (probs_ready, k * JOBS), (shift_ready, k * JOBS),
                                                          (pt_made0, k * JOBS), (pt_made1, k * JOBS_1), (pt_copied1, k * JOBS_1),
                                                          (o_taken, k * JOBS), (o_stage_taken, 2 * k)])
            with loop(act, G, 2) as g:
                with loop(act, 2, 1) as hp:
                    nq_flat = nq[:, :, :].rearrange("p a s -> p (a s)")
                    at_q = act.snap((g * 2 + hp) * SEQ)
                    for u in range(2):
                        f(q_st[u][rows(u), :], nq_flat[rows(u), bass.ds(at_q, SEQ)], ACT.Copy).then_inc(
                            q_hi_ready.sem, q_hi_ready.up())
                    for st in range(JOBS + 3):
                        if st < JOBS:
                            u, i, br = job_of(st)
                            n = (i + 1 if br == 0 else min(i, WT) + 1) * P
                            if st >= 3:
                                act.wait_ge(pt_made0.sem, pt_made0.value())
                                if any(has_second(a) for a in range(st - 2)):
                                    act.wait_ge(pt_made1.sem, pt_made1.value())
                            act.wait_ge(shift_ready.sem, shift_ready.next())
                            flat = ps_flat[:, 2 * (st % 2) * HALF:2 * (st % 2) * HALF + 2 * HALF]
                            c0_ = 2 * (st % 4)
                            if br == 0:
                                f(probs[st % 3][:, 0:n], flat[:, 0:n], ACT.Exp,
                                              bias=shift[:, c0_:c0_ + 1], accum_out=sums[:, c0_:c0_ + 1]).then_inc(
                                                  probs_ready.sem, probs_ready.up())
                            else:
                                f(probs[st % 3][:, 0:n], flat[:, 0:n], ACT.Exp, bias=shift[:, c0_ + 1:c0_ + 2],
                                  accum_out=sums[:, c0_ + 1:c0_ + 2])
                                f(probs[st % 3][:, 5 * P:5 * P + DH], flat[:, 5 * P:5 * P + DH], ACT.Exp,
                                              bias=shift[:, c0_:c0_ + 1], accum_out=sums[:, c0_:c0_ + 1]).then_inc(
                                                  probs_ready.sem, probs_ready.up())
                        z = st - 2
                        if 0 <= z < JOBS:
                            u, i, br = job_of(z)
                            n = i + 1 if br == 0 else min(i, WT) + 1
                            pt_made0.add(1)
                            if has_second(z):
                                act.wait_ge(pt_made1.sem, pt_made1.next())
                                m = max(0, n - 4)
                                last = None
                                if m:
                                    last = f(probs_t[z % 2][:, 4:n, :], ps[:, 5, 0:m * P], ACT.Copy)
                                if br == 1:
                                    last = f(probs_t[z % 2][0:DH, TT - 1, :], ps[0:DH, 5, 3 * P:4 * P], ACT.Copy)
                                last.then_inc(pt_copied1.sem, pt_copied1.up())
                    for u in range(2):
                        o_taken.add(JOBS // 2)
                        act.wait_ge(o_taken.sem, o_taken.value())
                        f(o_nsa[:, :, bass.ds(act.snap((g * 4 + hp * 2 + u) * DH), DH)],
                                       o_stage[:, u, :, :], ACT.Copy).then_inc(o_stage_taken.sem, o_stage_taken.up())

            with engine_loop(act, MH, [(chunk_done, 32), (conv_ready, 2), (hi_ready, 2), (silu_done, 2),
                                       (diag_ready, 1), (decay_ready, 12), (hm_ready, 1),
                                       (hm_taken, 1)]) as h:
                for hi, scale in ((mq_hi, MDH ** -0.5), (mk_hi, 1.0)):
                    act.wait_ge(conv_ready.sem, conv_ready.next())
                    f(u_conv[:, :], u_conv[:, :], ACT.Silu).then_inc(silu_done.sem, silu_done.up())
                    act.wait_ge(silu_done.sem, silu_done.value())
                    f(hi[:, :], u_conv[:, :], ACT.Copy, scale=scale).then_inc(hi_ready.sem, hi_ready.up())
                chunk_done.add(8 + 2 + 2)
                act.wait_ge(diag_ready.sem, diag_ready.next())
                f(u_conv[:, :], u_conv[:, :], ACT.Exp).then_inc(decay_ready.sem, decay_ready.up())
                for n, (j, a, e) in enumerate(pieces):
                    chunk_done.add(1)
                    a2 = a + P if a == P * j else a
                    if a2 < e:
                        if n >= 2:
                            act.wait_ge(chunk_freed.sem, chunk_done.value(2))
                        f(decay[n % 2][:, 0:e - a2], m_bc[:, a2:e], ACT.Exp, bias=head_a[:, 0, j:j + 1]).then_inc(
                            decay_ready.sem, decay_ready.up())
                chunk_done.add(8)
                act.wait_ge(hm_ready.sem, hm_ready.next())
                f(h_mls[:, :, bass.ds(act.snap(h * MDH), MDH)],
                                    u_conv[:, :].rearrange("p (t d) -> p t d", d=MDH), ACT.Copy).then_inc(
                                        hm_taken.sem, hm_taken.up())

            x_v = x[0, :, :].rearrange("(t p) d -> p t d", p=P)
            act.wait_ge(chunk_done.sem, chunk_done.value())
            act.dma_start(x_half[:, :, :], x_v[:, 0:TT // 2, :]).then_inc(xh_loaded.sem, xh_loaded.up())
            freed_now()
            f(o_gate[:, :, :], o_gate[:, :, :], ACT.Sigmoid).then_inc(gate_done.sem, gate_done.up())
            act.wait_ge(ssq_ready.sem, ssq_ready.next())
            f(rstd[:, :, 0:NH], ssq[:, :, 0:NH], ACT.Sqrt, scale=1.0 / DH, bias=EPS).then_inc(
                std_ready.sem, std_ready.up())
            f(rstd[:, :, NH:NH + MH], ssq[:, :, NH:NH + MH], ACT.Sqrt, scale=1.0 / MDH, bias=EPS).then_inc(
                std_ready.sem, std_ready.up())
            chunk_done.add(KT)
            act.wait_ge(chunk_done.sem, chunk_done.value())
            act.dma_start(x_half[:, :, :], x_v[:, TT // 2:TT, :]).then_inc(xh_loaded.sem, xh_loaded.up())
            for k in range(4):
                for c in range(2):
                    b = chunk()
                    f(h_hi[:, k, c * HALF:c * HALF + HALF], ps[:, b, :], ACT.Copy,
                                   scale=gains[:, G_HEAD, k:k + 1]).then_inc(hi_ready.sem, hi_ready.up())
            for k in range(4, 8):
                for c in range(2):
                    chunk_done.add(1)
                    freed_now()
                    f(h_hi[:, k, c * HALF:c * HALF + HALF], gated[c][:, :], ACT.Copy).then_inc(
                        hi_ready.sem, hi_ready.up())
            act.wait_ge(chunk_done.sem, chunk_done.value())
            act.dma_start(mem_tok[:, :, :], mem[0, :, :].rearrange("(t p) d -> p t d", p=P)).then_inc(
                mem_loaded.sem, mem_loaded.up())
            chunk_done.add(KT)


            def square(u, src):
                freed_now()
                act.wait_ge(sq_used.sem, sq_used.value(1))
                f(sq[u][:, :], src, ACT.Square).then_inc(sq_ready.sem, sq_ready.up())
                sq_used.add(1)

            def square_loop():
                sq_used.add(2)
                x_flat = x_t[:, :, :].rearrange("p k s -> p (k s)")
                with engine_loop(act, KT // 2, [(chunk_done, 4), (sq_ready, 2), (sq_used, 2)]) as i:
                    for u in range(2):
                        chunk_done.add(2)
                        square(u, x_flat[:, bass.ds(act.snap(i * (2 * SEQ) + u * SEQ), SEQ)])

            def norm_root():
                chunk_done.add(2)
                freed_now()
                f(col[:, 0, :], col[:, 0, :], ACT.Sqrt, scale=1.0 / D, bias=EPS).then_inc(
                    std_ready.sem, std_ready.up())
                chunk_done.add(2)

            def split_hi():
                for n in range(2 * KT):
                    c, k = n // KT, n % KT
                    act.wait_ge(tmp_ready.sem, tmp_ready.next())
                    f(h_hi[:, k, c * HALF:c * HALF + HALF], tmp[n % 4][:, :], ACT.Copy).then_inc(
                        hi_ready.sem, hi_ready.up())

            square_loop()

            act.wait_ge(mem_loaded.sem, mem_loaded.value())
            act.wait_ge(sq_used.sem, sq_used.value())
            for i in range(MEMT):
                f(sq[0][:, :], mem_tok[:, i, :], ACT.Square, accum_out=ssq[:, i, 0:1]).then_inc(
                    junk_written.sem, junk_written.up())
                act.wait_ge(junk_written.sem, junk_written.value())
            f(rstd[:, 0:MEMT, 0:1], ssq[:, 0:MEMT, 0:1], ACT.Sqrt, scale=1.0 / D, bias=EPS).then_inc(
                std_ready.sem, std_ready.up())
            for k in range(KT):
                b = chunk()
                f(hm_hi[:, k, :], ps[:, b, 0:MEM], ACT.Copy, scale=gains[:, G_MKV, k:k + 1]).then_inc(
                    hi_ready.sem, hi_ready.up())
            norm_root()
            split_hi()
            chunk_done.add(2 * KT + 2 * MEMT)
            with engine_loop(act, XH, [(chunk_done, 20), (x_shift_ready, TT), (x_exp_ready, TT)]):
                chunk_done.add(4)
                for what, i in X_ORDER:
                    b = chunk_done.n % 4
                    chunk_done.add(1)
                    if what == "s":
                        act.wait_ge(x_shift_ready.sem, x_shift_ready.next())
                        f(xp[i % 4][:, :], ps[:, b, 0:MEM], ACT.Exp, bias=shift[:, i % 4:i % 4 + 1],
                                    accum_out=sums[:, i % 4:i % 4 + 1]).then_inc(x_exp_ready.sem, x_exp_ready.up())
                chunk_done.add(4)
            freed_now()
            for k in range(KT):
                f(h_hi[:, k, :], xo[:, k, :], ACT.Copy).then_inc(hi_ready.sem, hi_ready.up())
            square_loop()
            norm_root()
            split_hi()


            def up_copies(s, skip=False):
                if not skip:
                    act.wait_ge(conv_done.sem, conv_done.value(1))
                for c in range(2):
                    b = chunk()
                    f(fu[s][:, 8 + c * HALF:8 + c * HALF + HALF], ps[:, b, :], ACT.Copy).then_inc(
                        u_ready.sem, u_ready.up())

            def pair(b, downs, first=False):
                up_copies(0, first)
                act.wait_ge(conv_done.sem, conv_done.next())
                f(fg[:, :], fc[0][:, :], ACT.Gelu).then_inc(gelu_ready.sem, gelu_ready.up())
                up_copies(1, first)
                conv_done.add(1)
                chunk_done.add(16 * downs)
                act.wait_ge(z_made.sem, z_made.next())
                f(z_hi[b][:, :], fc[1][:, :], ACT.Copy).then_inc(hi_ready.sem, hi_ready.up())

            pair(0, 0, first=True)
            with engine_loop(act, (FT - 2) // 2, [(conv_done, 4), (chunk_done, 40), (u_ready, 8), (gelu_ready, 2),
                                                  (z_made, 2), (hi_ready, 2)]):
                pair(1, 1)
                pair(0, 1)
            pair(1, 1)
            sq_used.add(2)
            for m in range(KT):
                chunk_done.add(2)
                square(m % 2, x_t[:, m, :])
            norm_root()

        @block.vector
        def _(dve):
            t = View()
            chunk_done, chunk_freed, conv_done = t("chunk_done"), t("chunk_freed"), t("conv_done")
            conv_ready, decay_ready, diag_ready = t("conv_ready"), t("decay_ready"), t("diag_ready")
            f_abs_ready, gate_done, gates_ready = t("f_abs_ready"), t("gate_done"), t("gates_ready")
            gelu_ready, h_ready, hi_ready = t("gelu_ready"), t("h_ready"), t("hi_ready")
            hm_ready, hm_taken, khi_ready = t("hm_ready"), t("hm_taken"), t("khi_ready")
            ln_step, log_rows_ready, mem_scaled = t("ln_step"), t("log_rows_ready"), t("mem_scaled")
            mixed_ready, o_ready, o_stage_taken = t("mixed_ready"), t("o_ready"), t("o_stage_taken")
            o_taken, pick_ready, probs_ready = t("o_taken"), t("pick_ready"), t("probs_ready")
            pt_copied0, pt_made0, q_hi_ready = t("pt_copied0"), t("pt_made0"), t("q_hi_ready")
            q_ready, qk_ready, r_col_ready = t("q_ready"), t("qk_ready"), t("r_col_ready")
            scores_ready, shift_ready, split_ready = t("scores_ready"), t("shift_ready"), t("split_ready")
            sq_ready, sq_used, ssq_ready = t("sq_ready"), t("sq_used"), t("ssq_ready")
            std_ready, tmp_ready, u_ready = t("std_ready"), t("tmp_ready"), t("u_ready")
            vector_chain, x_exp_ready, x_scaled = t("vector_chain"), t("x_exp_ready"), t("x_scaled")
            x_shift_ready, xv_ready, y_ready = t("x_shift_ready"), t("xv_ready"), t("y_ready")
            y_t_ready, z_made, z_ready = t("y_t_ready"), t("z_made"), t("z_ready")
            params_loaded = t("params_loaded", 16)
            tt, ts, stt = dve.tensor_tensor, dve.tensor_scalar, dve.scalar_tensor_tensor

            def chunk(k=1):
                assert chunk_freed.n == chunk_done.n
                b = chunk_done.n % 4
                chunk_done.add(k)
                dve.wait_ge(chunk_done.sem, chunk_done.value())
                return b

            def both(b):
                assert b % 2 == 0
                return ps_flat[:, b * HALF:b * HALF + SEQ]

            def wait_hi():
                dve.wait_ge(hi_ready.sem, hi_ready.next())

            def low(out_lo, src, hi, gain=None):
                if gain is None:
                    return tt(out_lo, src, hi.bitcast(FP32), ALU.subtract)
                return stt(out_lo, src, gain, hi.bitcast(FP32), ALU.mult, ALU.subtract)

            for n in range(0, 4, 2):
                b = chunk()
                width = PAR_TILES[n][0] + PAR_TILES[n + 1][0]
                dve.tensor_copy(par[:, PAR_TILES[n][1]:PAR_TILES[n][1] + width], ps[:, b, 0:width]).then_inc(
                    chunk_freed.sem, chunk_freed.up())
            dve.wait_ge(chunk_freed.sem, chunk_freed.value())
            for half in range(2):
                hs = slice(4 * half, 4 * half + 4)
                dve.wait_ge(std_ready.sem, std_ready.next())
                dve.reciprocal(rstd[:, hs, 0:1], rstd[:, hs, 0:1]).then_inc(vector_chain.sem, vector_chain.up())
                dve.wait_ge(vector_chain.sem, vector_chain.value())
                for i in range(4 * half, 4 * half + 4):
                    ts(x_tok[:, i, :], x_tok[:, i, :], rstd[:, i, 0:1], None, ALU.mult).then_inc(
                        x_scaled.sem, x_scaled.up())
            for half in range(2):
                for k in range(KT):
                    b = chunk()
                    wait_hi()
                    low(h_lo[:, k, half * HALF:half * HALF + HALF], ps[:, b, :],
                             h_hi[:, k, half * HALF:half * HALF + HALF], gains[:, G_MIX, k:k + 1]).then_inc(
                                 chunk_freed.sem, chunk_freed.up())

            for z in (kc_a, kc_b, vc):
                dve.memset(whole(z).bitcast(FP32), 0.0).then_inc(vector_chain.sem, vector_chain.up())
            params_loaded.add(PARAM_LOADS)
            dve.wait_ge(params_loaded.sem, params_loaded.value())
            for kv in range(2):
                for c in range(2):
                    b = chunk()
                    for part in range(2):
                        cs = slice(c * HALF, c * HALF + HALF)
                        ins = tt(kvp[:, kv, part, cs].rearrange("p (n l) -> p n l", l=CMP_STRIDE),
                                 ps[:, b, :].rearrange("p (n l) -> p n l", l=CMP_STRIDE),
                                 pos[:, kv, None, part * CMP_STRIDE:part * CMP_STRIDE + CMP_STRIDE].to_broadcast(
                                     [P, HALF // CMP_STRIDE, CMP_STRIDE]), ALU.add)
                    ins.then_inc(chunk_freed.sem, chunk_freed.up())
            for kv in range(2):
                for g in range(G):
                    b = chunk()
                    dve.tensor_copy(hid[:, kv, g, :], ps[0:CMP_HID, b, 0:NCMP]).then_inc(
                        chunk_freed.sem, chunk_freed.up())
            b = chunk()
            dve.wait_ge(vector_chain.sem, vector_chain.value())
            for g in range(G):
                src = ps[0:DH, b, DH * g:DH * g + NCMP]
                dve.tensor_copy(kc_b[rows(1), g, 0:NCMP], src).then_inc(vector_chain.sem, vector_chain.up())
                dve.tensor_copy(kc_a[rows(0), g, 0:NCMP], src).then_inc(vector_chain.sem, vector_chain.up())
                dve.wait_ge(vector_chain.sem, vector_chain.value())
                low(kc_a[rows(1), g, 0:NCMP], src, kc_a[rows(0), g, 0:NCMP]).then_inc(
                    vector_chain.sem, vector_chain.up())
                last = low(kc_b[rows(0), g, 0:NCMP], src, kc_a[rows(0), g, 0:NCMP])
                if g == 0:
                    last.then_inc(vector_chain.sem, vector_chain.up())
            last.then_inc(chunk_freed.sem, chunk_freed.up())
            b = chunk()
            dve.tensor_copy(vc[0:NCMP, :, :], ps[0:NCMP, b, 0:P].rearrange("n (g d) -> n g d", g=G)).then_inc(
                chunk_freed.sem, chunk_freed.up())
            for br in range(2):
                for c in range(2):
                    b = chunk()
                    cs = slice(c * HALF, c * HALF + HALF)
                    for g in range(G):
                        khi_ready.add(2)
                        dve.wait_ge(khi_ready.sem, khi_ready.value())
                        low(k_a[br][rows(1 - g), g, cs], ps[rows(g), b, :], k_a[br][rows(g), g, cs]).then_inc(
                            vector_chain.sem, vector_chain.up())
                        last = low(k_b[br][rows(g), g, cs], ps[rows(g), b, :], k_a[br][rows(g), g, cs])
                        if g == 0:
                            last.then_inc(vector_chain.sem, vector_chain.up())
                    last.then_inc(chunk_freed.sem, chunk_freed.up())
                b = chunk(2)
                dve.tensor_copy(v_feat[:, br, :], both(b)).then_inc(chunk_freed.sem, chunk_freed.up(2))
            b = chunk(2)
            dve.tensor_copy(g_rows[:, :], ps_flat[0:NH * 3, b * HALF:b * HALF + SEQ]).then_inc(
                vector_chain.sem, vector_chain.up())
            dve.tensor_copy(g_i[:, :], ps_flat[R_I:R_I + MH, b * HALF:b * HALF + SEQ]).then_inc(
                vector_chain.sem, vector_chain.up())
            dve.tensor_copy(g_f[:, :], ps_flat[R_F:R_F + MH, b * HALF:b * HALF + SEQ]).then_inc(
                chunk_freed.sem, chunk_freed.up(2))
            dve.wait_ge(vector_chain.sem, vector_chain.value())
            dve.wait_ge(chunk_freed.sem, chunk_freed.value())
            ts(g_i[:, :], g_i[:, :], bias_if[:, 0:1], None, ALU.add).then_inc(vector_chain.sem, vector_chain.up())
            dve.wait_ge(vector_chain.sem, vector_chain.value())
            ts(g_f[:, :], g_f[:, :], bias_if[:, 1:2], None, ALU.add).then_inc(vector_chain.sem, vector_chain.up())
            dve.wait_ge(vector_chain.sem, vector_chain.value())
            stt(g_t[:, :], g_f[:, :], -1.0, g_f[:, :], ALU.mult, ALU.min).then_inc(f_abs_ready.sem, f_abs_ready.up())
            for k in range(4):
                b = chunk(2)
                ts(nq[:, k, :], both(b), DH ** -0.5, None, ALU.mult).then_inc(chunk_freed.sem, chunk_freed.up(2))
            ln_step.add(2)
            dve.wait_ge(ln_step.sem, ln_step.value())
            stt(g_f[:, :], g_f[:, :], 0.0, g_t[:, :], ALU.min, ALU.subtract).then_inc(
                vector_chain.sem, vector_chain.up())
            dve.wait_ge(vector_chain.sem, vector_chain.value())
            dve.tensor_tensor_scan(g_t[:, :], g_f[:, :], g_f[:, :], 0.0, ALU.add, ALU.min).then_inc(
                vector_chain.sem, vector_chain.up())
            dve.wait_ge(vector_chain.sem, vector_chain.value())
            tt(g_i[:, :], g_i[:, :], g_t[:, :], ALU.subtract).then_inc(vector_chain.sem, vector_chain.up())
            dve.wait_ge(vector_chain.sem, vector_chain.value())
            dve.tensor_tensor_scan(m_rows[:, :], g_i[:, :], g_i[:, :], 0.0, ALU.max, ALU.max).then_inc(
                vector_chain.sem, vector_chain.up())
            dve.wait_ge(vector_chain.sem, vector_chain.value())
            tt(g_f[:, :], g_t[:, :], m_rows[:, :], ALU.add).then_inc(log_rows_ready.sem, log_rows_ready.up())
            for br in range(2):
                for q in range(2):
                    b = chunk()
                    dve.tensor_copy(v_tok[:, br, 4 * q:4 * q + 4, :],
                                         ps[:, b, :].rearrange("p (t d) -> p t d", d=P)).then_inc(
                                             chunk_freed.sem, chunk_freed.up())
            b = chunk()
            dve.tensor_copy(gate_sig[:, :, :],
                                 ps[:, b, 0:TT * 32].rearrange("p (t h) -> p t h", h=32)[:, :, 0:NH * 3]).then_inc(
                                     chunk_freed.sem, chunk_freed.up())
            b = chunk()
            dve.tensor_copy(log_in[:, :, :], ps[:, b, 0:TT * MH].rearrange("p (t h) -> p t h", h=MH)).then_inc(
                o_stage_taken.sem, o_stage_taken.up())
            dve.tensor_copy(den_floor[:, :, :], ps[:, b, 64:64 + TT * MH].rearrange("p (t h) -> p t h", h=MH)).then_inc(
                chunk_freed.sem, chunk_freed.up())
            dve.wait_ge(gates_ready.sem, gates_ready.next())

            CH_B = 2 + 2 * JOBS + JOBS + 2
            loop = lambda n, k: engine_loop(dve, n, [(q_hi_ready, 2 * k), (q_ready, 2 * k), (probs_ready, k * JOBS),
                                                     (scores_ready, k * JOBS), (shift_ready, k * JOBS), (pt_made0, k * JOBS),
                                                     (pt_copied0, k * JOBS), (o_ready, k * JOBS), (o_taken, k * JOBS),
                                                     (o_stage_taken, 2 * k), (vector_chain, k * CH_B)])
            with loop(G, 2) as g:
                with loop(2, 1) as hp:
                    at_q = dve.snap((g * 2 + hp) * SEQ)
                    at_h = dve.snap((g * 2 + hp) * 6)
                    nq_flat = nq[:, :, :].rearrange("p a s -> p (a s)")
                    q_hi_ready.add(2)
                    dve.wait_ge(q_hi_ready.sem, q_hi_ready.value())
                    for u in range(2):
                        low(q_st[u][rows(1 - u), :], nq_flat[rows(u), bass.ds(at_q, SEQ)], q_st[u][rows(u), :]).then_inc(
                            q_ready.sem, q_ready.up())
                    for u in range(2):
                        dve.tensor_copy(gate_h[:, u, :, :], gate_sig[:, :, bass.ds(at_h + 3 * u, 3)]).then_inc(
                            vector_chain.sem, vector_chain.up())
                    for st in range(JOBS + 4):
                        z = st - 4
                        if 0 <= z < JOBS:
                            u, i, br = job_of(z)
                            c0 = 2 * (z % 4)
                            o = ps[:, 6 + z % 2, :]
                            dve.wait_ge(probs_ready.sem, probs_ready.next())
                            if z == 0:
                                dve.wait_ge(o_stage_taken.sem, o_stage_taken.value())
                            if br == 0:
                                dve.reciprocal(coef[:, c0:c0 + 1], sums[:, c0:c0 + 1]).then_inc(
                                    vector_chain.sem, vector_chain.up())
                                dve.wait_ge(vector_chain.sem, vector_chain.value())
                                tt(coef[:, c0:c0 + 1], coef[:, c0:c0 + 1], gate_h[:, u, i, 1:2], ALU.mult).then_inc(
                                    vector_chain.sem, vector_chain.up())
                                dve.wait_ge(vector_chain.sem, vector_chain.value())
                                dve.wait_ge(o_ready.sem, o_ready.next())
                                ts(o_stage[:, u, i, :], o[:, 0:DH], coef[:, c0:c0 + 1], None, ALU.mult).then_inc(
                                    o_taken.sem, o_taken.up())
                            else:
                                dve.reciprocal(coef[:, c0:c0 + 2], sums[:, c0:c0 + 2]).then_inc(
                                    vector_chain.sem, vector_chain.up())
                                dve.wait_ge(vector_chain.sem, vector_chain.value())
                                tt(coef[:, c0:c0 + 2], coef[:, c0:c0 + 2], gate_h[:, u, i, 0:3:2], ALU.mult).then_inc(
                                    vector_chain.sem, vector_chain.up())
                                dve.wait_ge(vector_chain.sem, vector_chain.value())
                                if i == 0:
                                    tt(coef[:, c0:c0 + 1], coef[:, c0:c0 + 1], keep_cmp[:, :], ALU.mult).then_inc(
                                        vector_chain.sem, vector_chain.up())
                                    dve.wait_ge(vector_chain.sem, vector_chain.value())
                                dve.wait_ge(o_ready.sem, o_ready.next())
                                dve.wait_ge(o_taken.sem, o_taken.value())
                                stt(o_stage[:, u, i, :], o[:, 0:DH], coef[:, c0 + 1:c0 + 2],
                                                 o_stage[:, u, i, :], ALU.mult, ALU.add).then_inc(
                                                     vector_chain.sem, vector_chain.up())
                                dve.wait_ge(vector_chain.sem, vector_chain.value())
                                stt(o_stage[:, u, i, :], o[:, DH:2 * DH], coef[:, c0:c0 + 1],
                                                o_stage[:, u, i, :], ALU.mult, ALU.add).then_inc(
                                                    o_taken.sem, o_taken.up())
                        if st < JOBS:
                            u, i, br = job_of(st)
                            n = (i + 1 if br == 0 else min(i, WT) + 1) * P
                            c0 = 2 * (st % 4)
                            flat = ps_flat[:, 2 * (st % 2) * HALF:2 * (st % 2) * HALF + 2 * HALF]
                            dve.wait_ge(scores_ready.sem, scores_ready.next())
                            if br == 0:
                                dve.tensor_reduce(shift[:, c0:c0 + 1], flat[:, 0:n], AX.X, ALU.max,
                                                                  negate=True).then_inc(
                                                                      shift_ready.sem, shift_ready.up())
                            else:
                                dve.tensor_reduce(shift[:, c0 + 1:c0 + 2], flat[:, 0:n], AX.X, ALU.max, negate=True).then_inc(
                                    vector_chain.sem, vector_chain.up())
                                dve.tensor_reduce(shift[:, c0:c0 + 1], flat[:, 5 * P:5 * P + DH], AX.X,
                                                                  ALU.max, negate=True).then_inc(
                                                                      shift_ready.sem, shift_ready.up())
                        z = st - 2
                        if 0 <= z < JOBS:
                            u, i, br = job_of(z)
                            n = i + 1 if br == 0 else min(i, WT) + 1
                            dve.wait_ge(pt_made0.sem, pt_made0.next())
                            dve.tensor_copy(probs_t[z % 2][:, 0:min(n, 4), :],
                                                    ps[:, 4, 0:min(n, 4) * P].rearrange("p (a k) -> p a k", k=P)).then_inc(
                                                        pt_copied0.sem, pt_copied0.up())
                    o_stage_taken.add(2)

            dve.memset(u_raw[:, 0:4], 0.0).then_inc(vector_chain.sem, vector_chain.up())
            dve.memset(mv_tok[:, :, MDH:MDH + 1], 1.0).then_inc(hm_taken.sem, hm_taken.up())
            CH_C = 39
            with engine_loop(dve, MH, [(chunk_done, 32), (chunk_freed, 32), (vector_chain, CH_C), (conv_ready, 2), (hi_ready, 2),
                                       (qk_ready, 1), (pick_ready, 1), (diag_ready, 1),
                                       (decay_ready, 12), (hm_ready, 1), (hm_taken, 1)]) as h:
                dve.tensor_copy(head_w[:, 0, :], conv_m[:, :, bass.ds(h, 1)]).then_inc(
                    vector_chain.sem, vector_chain.up())
                dve.tensor_copy(head_w[:, 1, :], conv_m[:, :, bass.ds(dve.snap(h + MH), 1)]).then_inc(
                    vector_chain.sem, vector_chain.up())
                dve.tensor_copy(head_a[:, 0, :], log_in[:, :, bass.ds(h, 1)]).then_inc(
                    vector_chain.sem, vector_chain.up())
                dve.tensor_copy(head_a[:, 1, :], den_floor[:, :, bass.ds(h, 1)]).then_inc(
                    vector_chain.sem, vector_chain.up())
                ts(m_pick[:, :], ident[0:MH, bass.ds(h, 1)].to_broadcast([MH, P]), -1.0, None, ALU.mult).then_inc(
                    pick_ready.sem, pick_ready.up())
                dve.wait_ge(hm_taken.sem, hm_taken.value())
                for s, (hi, lo, scale) in enumerate(((mq_hi, mq_lo, MDH ** -0.5), (mk_hi, mk_lo, 1.0))):
                    b = chunk(2)
                    dve.tensor_copy(u_raw[:, 4:4 + SEQ], both(b)).then_inc(chunk_freed.sem, chunk_freed.up(2))
                    dve.wait_ge(chunk_freed.sem, chunk_freed.value())
                    dve.wait_ge(vector_chain.sem, vector_chain.value())
                    ts(u_conv[:, :], u_raw[:, 4:4 + SEQ], head_w[:, s, TAPS - 1:TAPS], None, ALU.mult).then_inc(
                        vector_chain.sem, vector_chain.up())
                    dve.wait_ge(vector_chain.sem, vector_chain.value())
                    for k in range(1, TAPS):
                        ins = stt(u_conv[:, :], u_raw[:, 4 - k:4 - k + SEQ], head_w[:, s, TAPS - 1 - k:TAPS - k],
                                  u_conv[:, :], ALU.mult, ALU.add)
                        if k < TAPS - 1:
                            ins.then_inc(vector_chain.sem, vector_chain.up())
                            dve.wait_ge(vector_chain.sem, vector_chain.value())
                    ins.then_inc(conv_ready.sem, conv_ready.up())
                    wait_hi()
                    ins = low(lo[:, :], u_conv[:, :], hi[:, :], scale)
                    if s == 0:
                        ins.then_inc(vector_chain.sem, vector_chain.up())
                    else:
                        ins.then_inc(qk_ready.sem, qk_ready.up())
                b = chunk(2)
                dve.tensor_copy(mv_feat[:, :], both(b)).then_inc(chunk_freed.sem, chunk_freed.up(2))
                b = chunk(2)
                dve.tensor_copy(o_gate[:, bass.ds(h, 1), :], both(b)).then_inc(chunk_freed.sem, chunk_freed.up(2))
                b = chunk(2)
                dve.tensor_copy(m_bc[:, :], both(b)).then_inc(chunk_freed.sem, chunk_freed.up(2))
                dve.wait_ge(chunk_freed.sem, chunk_freed.value())
                dve.wait_ge(qk_ready.sem, qk_ready.value())
                for j in range(TT):
                    js = slice(j * P, j * P + P)
                    ins = stt(u_conv[:, js], m_bc[:, js], head_a[:, 0, j:j + 1], mmask[:, :], ALU.add, ALU.min)
                    if j < TT - 1:
                        ins.then_inc(vector_chain.sem, vector_chain.up())
                ins.then_inc(diag_ready.sem, diag_ready.up())
                for q in range(2):
                    b = chunk()
                    dve.tensor_copy(mv_tok[:, 4 * q:4 * q + 4, 0:MDH],
                                         ps[:, b, :].rearrange("p (t d) -> p t d", d=P)).then_inc(
                                             chunk_freed.sem, chunk_freed.up())
                decay_ready.add(1)
                for n, (j, a, e) in enumerate(pieces):
                    b = chunk()
                    a2 = a + P if a == P * j else a
                    first = tri_at(j, a // P)
                    if a2 < e:
                        decay_ready.add(1)
                    dve.wait_ge(decay_ready.sem, decay_ready.value())
                    if a2 > a:
                        ins = tt(tri[:, first, :], ps[:, b, 0:P], u_conv[:, j * P:j * P + P], ALU.mult)
                        if a2 < e:
                            ins.then_inc(vector_chain.sem, vector_chain.up())
                    if a2 < e:
                        at_blk = first + (a2 - a) // P
                        ins = tt(tri[:, at_blk:at_blk + (e - a2) // P, :].rearrange("p b t -> p (b t)"),
                                 ps[:, b, a2 - a:e - a], decay[n % 2][:, 0:e - a2], ALU.mult)
                    ins.then_inc(chunk_freed.sem, chunk_freed.up())
                hv = u_raw[:, 4:4 + SEQ].rearrange("p (t d) -> p t d", d=MDH)
                for i in range(TT):
                    b = chunk()
                    dve.tensor_copy(hv[:, i, :], ps[:, b, 0:MDH]).then_inc(vector_chain.sem, vector_chain.up())
                    dve.tensor_copy(head_d[:, 0, i:i + 1], ps[:, b, MDH:MDH + 1]).then_inc(
                        chunk_freed.sem, chunk_freed.up())
                dve.wait_ge(chunk_freed.sem, chunk_freed.value())
                stt(head_d[:, 1, :], head_d[:, 0, :], -1.0, head_d[:, 0, :], ALU.mult, ALU.max).then_inc(
                    vector_chain.sem, vector_chain.up())
                dve.wait_ge(vector_chain.sem, vector_chain.value())
                tt(head_d[:, 1, :], head_d[:, 1, :], head_a[:, 1, :], ALU.max).then_inc(
                    vector_chain.sem, vector_chain.up())
                dve.wait_ge(vector_chain.sem, vector_chain.value())
                dve.reciprocal(head_d[:, 1, :], head_d[:, 1, :]).then_inc(vector_chain.sem, vector_chain.up())
                dve.wait_ge(vector_chain.sem, vector_chain.value())
                cv = u_conv[:, :].rearrange("p (t d) -> p t d", d=MDH)
                tt(cv, hv, head_d[:, 1, :, None].to_broadcast([P, TT, MDH]), ALU.mult).then_inc(
                    hm_ready.sem, hm_ready.up())
                dve.wait_ge(hm_ready.sem, hm_ready.value())
                tt(hv, cv, cv, ALU.mult).then_inc(vector_chain.sem, vector_chain.up())
                dve.wait_ge(vector_chain.sem, vector_chain.value())
                dve.tensor_reduce(head_d[:, 2, :], hv, AX.X, ALU.add).then_inc(vector_chain.sem, vector_chain.up())
                dve.wait_ge(vector_chain.sem, vector_chain.value())
                dve.tensor_copy(ssq[:, :, bass.ds(dve.snap(h + NH), 1)], head_d[:, 2, :, None]).then_inc(
                    vector_chain.sem, vector_chain.up())
                hm_taken.add(1)

            dve.wait_ge(hm_taken.sem, hm_taken.value())
            dve.wait_ge(vector_chain.sem, vector_chain.value())
            nsa_sq = x_t[:, 0:4, :].rearrange("p k s -> p (k s)")
            nsa_v = o_nsa[:, :, :].rearrange("p t d -> p (t d)")
            tt(nsa_sq, nsa_v, nsa_v, ALU.mult).then_inc(vector_chain.sem, vector_chain.up())
            dve.wait_ge(vector_chain.sem, vector_chain.value())
            dve.tensor_reduce(ssq[:, :, 0:NH], nsa_sq.rearrange("p (t h d) -> p t h d", h=NH, d=DH),
                                                 AX.X, ALU.add).then_inc(ssq_ready.sem, ssq_ready.up())
            std_ready.add(2)
            dve.wait_ge(std_ready.sem, std_ready.value())
            dve.reciprocal(rstd[:, :, :], rstd[:, :, :]).then_inc(vector_chain.sem, vector_chain.up())
            dve.wait_ge(vector_chain.sem, vector_chain.value())
            for i in range(TT):
                tt(o_nsa[:, i, :].rearrange("p (h d) -> p h d", d=DH),
                          o_nsa[:, i, :].rearrange("p (h d) -> p h d", d=DH),
                          rstd[:, i, 0:NH, None].to_broadcast([P, NH, DH]), ALU.mult).then_inc(
                              vector_chain.sem, vector_chain.up())
                ins = tt(h_mls[:, i, :].rearrange("p (h d) -> p h d", d=MDH),
                         h_mls[:, i, :].rearrange("p (h d) -> p h d", d=MDH),
                         rstd[:, i, NH:NH + MH, None].to_broadcast([P, MH, MDH]), ALU.mult)
                if i < TT - 1:
                    ins.then_inc(vector_chain.sem, vector_chain.up())
            ins.then_inc(mixed_ready.sem, mixed_ready.up())

            def residual_copies(half):
                for k in range(KT):
                    b = chunk()
                    dve.tensor_copy(x_t[:, k, half * HALF:half * HALF + HALF], ps[:, b, :]).then_inc(
                        chunk_freed.sem, chunk_freed.up())

            residual_copies(0)
            for k in range(4):
                for c in range(2):
                    b = chunk()
                    wait_hi()
                    cs = slice(c * HALF, c * HALF + HALF)
                    low(h_lo[:, k, cs], ps[:, b, :], h_hi[:, k, cs], gains[:, G_HEAD, k:k + 1]).then_inc(
                        chunk_freed.sem, chunk_freed.up())
            dve.wait_ge(gate_done.sem, gate_done.next())
            for n in range(8):
                k, c = 4 + n // 2, n % 2
                cs = slice(c * HALF, c * HALF + HALF)
                b = chunk()
                stt(gated[c][:, :], ps[:, b, :], gains[:, G_HEAD, k:k + 1], o_gate[:, k - 4, cs], ALU.mult, ALU.mult).then_inc(
                    chunk_freed.sem, chunk_freed.up())
                dve.wait_ge(chunk_freed.sem, chunk_freed.value())
                wait_hi()
                low(h_lo[:, k, cs], gated[c][:, :], h_hi[:, k, cs]).then_inc(split_ready.sem, split_ready.up())
            residual_copies(1)


            def clear_sums():
                for c in range(2):
                    dve.memset(acc[:, c * HALF:c * HALF + HALF], 0.0).then_inc(sq_used.sem, sq_used.up())
                    dve.wait_ge(sq_used.sem, sq_used.value())

            def add_square(u):
                dve.wait_ge(sq_ready.sem, sq_ready.next())
                dve.wait_ge(sq_used.sem, sq_used.value())
                tt(acc[:, :], acc[:, :], sq[u][:, :], ALU.add).then_inc(sq_used.sem, sq_used.up())

            def residual_loop():
                clear_sums()
                with engine_loop(dve, KT // 2, [(chunk_done, 4), (chunk_freed, 4), (sq_ready, 2), (sq_used, 2)]) as i:
                    x_flat = x_t[:, :, :].rearrange("p k s -> p (k s)")
                    for u in range(2):
                        b = chunk(2)
                        dst = x_flat[:, bass.ds(dve.snap(i * (2 * SEQ) + u * SEQ), SEQ)]
                        tt(dst, both(b), dst, ALU.add).then_inc(chunk_freed.sem, chunk_freed.up(2))
                    for u in range(2):
                        add_square(u)
                dve.wait_ge(chunk_freed.sem, chunk_freed.value())

            def norm_columns():
                for c in range(2):
                    b = chunk()
                    dve.tensor_copy(col[:, 0, 4 * c:4 * c + 4], ps[:, b, 0:4]).then_inc(
                        chunk_freed.sem, chunk_freed.up())
                dve.wait_ge(std_ready.sem, std_ready.next())
                dve.reciprocal(col[:, 0, :], col[:, 0, :]).then_inc(r_col_ready.sem, r_col_ready.up())
                for c in range(2):
                    b = chunk()
                    dve.tensor_copy(r_bc[:, c * HALF:c * HALF + HALF], ps[:, b, :]).then_inc(
                        chunk_freed.sem, chunk_freed.up())
                dve.wait_ge(chunk_freed.sem, chunk_freed.value())

            def normed(dst, k, c, gain):
                cs = slice(c * HALF, c * HALF + HALF)
                return stt(dst, x_t[:, k, cs], gains[:, gain, k:k + 1], r_bc[:, cs], ALU.mult, ALU.mult)

            def split_low(gain):
                normed(tmp[0][:, :], 0, 0, gain).then_inc(tmp_ready.sem, tmp_ready.up())
                for n in range(2 * KT):
                    c, k = n // KT, n % KT
                    if n + 1 < 2 * KT:
                        normed(tmp[(n + 1) % 4][:, :], (n + 1) % KT, (n + 1) // KT, gain).then_inc(
                            tmp_ready.sem, tmp_ready.up())
                    wait_hi()
                    cs = slice(c * HALF, c * HALF + HALF)
                    low(h_lo[:, k, cs], tmp[n % 4][:, :], h_hi[:, k, cs]).then_inc(h_ready.sem, h_ready.up())

            residual_loop()

            dve.wait_ge(std_ready.sem, std_ready.next())
            dve.reciprocal(rstd[:, 0:MEMT, 0:1], rstd[:, 0:MEMT, 0:1]).then_inc(vector_chain.sem, vector_chain.up())
            dve.wait_ge(vector_chain.sem, vector_chain.value())
            for i in range(MEMT):
                ins = ts(mem_tok[:, i, :], mem_tok[:, i, :], rstd[:, i, 0:1], None, ALU.mult)
                if i < MEMT - 1:
                    ins.then_inc(vector_chain.sem, vector_chain.up())
            ins.then_inc(mem_scaled.sem, mem_scaled.up())
            for k in range(KT):
                b = chunk()
                wait_hi()
                low(hm_lo[:, k, :], ps[:, b, 0:MEM], hm_hi[:, k, :], gains[:, G_MKV, k:k + 1]).then_inc(
                    chunk_freed.sem, chunk_freed.up())
            norm_columns()
            split_low(G_MQ)
            for dst in (xk, xv_feat):
                with engine_loop(dve, KT // 4, [(chunk_done, 4), (chunk_freed, 4)]) as i:
                    flat = dst[:, :, :].rearrange("p k m -> p (k m)")
                    for u in range(4):
                        b = chunk()
                        dve.tensor_copy(flat[:, bass.ds(dve.snap(i * (4 * MEM) + u * MEM), MEM)], ps[:, b, 0:MEM]).then_inc(
                            chunk_freed.sem, chunk_freed.up())
            for j in range(MEMT):
                for q in range(2):
                    b = chunk()
                    dve.tensor_copy(xv[:, j, q * HALF:q * HALF + HALF], ps[:, b, :]).then_inc(
                        chunk_freed.sem, chunk_freed.up())
            dve.wait_ge(chunk_freed.sem, chunk_freed.value())
            with engine_loop(dve, XH, [(chunk_done, 20), (chunk_freed, 20), (x_shift_ready, TT), (x_exp_ready, TT), (vector_chain, TT),
                                       (xv_ready, 1)]) as hd:
                dve.tensor_copy(xv_h[:, :, :], xv[:, :, bass.ds(dve.snap(hd * XDH), XDH)]).then_inc(
                    xv_ready.sem, xv_ready.up())
                for z in range(2):
                    b = chunk(2)
                    ts(xq[:, z, :], both(b), XDH ** -0.5, None, ALU.mult).then_inc(chunk_freed.sem, chunk_freed.up(2))
                waiting = []

                def finish():
                    i = waiting.pop(0)
                    dve.wait_ge(x_exp_ready.sem, x_exp_ready.next())
                    dve.reciprocal(sums[:, i % 4:i % 4 + 1], sums[:, i % 4:i % 4 + 1]).then_inc(
                        vector_chain.sem, vector_chain.up())
                    dve.wait_ge(vector_chain.sem, vector_chain.value())
                    ts(xp[i % 4][:, :], xp[i % 4][:, :], sums[:, i % 4:i % 4 + 1], None, ALU.mult).then_inc(
                        chunk_freed.sem, chunk_freed.up())

                for what, i in X_ORDER:
                    if what == "s":
                        b = chunk_done.n % 4
                        dve.wait_ge(chunk_done.sem, chunk_done.next())
                        dve.tensor_reduce(shift[:, i % 4:i % 4 + 1], ps[:, b, 0:MEM], AX.X, ALU.max,
                                                      negate=True).then_inc(x_shift_ready.sem, x_shift_ready.up())
                        waiting.append(i)
                        if len(waiting) > 1:
                            finish()
                    else:
                        while waiting:
                            finish()
                        b = chunk()
                        dve.tensor_copy(xp_t[:, :, i * P:i * P + 2 * P],
                                             ps[:, b, :].rearrange("p (j q) -> p j q", j=MEMT)).then_inc(
                                                 chunk_freed.sem, chunk_freed.up())
                x_flat = xo[:, :, :].rearrange("p k s -> p (k s)")
                for z in range(2):
                    b = chunk(2)
                    dve.tensor_copy(x_flat[:, bass.ds(dve.snap(hd * (2 * SEQ) + z * SEQ), SEQ)], both(b)).then_inc(
                        chunk_freed.sem, chunk_freed.up(2))
            dve.wait_ge(chunk_freed.sem, chunk_freed.value())
            for k in range(KT):
                wait_hi()
                low(h_lo[:, k, :], xo[:, k, :], h_hi[:, k, :]).then_inc(h_ready.sem, h_ready.up())
            residual_loop()
            norm_columns()
            split_low(G_FFN)

            for s in range(2):
                dve.memset(fu[s][:, 0:8], 0.0).then_inc(vector_chain.sem, vector_chain.up())
            dve.wait_ge(vector_chain.sem, vector_chain.value())

            def taps_start(s):
                for c in range(2):
                    b = chunk()
                    dve.wait_ge(u_ready.sem, u_ready.next())
                    ts(fc[s][:, c * HALF:c * HALF + HALF], ps[:, b, :], fw[:, s, FTAPS - 1:FTAPS], None, ALU.mult).then_inc(
                        chunk_freed.sem, chunk_freed.up())

            def taps_rest(s):
                dve.wait_ge(chunk_freed.sem, chunk_freed.value())
                for k in range(1, FTAPS):
                    ins = stt(fc[s][:, :], fu[s][:, 8 - k:8 - k + SEQ], fw[:, s, FTAPS - 1 - k:FTAPS - k], fc[s][:, :],
                              ALU.mult, ALU.add)
                    if k < FTAPS - 1:
                        ins.then_inc(vector_chain.sem, vector_chain.up())
                        dve.wait_ge(vector_chain.sem, vector_chain.value())
                ins.then_inc(conv_done.sem, conv_done.up())

            def down_tiles():
                for m in range(KT):
                    b = chunk(2)
                    tt(x_t[:, m, :], both(b), x_t[:, m, :], ALU.add).then_inc(chunk_freed.sem, chunk_freed.up(2))

            def pair(b, p, downs):
                at_p = [p + s * FT if isinstance(p, int) else dve.snap(p + s * FT) for s in range(2)]
                dve.tensor_copy(fw[:, 0, :], conv_f[:, :, bass.ds(at_p[0], 1)]).then_inc(
                    vector_chain.sem, vector_chain.up())
                dve.tensor_copy(fw[:, 1, :], conv_f[:, :, bass.ds(at_p[1], 1)]).then_inc(
                    vector_chain.sem, vector_chain.up())
                dve.wait_ge(vector_chain.sem, vector_chain.value())
                taps_start(0)
                taps_rest(0)
                taps_start(1)
                if downs:
                    down_tiles()
                taps_rest(1)
                dve.wait_ge(conv_done.sem, conv_done.value())
                dve.wait_ge(gelu_ready.sem, gelu_ready.next())
                tt(fc[1][:, :], fg[:, :], fc[1][:, :], ALU.mult).then_inc(z_made.sem, z_made.up())
                dve.wait_ge(z_made.sem, z_made.value())
                wait_hi()
                low(z_lo[b][:, :], fc[1][:, :], z_hi[b][:, :]).then_inc(z_ready.sem, z_ready.up())

            pair(0, 0, 0)
            with engine_loop(dve, (FT - 2) // 2, [(chunk_done, 40), (chunk_freed, 40), (vector_chain, 8), (conv_done, 4), (u_ready, 8),
                                                  (gelu_ready, 2), (z_made, 2), (z_ready, 2),
                                                  (hi_ready, 2)]) as i:
                pair(1, i * 2 + 1, 1)
                pair(0, i * 2 + 2, 1)
            pair(1, FT - 1, 1)
            clear_sums()
            for m in range(KT):
                b = chunk(2)
                tt(x_t[:, m, :], both(b), x_t[:, m, :], ALU.add).then_inc(chunk_freed.sem, chunk_freed.up(2))
                if m:
                    add_square((m - 1) % 2)
            add_square((KT - 1) % 2)

            norm_columns()
            for n in range(2 * KT):
                c, k = n // KT, n % KT
                normed(y_t[:, k, c * HALF:c * HALF + HALF], k, c, G_FIN).then_inc(y_t_ready.sem, y_t_ready.up())
            stored = [t(f"stored{b}", 16) for b in range(4)]
            for n in range(2 * TT):
                b = chunk()
                if n >= 4:
                    stored[n % 4].add(1)
                    dve.wait_ge(stored[n % 4].sem, stored[n % 4].value())
                dve.tensor_copy(y_tok[n % 4][:, :], ps[:, b, :]).then_inc(y_ready.sem, y_ready.up())
                chunk_freed.n += 1


_INS = ["x", "mem", "g_mix", "w_in", "cmp_pos_k", "cmp_w1_k", "cmp_w2_k", "cmp_pos_v", "cmp_w1_v", "cmp_w2_v",
        "mlstm_conv_w", "mlstm_b_i", "mlstm_b_f", "g_head_nsa", "g_head_mlstm", "w_out", "g_mem_q", "g_mem_kv",
        "w_mem_q", "w_mem_k", "w_mem_v", "w_mem_o", "g_ffn", "w_up", "ffn_conv_w", "w_down", "g_final"]


def kernel(**inputs):
    import numpy as np
    import concourse.bacc as bacc
    from concourse.bass_utils import run_bass_kernel_spmd

    nc = bacc.Bacc("TRN2", target_bir_lowering=False, num_devices=1)
    arrays, args = {}, []
    for name in _INS:
        a = np.ascontiguousarray(inputs[name])
        arrays[f"in_{name}"] = a
        args.append(nc.dram_tensor(f"in_{name}", a.shape, mybir.dt.from_np(a.dtype), kind="ExternalInput").ap())
    args.append(nc.dram_tensor("out_y", (1, SEQ, D), FP32, kind="ExternalOutput").ap())
    build(nc, *args)
    r = run_bass_kernel_spmd(nc, [arrays], core_ids=[0])
    return r.results[0]["out_y"]
```

```python
from contextlib import ExitStack, contextmanager

import concourse.bass as bass
from concourse import mybir

FP32 = mybir.dt.float32
FP32R = mybir.dt.float32r
ACT = mybir.ActivationFunctionType
ALU = mybir.AluOpType
AX = mybir.AxisListType

P = 128
D = 1024
SEQ = 1024
KT = D // P
TT = SEQ // P
HALF = 512
NH, G, DH = 8, 2, 64
CMP_LEN, CMP_STRIDE, CMP_HID = 32, 16, 64
NCMP = (SEQ - CMP_LEN) // CMP_STRIDE + 1
WT = 512 // P
MH, MDH, TAPS = 4, 128, 4
MEMT = 256 // P
MEM = 256
XH, XDH = 4, 256
FF = 2816
FT = FF // P
FTAPS = 3
EPS = 1e-6
NEG = -1e30
C_Q, C_KC, C_VC, C_KS, C_VS, C_KW, C_VW, C_GT = 0, 512, 640, 768, 896, 1024, 1152, 1280
C_MQ, C_MK, C_MV, C_MO, C_MI, C_MF = 1304, 1816, 2328, 2840, 3352, 3356
R_I, R_F = 32, 64


PARAM_LOADS = 18
Q_SPLITS = (2, 2 * TT + 3)
JOB_ORDER = [(k % TT, k // TT) for k in range(2 * TT)]
FIRST_KV = 11 + 4 * MH + KT
TILES = FIRST_KV + 4 * KT + 3 * FT
JOBS = 2 * 2 * TT


def job_of(j):
    return (j // (2 * TT), *JOB_ORDER[j % (2 * TT)])


def comes_first(j):
    u, i, br = job_of(j)
    return JOB_ORDER.index((i, br)) < JOB_ORDER.index((i, 1 - br))


def has_second(j):
    _, i, br = job_of(j)
    return br == 1 or i >= 4


X_ORDER = [("s", 0), ("s", 1), ("s", 2), ("s", 3), ("t", 0), ("s", 4), ("s", 5), ("t", 2),
           ("s", 6), ("s", 7), ("v", 0), ("t", 4), ("v", 1), ("t", 6), ("v", 2), ("v", 3)]
JOBS_1 = sum(has_second(j) for j in range(JOBS))


class Tally:

    def __init__(self, sem, step=1):
        self.sem, self.step, self.n, self.loops = sem, step, 0, []

    def add(self, k=1):
        self.n += k

    def value(self, behind=0):
        v = (self.n - behind) * self.step
        assert v > 0
        for i, per in self.loops:
            v = i * (per * self.step) + v
        return v

    def past(self, k):
        return bool(self.loops) or self.n > k

    def next(self):
        self.n += 1
        return self.value()

    def up(self, k=1):
        self.n += k
        return self.step * k


class Ring:

    def __init__(self, chunk_done):
        self.chunks, self.size, self.start = chunk_done, 4, 0

    def resize(self, size):
        self.size, self.start = size, self.chunks.n

    def bank(self):
        return (self.chunks.n - self.start) % self.size


@contextmanager
def engine_loop(eng, turns, per_turn):
    with eng.Fori(0, turns) as i:
        began = {t: t.n for t, _ in per_turn}
        for t, per in per_turn:
            t.loops.append((i, per))
        yield i
        off = [(t.sem, t.n - began[t], per) for t, per in per_turn if t.n - began[t] != per]
        assert not off, off
        for t, per in per_turn:
            t.loops.pop()
            t.n = began[t] + per * turns


def build(nc, x, mem, g_mix, w_in, cmp_pos_k, cmp_w1_k, cmp_w2_k, cmp_pos_v, cmp_w1_v, cmp_w2_v,
          mlstm_conv_w, mlstm_b_i, mlstm_b_f, g_head_nsa, g_head_mlstm, w_out, g_mem_q, g_mem_kv,
          w_mem_q, w_mem_k, w_mem_v, w_mem_o, g_ffn, w_up, ffn_conv_w, w_down, g_final, out):
    ctx = ExitStack()
    with ctx:
        KB = 1024
        BASE = 16 * KB + 128
        END = 229344

        def at(name, offset, shape, dt=FP32):
            size = 4
            for s in shape[1:]:
                size *= s
            assert BASE + offset + size <= END, (name, BASE + offset + size - END)
            return nc.alloc_sbuf_tensor_at(name, shape, dt, offset=BASE + offset)

        cursor = [0]

        def keep(name, shape, dt=FP32):
            size = 4
            for s in shape[1:]:
                size *= s
            t = at(name, cursor[0], shape, dt)
            cursor[0] += (size + 31) // 32 * 32
            return t

        h_hi = keep("h_hi", [P, KT, SEQ], FP32R)
        h_lo = keep("h_lo", [P, KT, SEQ], FP32R)
        w_raw = [keep(f"w_raw{s}", [P, KT * P]) for s in range(2)]
        w_hi = [keep(f"w_hi{s}", [P, KT * P], FP32R) for s in range(2)]
        w_lo = [keep(f"w_lo{s}", [P, KT * P], FP32R) for s in range(2)]
        ident = keep("ident", [P, P])
        ones = keep("ones", [P, 1])
        N_GAIN, N_CM, N_POS, N_CF = 6 * KT, TAPS * 2 * MH, 2 * CMP_LEN, FTAPS * 2 * FT
        par = keep("par", [P, N_GAIN + N_CM + N_POS + N_CF])
        par_rows = at("par_rows", KB * 160, [P, 4, P])
        gains = par[:, 0:N_GAIN].rearrange("p (n k) -> p n k", k=KT)
        G_MIX, G_HEAD, G_MQ, G_MKV, G_FFN, G_FIN = range(6)
        conv_m = par[:, N_GAIN:N_GAIN + N_CM].rearrange("p (t k) -> p t k", t=TAPS)
        pos = par[:, N_GAIN + N_CM:N_GAIN + N_CM + N_POS].rearrange("p (a l) -> p a l", a=2)
        conv_f = par[:, N_GAIN + N_CM + N_POS:].rearrange("p (t k) -> p t k", t=FTAPS)
        PAR_TILES = [(N_GAIN + N_CM, 0), (N_POS, N_GAIN + N_CM), (2 * 2 * FT, N_GAIN + N_CM + N_POS),
                     (2 * FT, N_GAIN + N_CM + N_POS + 2 * 2 * FT)]
        bias_if = keep("bias_if", [MH, 2])
        gate_sig = keep("gate_sig", [P, TT, NH * 3])
        log_in = keep("log_in", [P, TT, MH])
        den_floor = keep("den_floor", [P, TT, MH])
        ssq = keep("ssq", [P, TT, NH + MH])
        rstd = keep("rstd", [P, TT, NH + MH])
        sums = keep("sums", [P, 8])
        shift = keep("shift", [P, 8])
        coef = keep("coef", [P, 8])
        fw = keep("fw", [P, 2, FTAPS])
        col = keep("col", [P, 4, TT])
        mmask = keep("mmask", [P, P])
        FREE = cursor[0]

        x_tok = at("x_tok", FREE, [P, TT, D])
        junk = at("junk", FREE + 32 * KB, [P, D])

        nq = at("nq", FREE, [P, NH // 2, SEQ])
        w1 = at("w1", FREE, [P, 2, CMP_LEN, CMP_HID])
        k_a = [at(f"k_a{br}", FREE + (16 + 16 * br) * KB, [P, G, SEQ], FP32R) for br in range(2)]
        k_b = [at(f"k_b{br}", FREE + (24 + 16 * br) * KB, [P, G, SEQ], FP32R) for br in range(2)]
        v_tok = at("v_tok", FREE + 48 * KB, [P, 2, TT, P])
        o_nsa = at("o_nsa", FREE + 56 * KB, [P, TT, NH * DH])
        g_rows = at("g_rows", FREE + 56 * KB, [NH * 3, SEQ])
        g_i = at("g_i", FREE + 60 * KB, [MH, SEQ])
        g_f = at("g_f", FREE + 64 * KB, [MH, SEQ])
        g_t = at("g_t", FREE + 68 * KB, [MH, SEQ])
        m_rows = at("m_rows", FREE + 72 * KB, [MH, SEQ])
        o = FREE + 76 * KB
        kc_a = at("kc_a", o, [P, G, DH], FP32R)
        kc_b = at("kc_b", o + 512, [P, G, DH], FP32R)
        vc = at("vc", o + 1024, [DH, G, DH])
        ident_r = at("ident_r", o + 1536, [P, P], FP32R)
        mask_diag = at("mask_diag", o + 2048, [P, P], FP32R)
        mask_edge = at("mask_edge", o + 2560, [P, P], FP32R)
        mask_cmp = at("mask_cmp", o + 3072, [P, TT, DH], FP32R)
        keep_cmp = at("keep_cmp", o + 5120, [P, 1])
        gate_h = at("gate_h", o + 5376, [P, 2, TT, 3])
        r = o + 5632
        kvp = at("kvp", r, [P, 2, 2, SEQ])
        mask_src = at("mask_src", r + 24 * KB, [P, TT, DH])
        mask_sq = at("mask_sq", r + 26 * KB, [P, 2, P])
        v_feat = at("v_feat", r + 16 * KB, [P, 2, SEQ])
        w2 = at("w2", r + 28 * KB + 256, [CMP_HID, 2, DH])
        hid = at("hid", r + 29 * KB, [CMP_HID, 2, G, NCMP])
        q_st = [at(f"q_st{u}", r + 4 * KB * u, [P, SEQ], FP32R) for u in range(2)]
        probs = [at(f"probs{b}", r + (8 + 4 * b) * KB, [P, SEQ]) for b in range(3)]
        probs_t = [at(f"probs_t{b}", r + (20 + 4 * b) * KB, [P, TT, P]) for b in range(2)]
        o_stage = at("o_stage", r + 28 * KB, [P, 2, TT, DH])

        o_gate = at("o_gate", FREE, [P, MH, SEQ])
        u_raw = at("u_raw", FREE + 16 * KB, [P, 4 + SEQ])
        c = FREE + 20 * KB + 32
        u_conv = at("u_conv", c, [P, SEQ])
        mq_hi = at("mq_hi", c + 4 * KB, [P, SEQ], FP32R)
        mq_lo = at("mq_lo", c + 8 * KB, [P, SEQ], FP32R)
        mk_hi = at("mk_hi", c + 12 * KB, [P, SEQ], FP32R)
        mk_lo = at("mk_lo", c + 16 * KB, [P, SEQ], FP32R)
        mv_feat = at("mv_feat", c + 20 * KB, [P, SEQ])
        m_bc = at("m_bc", c + 24 * KB, [P, SEQ])
        decay = [at(f"decay{b}", c + (28 + 2 * b) * KB, [P, HALF]) for b in range(2)]
        m_pick = at("m_pick", c + 32 * KB, [MH, P])
        head_a = at("head_a", c + 32 * KB + 512, [P, 2, TT])
        head_d = at("head_d", c + 32 * KB + 576, [P, 4, TT])
        head_w = at("head_w", c + 32 * KB + 704, [P, 2, TAPS])
        h_mls = at("h_mls", FREE + 76 * KB, [P, TT, MH * MDH])
        mv_tok = at("mv_tok", FREE + 92 * KB, [P, TT, MDH + 4])
        tri = at("tri", FREE + 96 * KB + 128, [P, TT * (TT + 1) // 2, P])

        acc = at("acc", FREE, [P, SEQ])
        r_bc = at("r_bc", FREE + 4 * KB, [P, SEQ])
        x_t = at("x_t", FREE + 16 * KB, [P, KT, SEQ])
        x_half = [at(f"x_half{b}", FREE + (96 - 20 * b) * KB, [P, TT // 2, D]) for b in range(2)]
        hm_hi = at("hm_hi", FREE + 48 * KB, [P, KT, MEM], FP32R)
        hm_lo = at("hm_lo", FREE + 56 * KB, [P, KT, MEM], FP32R)
        mem_tok = at("mem_tok", FREE + 64 * KB, [P, MEMT, D])
        xo = at("xo", FREE + 48 * KB, [P, KT, SEQ])
        xk = at("xk", FREE + 80 * KB, [P, KT, MEM])
        xv = at("xv", FREE + 88 * KB, [P, MEMT, D])
        xv_feat = at("xv_feat", FREE + 96 * KB, [P, KT, MEM])
        xq = at("xq", FREE + 96 * KB, [P, 2, SEQ])
        xp_t = at("xp_t", FREE + 104 * KB, [P, MEMT, SEQ])
        xv_h = at("xv_h", FREE + 112 * KB, [P, MEMT, XDH])
        xp = [at(f"xp{b}", FREE + (8 + b) * KB, [P, MEM]) for b in range(4)]
        f = FREE + 48 * KB
        gated = [at(f"gated{b}", FREE + (48 + 2 * b) * KB, [P, HALF]) for b in range(4)]
        sq = [at(f"sq{b}", FREE + (8 + 4 * b) * KB, [P, SEQ]) for b in range(2)]
        fu = [at(f"fu{s}", f + (4 * KB + 32) * s, [P, 8 + SEQ]) for s in range(2)]
        f += 2 * (4 * KB + 32)
        fc = [at(f"fc{s}", f + 4 * KB * s, [P, SEQ]) for s in range(2)]
        fg = at("fg", f + 8 * KB, [P, SEQ])
        z_hi = [at(f"z_hi{b}", f + (12 + 4 * b) * KB, [P, SEQ], FP32R) for b in range(2)]
        z_lo = [at(f"z_lo{b}", f + (20 + 4 * b) * KB, [P, SEQ], FP32R) for b in range(2)]
        gain_bc = at("gain_bc", FREE, [P, D])
        y_tok = [at(f"y_tok{b}", FREE + (88 + 4 * b) * KB, [P, D]) for b in range(4)]

        ps = ctx.enter_context(nc.psum_tensor("ps", [P, 8, HALF], FP32))
        ps_flat = ps[:, :, :].rearrange("p b n -> p (b n)")

        names = {}

        for name in ("chunk_done chunk_freed tile_started weights_split w_loaded0 w_loaded1 w_hi_made gate_cols pool_chain "
                     "masks_ready vector_chain hi_ready std_ready x_scaled junk_written params_loaded w1_loaded "
                     "hid_ready khi_ready gates_ready f_abs_ready ln_step floor_ready log_rows_ready scores_ready "
                     "q_hi_ready q_ready probs_ready shift_ready pt_made0 pt_made1 pt_copied0 pt_copied1 o_ready o_taken "
                     "o_stage_taken conv_ready silu_done qk_ready pick_ready diag_ready decay_ready hm_ready hm_taken "
                     "xh_loaded gate_done ssq_ready mixed_ready split_ready mem_loaded mem_scaled sq_ready sq_used "
                     "r_col_ready sums_ready col_ready spread_ready kv_hi_made tap_ready h_ready x_shift_ready "
                     "x_exp_ready xv_ready conv_done gelu_ready "
                     "z_made z_ready y_t_ready y_ready stored0 stored1 stored2 stored3").split():
            names[name] = ctx.enter_context(nc.semaphore(name))
        for i in range(TT):
            names[f"x_loaded{i}"] = ctx.enter_context(nc.semaphore(f"x_loaded{i}"))

        class View:

            def __init__(self):
                self.t = {}

            def __call__(self, name, step=1):
                if name not in self.t:
                    self.t[name] = Tally(names[name], step)
                return self.t[name]

        whole = lambda m: m[tuple([slice(None)] * len(m.shape))]
        block = ctx.enter_context(nc.Block())
        rows = lambda g, s=1: slice(DH * g, DH * g + DH)
        tri_at = lambda j, i: sum(TT - a for a in range(j)) + i - j
        pieces = [(j, a, min(a + HALF, SEQ)) for j in range(TT) for a in range(P * j, SEQ, HALF)]

        @block.sync
        def _(sp):
            t = View()
            weights_split, y_ready = t("weights_split"), t("y_ready")
            gate_cols, w_loaded0, w_loaded1 = t("gate_cols", 16), t("w_loaded0", 16), t("w_loaded1", 16)
            params_loaded = t("params_loaded", 16)
            loaded, weights_split = [w_loaded0, w_loaded1], weights_split

            def load(weights, k_tiles=True):
                s = weights_split.n % 2
                weights_split.add(1)
                if weights_split.past(2):
                    sp.wait_ge(weights_split.sem, weights_split.value(2))
                if k_tiles:
                    sp.dma_start(w_raw[s][:, :].rearrange("p (k m) -> p k m", k=KT),
                                               weights.rearrange("(k p) m -> p k m", p=P)).then_inc(
                                                   loaded[s].sem, loaded[s].up())
                else:
                    sp.dma_start(w_raw[s][:, :], weights).then_inc(loaded[s].sem, loaded[s].up())

            def w_loop(turns, tiles):
                return engine_loop(sp, turns, [(weights_split, tiles), (loaded[0], tiles // 2), (loaded[1], tiles // 2)])

            x_v = x[0, :, :].rearrange("(t p) d -> p t d", p=P)
            for i in range(TT):
                sp.dma_start(x_tok[:, i, :], x_v[:, i, :]).then_inc(
                    t(f"x_loaded{i}", 16).sem, t(f"x_loaded{i}", 16).up())

            def load_param(dst, src):
                sp.dma_start(dst, src).then_inc(params_loaded.sem, params_loaded.up())

            as_rows = lambda g: g.rearrange("(k p) -> k p", p=P)
            n = 0
            for g in (g_mix[0, :], g_head_nsa[0, :], g_head_mlstm[0, :], g_mem_q[0, :], g_mem_kv[0, :], g_ffn[0, :],
                      g_final):
                k = g.shape[0] // P
                load_param(par_rows[n:n + k, 0, :], as_rows(g))
                n += k
            load_param(par_rows[n:n + N_CM, 0, :], mlstm_conv_w[0, :, :].rearrange("t (k p) -> (t k) p", p=P))
            for kv, pw in enumerate((cmp_pos_k, cmp_pos_v)):
                for g in range(G):
                    load_param(par_rows[kv * CMP_LEN:kv * CMP_LEN + CMP_LEN, 1, DH * g:DH * g + DH], pw[0, :, :])
            load_param(par_rows[0:4 * FT, 2, :], ffn_conv_w[0, 0:2, :].rearrange("t (k p) -> (t k) p", p=P))
            load_param(par_rows[0:2 * FT, 3, :], ffn_conv_w[0, 2, :].rearrange("(k p) -> k p", p=P))
            load_param(w2[:, 0, :], cmp_w2_k[0, :, :])
            load_param(w2[:, 1, :], cmp_w2_v[0, :, :])
            load_param(bias_if[:, 0:1], mlstm_b_i[0, :].rearrange("(h a) -> h a", a=1))
            load_param(bias_if[:, 1:2], mlstm_b_f[0, :].rearrange("(h a) -> h a", a=1))

            win = w_in[0, :, :]
            for c in (C_KC, C_VC, C_KS, C_VS, C_KW, C_VW):
                load(win[:, c:c + P])
            s = weights_split.n % 2
            weights_split.add(1)
            sp.wait_ge(weights_split.sem, weights_split.value(2))
            slot = w_raw[s][:, :].rearrange("p (k m) -> p k m", k=KT)
            for a, b, src in ((R_I, R_I + MH, C_MI), (R_I + MH, R_F, C_GT + 32), (R_F, R_F + MH, C_MF),
                              (R_F + MH, P, C_GT + 64)):
                sp.dma_start(slot[:, :, a:b], win[:, src:src + b - a].rearrange("(k p) m -> p k m", p=P)).then_inc(
                    gate_cols.sem, gate_cols.up())
            sp.wait_ge(gate_cols.sem, gate_cols.value())
            sp.dma_start(slot[:, :, 0:R_I], win[:, C_GT:C_GT + R_I].rearrange("(k p) m -> p k m", p=P)).then_inc(
                loaded[s].sem, loaded[s].up())
            for i in range(4):
                load(win[:, C_Q + P * i:C_Q + P * i + P])
            with w_loop(MH, 4) as i:
                for c in (C_MQ, C_MK, C_MV, C_MO):
                    load(win[:, bass.ds(i * P + c, P)])

            def load_all(weights):
                with w_loop(KT // 2, 2) as i:
                    for u in range(2):
                        load(weights[:, bass.ds(i * (2 * P) + u * P, P)])

            load_all(w_out[0, :, :])
            for w in (w_mem_k, w_mem_v, w_mem_q, w_mem_o):
                load_all(w[0, :, :])
            up, down = w_up[0, :, :], w_down[0, :, :]
            load(up[:, 0:P])
            load(up[:, FF:FF + P])
            with w_loop((FT - 2) // 2, 6) as i:
                for u in range(2):
                    load(up[:, bass.ds(i * (2 * P) + (1 + u) * P, P)])
                    load(up[:, bass.ds(i * (2 * P) + FF + (1 + u) * P, P)])
                    load(down[bass.ds(i * (2 * P) + u * P, P), :], k_tiles=False)
            load(up[:, FF - P:FF])
            load(up[:, 2 * FF - P:2 * FF])
            for p in (FT - 2, FT - 1):
                load(down[p * P:p * P + P, :], k_tiles=False)
            stored = [t(f"stored{b}", 16) for b in range(4)]
            for n in range(TT):
                sp.wait_ge(y_ready.sem, y_ready.next())
                sp.dma_start(out[0, P * n:P * n + P, :], y_tok[n % 4][:, :]).then_inc(
                    stored[n % 4].sem, stored[n % 4].up())
            for s in stored:
                sp.wait_ge(s.sem, s.value())

        @block.gpsimd
        def _(pool):
            t = View()
            masks_ready, pool_chain, tile_started = t("masks_ready"), t("pool_chain"), t("tile_started")
            w_hi_made, weights_split, kv_hi_made = t("w_hi_made"), t("weights_split"), t("kv_hi_made")
            w_loaded0, w_loaded1 = t("w_loaded0", 16), t("w_loaded1", 16)
            for m, v in ((ident, 0.0), (ones, 1.0), (mask_sq, 0.0), (mask_src, 0.0), (mmask, 0.0),
                         (keep_cmp, 1.0)):
                pool.memset(whole(m), v).then_inc(pool_chain.sem, pool_chain.up())
            pool.wait_ge(pool_chain.sem, pool_chain.value())
            sel = pool.affine_select
            sel(out=ident[:, :], in_=ident[:, :], compare_op=ALU.not_equal, fill=1.0, base=0,
                          pattern=[[-1, P]], channel_multiplier=1).then_inc(pool_chain.sem, pool_chain.up())
            sel(out=mask_sq[:, 0, :], in_=mask_sq[:, 0, :], compare_op=ALU.is_ge, fill=NEG, base=0,
                          pattern=[[-1, P]], channel_multiplier=1).then_inc(pool_chain.sem, pool_chain.up())
            sel(out=mask_sq[:, 1, :], in_=mask_sq[:, 1, :], compare_op=ALU.is_gt, fill=NEG, base=0,
                          pattern=[[1, P]], channel_multiplier=-1).then_inc(pool_chain.sem, pool_chain.up())
            sel(out=mask_src[:, :, :], in_=mask_src[:, :, :], compare_op=ALU.is_ge, fill=NEG,
                          base=-(CMP_LEN - 1), pattern=[[P, TT], [-CMP_STRIDE, DH]], channel_multiplier=1).then_inc(
                              pool_chain.sem, pool_chain.up())
            sel(out=keep_cmp[:, :], in_=keep_cmp[:, :], compare_op=ALU.is_ge, fill=0.0,
                          base=-(CMP_LEN - 1), pattern=[[0, 1]], channel_multiplier=1).then_inc(
                              pool_chain.sem, pool_chain.up())
            sel(out=mmask[:, :], in_=mmask[:, :], compare_op=ALU.is_ge, fill=NEG, base=0,
                          pattern=[[1, P]], channel_multiplier=-1).then_inc(pool_chain.sem, pool_chain.up())
            pool.wait_ge(pool_chain.sem, pool_chain.value())
            pool.tensor_copy(mask_diag[:, :], mask_sq[:, 0, :]).then_inc(masks_ready.sem, masks_ready.up())
            pool.tensor_copy(mask_edge[:, :], mask_sq[:, 1, :]).then_inc(masks_ready.sem, masks_ready.up())
            pool.tensor_copy(mask_cmp[:, :, :], mask_src[:, :, :]).then_inc(masks_ready.sem, masks_ready.up())
            pool.tensor_copy(ident_r[:, :], ident[:, :]).then_inc(masks_ready.sem, masks_ready.up())

            loaded, weights_split, tile_started = [w_loaded0, w_loaded1], weights_split, tile_started
            hi_made = w_hi_made

            def split_tile(s, with_high=True):
                pool.wait_ge(loaded[s].sem, loaded[s].next())
                if with_high:
                    if tile_started.past(0):
                        pool.wait_ge(tile_started.sem, tile_started.value())
                    pool.tensor_tensor(w_hi[s][:, :], w_raw[s][:, :], ones[:, :].to_broadcast([P, KT * P]), ALU.mult).then_inc(
                        w_hi_made.sem, w_hi_made.up())
                    pool.wait_ge(w_hi_made.sem, w_hi_made.value())
                else:
                    pool.wait_ge(kv_hi_made.sem, kv_hi_made.next())
                pool.tensor_tensor(w_lo[s][:, :], w_raw[s][:, :], w_hi[s][:, :].bitcast(FP32), ALU.subtract).then_inc(
                    weights_split.sem, weights_split.up())
                tile_started.add(1)

            def split_pairs(turns, with_high=True):
                per = [(loaded[0], 1), (loaded[1], 1), (weights_split, 2), (tile_started, 2),
                       (w_hi_made, 2) if with_high else (kv_hi_made, 2)]
                with engine_loop(pool, turns, per):
                    split_tile(1, with_high)
                    split_tile(0, with_high)

            assert FIRST_KV % 2 and TILES % 2
            split_tile(0)
            split_pairs(FIRST_KV // 2)
            split_pairs(KT, with_high=False)
            split_pairs((TILES - FIRST_KV - 2 * KT) // 2)

        @block.tensor
        def _(pe):
            t = View()
            chunk_done, chunk_freed, h_ready = t("chunk_done"), t("chunk_freed"), t("h_ready")
            hid_ready, log_rows_ready, masks_ready = t("hid_ready"), t("log_rows_ready"), t("masks_ready")
            mem_scaled, mixed_ready, o_ready = t("mem_scaled"), t("mixed_ready"), t("o_ready")
            o_taken, pick_ready, probs_ready = t("o_taken"), t("pick_ready"), t("probs_ready")
            pt_copied0, pt_copied1, pt_made0 = t("pt_copied0"), t("pt_copied1"), t("pt_made0")
            pt_made1, q_ready, qk_ready = t("pt_made1"), t("q_ready"), t("qk_ready")
            r_col_ready, scores_ready, split_ready = t("r_col_ready"), t("scores_ready"), t("split_ready")
            sums_ready, spread_ready = t("sums_ready"), t("spread_ready")
            sq_used, tile_started, weights_split = t("sq_used"), t("tile_started"), t("weights_split")
            x_scaled, xv_ready, y_ready = t("x_scaled"), t("xv_ready"), t("y_ready")
            y_t_ready, z_ready = t("y_t_ready"), t("z_ready")
            params_loaded, w1_loaded, xh_loaded = t("params_loaded", 16), t("w1_loaded", 16), t("xh_loaded", 16)
            mm, transpose = nc.tensor.matmul, nc.tensor.transpose
            ring = Ring(chunk_done)

            def open_chunk():
                if chunk_done.n >= 4:
                    pe.wait_ge(chunk_freed.sem, chunk_done.value(ring.size - 1))
                return ring.bank()

            def freed_now():
                pe.wait_ge(chunk_freed.sem, chunk_done.value())

            def product(out_ap, slot_k, x_hi, x_lo, first, last, tag=None):
                whi, wlo = slot_k
                ins = mm(out_ap, whi, x_hi, start=first, stop=False)
                if tag:
                    ins.then_inc(tile_started.sem, tile_started.up())
                mm(out_ap, whi, x_lo, start=False, stop=False)
                return mm(out_ap, wlo, x_hi, start=False, stop=last)

            def next_weights():
                pe.wait_ge(weights_split.sem, weights_split.next())
                return (weights_split.n - 1) % 2

            def each_piece(c, k):
                pe.wait_ge(h_ready.sem, h_ready.next())

            def gemm_tile(x_hi, x_lo, width=SEQ, wait_piece=None):
                s = next_weights()
                for c in range(0, width, HALF):
                    n = min(HALF, width - c)
                    b = open_chunk()
                    for k in range(KT):
                        if wait_piece:
                            wait_piece(c // HALF, k)
                        w = (w_hi[s][:, k * P:k * P + P], w_lo[s][:, k * P:k * P + P])
                        last = product(ps[:, b, 0:n], w, x_hi[:, k, c:c + n], x_lo[:, k, c:c + n],
                                       k == 0, k == KT - 1, tag=(c == 0 and k == 0))
                    last.then_inc(chunk_done.sem, chunk_done.up())

            def gemm_loop(turns, tiles, x_hi, x_lo, width=SEQ):
                per = tiles * ((width + HALF - 1) // HALF)
                assert per % 4 == 0
                with engine_loop(pe, turns, [(weights_split, tiles), (tile_started, tiles), (chunk_done, per)]):
                    for _ in range(tiles):
                        gemm_tile(x_hi, x_lo, width)

            def transposes(parts):
                b = open_chunk()
                for src, n, at_col in parts:
                    m = src.shape[-1]
                    last = transpose(ps[0:m, b, at_col:at_col + n], src, ident[0:n, 0:n])
                last.then_inc(chunk_done.sem, chunk_done.up())

            masks_ready.add(4)
            pe.wait_ge(masks_ready.sem, masks_ready.value())
            params_loaded.add(PARAM_LOADS)
            pe.wait_ge(params_loaded.sem, params_loaded.value())
            for n in range(0, 4, 2):
                b = open_chunk()
                for m in (n, n + 1):
                    r_, c_ = PAR_TILES[m]
                    c_ -= PAR_TILES[n][1]
                    last = transpose(ps[:, b, c_:c_ + r_], par_rows[0:r_, m, :], ident[0:r_, 0:r_])
                last.then_inc(chunk_done.sem, chunk_done.up())
            for half in range(2):
                x_scaled.add(4)
                pe.wait_ge(x_scaled.sem, x_scaled.value())
                for k in range(KT):
                    transposes([(x_tok[:, 4 * half + j, k * P:k * P + P], P, j * P) for j in range(4)])
            freed_now()

            gemm_tile(h_hi, h_lo)
            gemm_tile(h_hi, h_lo)
            freed_now()
            w1_loaded.add(4)
            pe.wait_ge(w1_loaded.sem, w1_loaded.value())
            for kv in range(2):
                banks = []
                for g in range(G):
                    banks.append(open_chunk())
                    chunk_done.n += 1
                chunk_done.n -= G
                for l in range(CMP_LEN):
                    lo_t = l % CMP_STRIDE + (CMP_STRIDE if l >= CMP_STRIDE else 0)
                    for g in range(G):
                        src = kvp[rows(g), kv, l // CMP_STRIDE, :]
                        last = mm(ps[0:CMP_HID, banks[g], 0:NCMP], w1[rows(g), kv, l, :],
                                  src[:, lo_t:lo_t + CMP_STRIDE * (NCMP - 1) + 1:CMP_STRIDE],
                                  start=(l == 0), stop=(l == CMP_LEN - 1))
                        if l == CMP_LEN - 1:
                            last.then_inc(chunk_done.sem, chunk_done.up())
            pe.wait_ge(hid_ready.sem, hid_ready.next())
            b = open_chunk()
            for g in range(G):
                last = mm(ps[0:DH, b, DH * g:DH * g + NCMP], w2[:, 0, :], hid[:, 0, g, :], start=True, stop=True)
            last.then_inc(chunk_done.sem, chunk_done.up())
            b = open_chunk()
            for g in range(G):
                last = mm(ps[0:NCMP, b, DH * g:DH * g + DH], hid[:, 1, g, :], w2[:, 1, :], start=True, stop=True)
            last.then_inc(chunk_done.sem, chunk_done.up())
            for _ in range(5 + NH // 2):
                gemm_tile(h_hi, h_lo)
            for br in range(2):
                for q in range(2):
                    transposes([(v_feat[:, br, (4 * q + j) * P:(4 * q + j + 1) * P], P, j * P) for j in range(4)])
            transposes([(g_rows[:, j * P:j * P + P], NH * 3, j * 32) for j in range(TT)])
            pe.wait_ge(log_rows_ready.sem, log_rows_ready.next())
            b = open_chunk()
            for src, at_col in ((g_i, 0), (g_f, 64)):
                for j in range(TT):
                    last = transpose(ps[:, b, at_col + MH * j:at_col + MH * j + MH], src[:, j * P:j * P + P],
                                     ident[0:MH, 0:MH])
            last.then_inc(chunk_done.sem, chunk_done.up())
            freed_now()

            with engine_loop(pe, G, [(scores_ready, 2 * JOBS), (q_ready, 4), (probs_ready, 2 * JOBS), (pt_made0, 2 * JOBS),
                                     (pt_made1, 2 * JOBS_1), (pt_copied0, 2 * JOBS), (pt_copied1, 2 * JOBS_1), (o_ready, 2 * JOBS),
                                     (o_taken, 2 * JOBS)]) as g:
                with engine_loop(pe, 2, [(scores_ready, JOBS), (q_ready, 2), (probs_ready, JOBS), (pt_made0, JOBS), (pt_made1, JOBS_1),
                                         (pt_copied0, JOBS), (pt_copied1, JOBS_1), (o_ready, JOBS), (o_taken, JOBS)]):
                    ga = pe.snap(g * SEQ)
                    gc = pe.snap(g * DH)
                    gv = gc

                    def moving(tensor, base, off, n):
                        return tensor[:, :, :].rearrange("p g s -> p (g s)")[:, bass.ds(base + off, n)]

                    def scores(j):
                        u, i, br = job_of(j)
                        if j % (2 * TT) == 0:
                            pe.wait_ge(q_ready.sem, q_ready.next())
                        if j >= 2:
                            pe.wait_ge(probs_ready.sem, scores_ready.value(1))
                        first = 0 if br == 0 else max(0, i - WT)
                        n = (i - first + 1) * P
                        q = q_st[u][:, i * P:i * P + P]
                        bank = 2 * (j % 2)
                        for c in range(0, n, HALF):
                            m = min(HALF, n - c)
                            o = ps[:, bank + c // HALF, 0:m]
                            at_key = first * P + c
                            masks = []
                            if c <= n - P < c + HALF:
                                masks.append((n - P - c, mask_diag))
                            if br == 1 and i >= WT and c == 0:
                                masks.append((0, mask_edge))
                            mm(o, q, moving(k_a[br], ga, at_key, m), start=True, stop=False)
                            last = mm(o, q, moving(k_b[br], ga, at_key, m), start=False, stop=not masks)
                            for z, (a, mask) in enumerate(masks):
                                last = mm(ps[:, bank + c // HALF, a:a + P], ident_r[:, :], mask[:, :],
                                          start=False, stop=z == len(masks) - 1)
                        if br == 1:
                            o = ps[:, bank + 1, P:P + DH]
                            kc_ = lambda z: z[:, :, :].rearrange("p g s -> p (g s)")[:, bass.ds(gc, DH)]
                            mm(o, q, kc_(kc_a), start=True, stop=False)
                            mm(o, q, kc_(kc_b), start=False, stop=False)
                            last = mm(o, ident_r[:, :], mask_cmp[:, i, :], start=False, stop=True)
                        last.then_inc(scores_ready.sem, scores_ready.up())

                    def turn(j):
                        u, i, br = job_of(j)
                        n = i + 1 if br == 0 else min(i, WT) + 1
                        pe.wait_ge(probs_ready.sem, probs_ready.next())
                        pr = probs[j % 3]
                        if j:
                            pe.wait_ge(pt_copied0.sem, pt_made0.value())
                        if has_second(j) and any(has_second(a) for a in range(j)):
                            pe.wait_ge(pt_copied1.sem, pt_made1.value())
                        for a in range(min(n, 4)):
                            last = transpose(ps[:, 4, a * P:a * P + P], pr[:, a * P:a * P + P], ident[:, :])
                        last.then_inc(pt_made0.sem, pt_made0.up())
                        if has_second(j):
                            for a in range(4, n):
                                last = transpose(ps[:, 5, (a - 4) * P:(a - 3) * P], pr[:, a * P:a * P + P], ident[:, :])
                            if br == 1:
                                last = transpose(ps[0:DH, 5, 3 * P:4 * P], pr[:, 5 * P:5 * P + DH], ident[:, :])
                            last.then_inc(pt_made1.sem, pt_made1.up())

                    def values(j):
                        u, i, br = job_of(j)
                        first = 0 if br == 0 else max(0, i - WT)
                        n = i + 1 - first
                        pe.wait_ge(pt_copied0.sem, pt_copied0.next())
                        if has_second(j):
                            pe.wait_ge(pt_copied1.sem, pt_copied1.next())
                        if j >= 2:
                            pe.wait_ge(o_taken.sem, o_ready.value(1))
                        v_flat = v_tok[:, br, :, :].rearrange("p t d -> p (t d)")
                        for a in range(n):
                            last = mm(ps[:, 6 + j % 2, 0:DH], probs_t[j % 2][:, a, :],
                                      v_flat[:, bass.ds(gv + (first + a) * P, DH)], start=a == 0, stop=a == n - 1)
                        if br == 1:
                            last = mm(ps[:, 6 + j % 2, DH:2 * DH], probs_t[j % 2][0:DH, TT - 1, :],
                                      vc[:, :, :].rearrange("n g d -> n (g d)")[:, bass.ds(gc, DH)],
                                      start=True, stop=True)
                        last.then_inc(o_ready.sem, o_ready.up())

                    for st in range(JOBS + 3):
                        if st < JOBS:
                            scores(st)
                        if 0 <= st - 2 < JOBS:
                            turn(st - 2)
                        if 0 <= st - 3 < JOBS:
                            values(st - 3)
                    o_taken.add(JOBS)
            pe.wait_ge(o_taken.sem, o_taken.value())

            ring.resize(8)
            with engine_loop(pe, MH, [(weights_split, 4), (tile_started, 4), (chunk_done, 32), (pick_ready, 1), (qk_ready, 1)]):
                for _ in range(3):
                    gemm_tile(h_hi, h_lo)
                pe.wait_ge(pick_ready.sem, pick_ready.next())
                for c in range(2):
                    b = open_chunk()
                    mm(ps[:, b, :], m_pick[:, :], m_rows[:, c * HALF:c * HALF + HALF], start=True, stop=True).then_inc(
                        chunk_done.sem, chunk_done.up())
                gemm_tile(h_hi, h_lo)
                pe.wait_ge(chunk_freed.sem, chunk_done.value(4))
                for q in range(2):
                    transposes([(mv_feat[:, (4 * q + j) * P:(4 * q + j + 1) * P], P, j * P) for j in range(4)])
                pe.wait_ge(qk_ready.sem, qk_ready.next())
                for j, a, e in pieces:
                    b = open_chunk()
                    product(ps[:, b, 0:e - a], (mk_hi[:, j * P:j * P + P], mk_lo[:, j * P:j * P + P]),
                                     mq_hi[:, a:e], mq_lo[:, a:e], True, True).then_inc(
                                         chunk_done.sem, chunk_done.up())
                for i in range(TT):
                    later = len(pieces) - 1 - pieces.index((i, P * i, min(P * i + HALF, SEQ)))
                    pe.wait_ge(chunk_freed.sem, chunk_done.value(later + i))
                    b = open_chunk()
                    for j in range(i + 1):
                        last = mm(ps[:, b, 0:MDH + 1], tri[:, tri_at(j, i), :], mv_tok[:, j, 0:MDH + 1],
                                  start=j == 0, stop=j == i)
                    last.then_inc(chunk_done.sem, chunk_done.up())

            freed_now()
            ring.resize(4)
            for f in range(KT):
                if f == 4:
                    pe.wait_ge(mixed_ready.sem, mixed_ready.next())
                src = o_nsa if f < 4 else h_mls
                for q in range(2):
                    transposes([(src[:, 4 * q + j, (f % 4) * P:(f % 4) * P + P], P, j * P) for j in range(4)])

            def mixed_piece(c, k):
                if k == 0 and c == 0:
                    pe.wait_ge(chunk_freed.sem, chunk_done.value(8))
                if k >= 4:
                    pe.wait_ge(split_ready.sem, 2 * (k - 4) + c + 1)

            gemm_tile(h_hi, h_lo, wait_piece=mixed_piece)
            xh_loaded.add(2)
            pe.wait_ge(xh_loaded.sem, xh_loaded.value())
            for k in range(KT):
                for half in range(2):
                    transposes([(x_half[half][:, j, k * P:k * P + P], P, j * P) for j in range(4)])
            gemm_tile(h_hi, h_lo)
            gemm_loop(KT // 2 - 1, 2, h_hi, h_lo)

            def token_sums():
                sq_used.add(2 + KT)
                pe.wait_ge(sq_used.sem, sq_used.value())
                for j in range(TT):
                    last = mm(ps[:, 4, j:j + 1], acc[:, j * P:j * P + P], ones[:, :], start=True, stop=True)
                last.then_inc(sums_ready.sem, sums_ready.up())

            def spread(bank, column):
                for j in range(TT):
                    last = mm(ps[:, bank + j // 4, (j % 4) * P:(j % 4 + 1) * P], column(j).to_broadcast([P, P]),
                              ident[:, :], start=True, stop=True)
                last.then_inc(spread_ready.sem, spread_ready.up())

            def spread_roots():
                pe.wait_ge(r_col_ready.sem, r_col_ready.next())
                spread(6, lambda j: col[:, 0, j:j + 1])

            pe.wait_ge(mem_scaled.sem, mem_scaled.next())
            for k in range(KT):
                transposes([(mem_tok[:, j, k * P:k * P + P], P, j * P) for j in range(MEMT)])
            freed_now()
            token_sums()
            gemm_loop(KT // 4, 4, hm_hi, hm_lo, MEM)
            spread_roots()
            gemm_loop(KT // 4, 4, hm_hi, hm_lo, MEM)
            freed_now()
            for j in range(MEMT):
                for q in range(2):
                    transposes([(xv_feat[:, 4 * q + k, j * P:j * P + P], P, k * P) for k in range(4)])
            h_ready.add(2 * KT)
            pe.wait_ge(h_ready.sem, h_ready.value())
            freed_now()
            with engine_loop(pe, XH, [(weights_split, 2), (tile_started, 2), (chunk_done, 20), (xv_ready, 1)]) as hd:
                for _ in range(2):
                    gemm_tile(h_hi, h_lo)
                queries = chunk_done.n
                keys = pe.snap(hd * (2 * MEM))
                xk_flat = xk[:, :, :].rearrange("p k m -> p (k m)")
                made, made_t = {}, {}

                def x_scores(i):
                    if i == 0 or i == 4:
                        pe.wait_ge(chunk_freed.sem, chunk_done.value(chunk_done.n - queries + (1 if i == 0 else 0)))
                    b = open_chunk()
                    for z in range(2):
                        last = mm(ps[:, b, 0:MEM], xq[:, z, i * P:i * P + P], xk_flat[:, bass.ds(keys + z * MEM, MEM)],
                                  start=z == 0, stop=z == 1)
                    last.then_inc(chunk_done.sem, chunk_done.up())
                    made[i] = chunk_done.n

                def x_turn(i):
                    pe.wait_ge(chunk_freed.sem, chunk_done.value(chunk_done.n - made[i + 1]))
                    b = open_chunk()
                    for j in range(MEMT):
                        for d in range(2):
                            last = transpose(ps[:, b, (2 * j + d) * P:(2 * j + d + 1) * P],
                                             xp[(i + d) % 4][:, j * P:j * P + P], ident[:, :])
                    last.then_inc(chunk_done.sem, chunk_done.up())
                    made_t[i] = chunk_done.n

                def x_values(i):
                    z, c = i % 2, i // 2
                    pe.wait_ge(chunk_freed.sem, chunk_done.value(chunk_done.n - made_t[4 * c + 2]))
                    b = open_chunk()
                    for j in range(MEMT):
                        last = mm(ps[:, b, :], xv_h[:, j, z * P:z * P + P], xp_t[:, j, c * HALF:c * HALF + HALF],
                                  start=j == 0, stop=j == MEMT - 1)
                    last.then_inc(chunk_done.sem, chunk_done.up())

                for what, i in X_ORDER:
                    if what == "s":
                        x_scores(i)
                    elif what == "t":
                        x_turn(i)
                    else:
                        if i == 0:
                            pe.wait_ge(xv_ready.sem, xv_ready.next())
                        x_values(i)
            gemm_tile(h_hi, h_lo, wait_piece=each_piece)
            gemm_tile(h_hi, h_lo)
            gemm_loop(KT // 2 - 1, 2, h_hi, h_lo)

            token_sums()
            freed_now()
            ring.resize(8)

            def down(b):
                s = next_weights()
                pe.wait_ge(z_ready.sem, z_ready.next())
                for m in range(KT):
                    for c in range(2):
                        bank = open_chunk()
                        w = (w_hi[s][:, m * P:m * P + P], w_lo[s][:, m * P:m * P + P])
                        product(ps[:, bank, :], w, z_hi[b][:, c * HALF:c * HALF + HALF],
                                         z_lo[b][:, c * HALF:c * HALF + HALF], True, True, tag=(m == 0 and c == 0)).then_inc(
                                             chunk_done.sem, chunk_done.up())

            gemm_tile(h_hi, h_lo, wait_piece=each_piece)
            spread_roots()
            spread(4, lambda k: gains[:, G_FIN, k:k + 1])
            gemm_tile(h_hi, h_lo)
            pe.wait_ge(chunk_freed.sem, chunk_done.value(2))
            with engine_loop(pe, (FT - 2) // 2, [(weights_split, 6), (tile_started, 6), (chunk_done, 40), (z_ready, 2)]):
                for u in range(2):
                    gemm_tile(h_hi, h_lo)
                    gemm_tile(h_hi, h_lo)
                    down(u)
            gemm_tile(h_hi, h_lo)
            gemm_tile(h_hi, h_lo)
            down(0)
            down(1)

            freed_now()
            for i in range(TT):
                if i >= 4:
                    pe.wait_ge(y_ready.sem, y_ready.next())
                for k in range(KT):
                    last = transpose(ps[:, 2 * (i % 4) + k // 4, (k % 4) * P:(k % 4 + 1) * P],
                                     x_t[:, k, i * P:i * P + P], ident[:, :])
                last.then_inc(y_t_ready.sem, y_t_ready.up())

        @block.scalar
        def _(act):
            t = View()
            chunk_done, chunk_freed, conv_done = t("chunk_done"), t("chunk_freed"), t("conv_done")
            conv_ready, decay_ready, diag_ready = t("conv_ready"), t("decay_ready"), t("diag_ready")
            f_abs_ready, floor_ready, gate_done = t("f_abs_ready"), t("floor_ready"), t("gate_done")
            gates_ready, gelu_ready, hi_ready = t("gates_ready"), t("gelu_ready"), t("hi_ready")
            hid_ready, hm_ready, hm_taken = t("hid_ready"), t("hm_ready"), t("hm_taken")
            junk_written, khi_ready, ln_step = t("junk_written"), t("khi_ready"), t("ln_step")
            o_stage_taken, o_taken, probs_ready = t("o_stage_taken"), t("o_taken"), t("probs_ready")
            pt_copied0, pt_made0, pt_made1 = t("pt_copied0"), t("pt_made0"), t("pt_made1")
            q_hi_ready, scores_ready, shift_ready = t("q_hi_ready"), t("scores_ready"), t("shift_ready")
            silu_done, sq_ready, sq_used = t("silu_done"), t("sq_ready"), t("sq_used")
            ssq_ready, std_ready = t("ssq_ready"), t("std_ready")
            x_exp_ready, x_shift_ready = t("x_exp_ready"), t("x_shift_ready")
            z_made, z_ready, col_ready, tap_ready = t("z_made"), t("z_ready"), t("col_ready"), t("tap_ready")
            kv_hi_made, tile_started, y_t_ready = t("kv_hi_made"), t("tile_started"), t("y_t_ready")
            w_loaded0, w_loaded1 = t("w_loaded0", 16), t("w_loaded1", 16)
            mem_loaded, w1_loaded = t("mem_loaded", 16), t("w1_loaded", 16)
            xh_loaded = t("xh_loaded", 16)
            f = act.activation
            ring = Ring(chunk_done)

            def chunk():
                b = ring.bank()
                act.wait_ge(chunk_done.sem, chunk_done.next())
                return b

            def freed_now():
                act.wait_ge(chunk_freed.sem, chunk_done.value())

            for half in range(2):
                for i in range(4 * half, 4 * half + 4):
                    t(f"x_loaded{i}", 16).add(1)
                    act.wait_ge(t(f"x_loaded{i}", 16).sem, t(f"x_loaded{i}", 16).value())
                    f(junk[:, :], x_tok[:, i, :], ACT.Square, accum_out=ssq[:, i, 0:1]).then_inc(
                        junk_written.sem, junk_written.up())
                    act.wait_ge(junk_written.sem, junk_written.value())
                f(rstd[:, 4 * half:4 * half + 4, 0:1], ssq[:, 4 * half:4 * half + 4, 0:1], ACT.Sqrt,
                                     scale=1.0 / D, bias=EPS).then_inc(std_ready.sem, std_ready.up())
            chunk_done.add(2)
            freed_now()
            for half in range(2):
                for k in range(KT):
                    b = chunk()
                    f(h_hi[:, k, half * HALF:half * HALF + HALF], ps[:, b, :], ACT.Copy,
                                   scale=gains[:, G_MIX, k:k + 1]).then_inc(hi_ready.sem, hi_ready.up())
            act.wait_ge(chunk_done.sem, chunk_done.value())
            for kv, w1w in enumerate((cmp_w1_k, cmp_w1_v)):
                for g in range(G):
                    act.dma_start(w1[rows(g), kv, :, :],
                                                         w1w[0, :, :].rearrange("(l d) h -> d l h", d=DH)).then_inc(
                                                             w1_loaded.sem, w1_loaded.up())

            chunk_done.add(4)
            chunk_done.add(2 * G)
            freed_now()
            f(hid[:, :, :, :].rearrange("h a g n -> h (a g n)"),
                                 hid[:, :, :, :].rearrange("h a g n -> h (a g n)"), ACT.Gelu).then_inc(
                                     hid_ready.sem, hid_ready.up())
            chunk_done.add(2)
            for br in range(2):
                for c in range(2):
                    b = chunk()
                    cs = slice(c * HALF, c * HALF + HALF)
                    for g in range(G):
                        f(k_a[br][rows(g), g, cs], ps[rows(g), b, :], ACT.Copy).then_inc(
                            khi_ready.sem, khi_ready.up())
                        f(k_b[br][rows(1 - g), g, cs], ps[rows(g), b, :], ACT.Copy).then_inc(
                            khi_ready.sem, khi_ready.up())
                chunk_done.add(2)
            act.wait_ge(f_abs_ready.sem, f_abs_ready.next())
            f(g_t[:, :], g_t[:, :], ACT.Exp).then_inc(ln_step.sem, ln_step.up())
            act.wait_ge(ln_step.sem, ln_step.value())
            f(g_t[:, :], g_t[:, :], ACT.Ln, bias=1.0).then_inc(ln_step.sem, ln_step.up())
            act.wait_ge(ln_step.sem, ln_step.value())
            chunk_done.add(2 + NH)
            chunk_done.add(4)
            chunk_done.add(1)
            freed_now()
            f(gate_sig[:, :, :], gate_sig[:, :, :], ACT.Sigmoid).then_inc(gates_ready.sem, gates_ready.up())
            chunk_done.add(1)
            freed_now()
            f(den_floor[:, :, :], den_floor[:, :, :], ACT.Exp, scale=-1.0).then_inc(floor_ready.sem, floor_ready.up())

            loop = lambda eng, n, k: engine_loop(eng, n, [(q_hi_ready, 2 * k), (probs_ready, k * JOBS), (shift_ready, k * JOBS),
                                                          (pt_made0, k * JOBS), (pt_made1, k * JOBS_1), (pt_copied0, k * JOBS),
                                                          (o_taken, k * JOBS), (o_stage_taken, 2 * k)])
            f(q_st[0][rows(0), :], nq[rows(0), 0, :], ACT.Copy).then_inc(q_hi_ready.sem, q_hi_ready.up())
            with loop(act, G, 2) as g:
                with loop(act, 2, 1) as hp:
                    nq_flat = nq[:, :, :].rearrange("p a s -> p (a s)")
                    at_q = act.snap((g * 2 + hp) * SEQ)
                    at_next = act.snap((g * 2 + hp + 1) % (NH // 2) * SEQ)
                    for st in range(JOBS + 3):
                        if st in Q_SPLITS:
                            u, at_head = (1, at_q) if st == Q_SPLITS[0] else (0, at_next)
                            f(q_st[u][rows(u), :], nq_flat[rows(u), bass.ds(at_head, SEQ)], ACT.Copy).then_inc(
                                q_hi_ready.sem, q_hi_ready.up())
                        z = st - 2
                        if 0 <= z < JOBS:
                            u, i, br = job_of(z)
                            n = i + 1 if br == 0 else min(i, WT) + 1
                            act.wait_ge(pt_made0.sem, pt_made0.next())
                            f(probs_t[z % 2][:, 0:min(n, 4), :],
                              ps[:, 4, 0:min(n, 4) * P].rearrange("p (a k) -> p a k", k=P), ACT.Copy).then_inc(
                                  pt_copied0.sem, pt_copied0.up())
                            pt_made1.add(int(has_second(z)))
                        if st < JOBS:
                            u, i, br = job_of(st)
                            n = (i + 1 if br == 0 else min(i, WT) + 1) * P
                            if st >= 3:
                                if any(has_second(a) for a in range(st - 2)):
                                    act.wait_ge(pt_made1.sem, pt_made1.value(int(has_second(st - 2))))
                            act.wait_ge(shift_ready.sem, shift_ready.next())
                            flat = ps_flat[:, 2 * (st % 2) * HALF:2 * (st % 2) * HALF + 2 * HALF]
                            c0_ = 2 * (st % 4)
                            if br == 0:
                                f(probs[st % 3][:, 0:n], flat[:, 0:n], ACT.Exp,
                                              bias=shift[:, c0_:c0_ + 1], accum_out=sums[:, c0_:c0_ + 1]).then_inc(
                                                  probs_ready.sem, probs_ready.up())
                            else:
                                f(probs[st % 3][:, 0:n], flat[:, 0:n], ACT.Exp, bias=shift[:, c0_ + 1:c0_ + 2],
                                  accum_out=sums[:, c0_ + 1:c0_ + 2])
                                f(probs[st % 3][:, 5 * P:5 * P + DH], flat[:, 5 * P:5 * P + DH], ACT.Exp,
                                              bias=shift[:, c0_:c0_ + 1], accum_out=sums[:, c0_:c0_ + 1]).then_inc(
                                                  probs_ready.sem, probs_ready.up())
                    for u in range(2):
                        o_taken.add(JOBS // 2)
                        act.wait_ge(o_taken.sem, o_taken.value())
                        f(o_nsa[:, :, bass.ds(act.snap((g * 4 + hp * 2 + u) * DH), DH)],
                                       o_stage[:, u, :, :], ACT.Copy).then_inc(o_stage_taken.sem, o_stage_taken.up())

            act.wait_ge(ssq_ready.sem, ssq_ready.next())
            f(rstd[:, :, 0:NH], ssq[:, :, 0:NH], ACT.Sqrt, scale=1.0 / DH, bias=EPS).then_inc(
                std_ready.sem, std_ready.up())
            ring.resize(8)
            with engine_loop(act, MH, [(chunk_done, 32), (conv_ready, 2), (hi_ready, 2), (silu_done, 2),
                                       (diag_ready, 1), (decay_ready, 12), (hm_ready, 1),
                                       (hm_taken, 1), (gate_done, 1)]) as h:
                for hi, scale in ((mq_hi, MDH ** -0.5), (mk_hi, 1.0)):
                    act.wait_ge(conv_ready.sem, conv_ready.next())
                    f(u_conv[:, :], u_conv[:, :], ACT.Silu).then_inc(silu_done.sem, silu_done.up())
                    act.wait_ge(silu_done.sem, silu_done.value())
                    f(hi[:, :], u_conv[:, :], ACT.Copy, scale=scale).then_inc(hi_ready.sem, hi_ready.up())
                chunk_done.add(8 + 2 + 2)
                act.wait_ge(diag_ready.sem, diag_ready.next())
                f(u_conv[:, :], u_conv[:, :], ACT.Exp).then_inc(decay_ready.sem, decay_ready.up())
                for n, (j, a, e) in enumerate(pieces):
                    chunk_done.add(1)
                    a2 = a + P if a == P * j else a
                    if a2 < e:
                        if n >= 2:
                            act.wait_ge(chunk_freed.sem, chunk_done.value(2))
                        f(decay[n % 2][:, 0:e - a2], m_bc[:, a2:e], ACT.Exp, bias=head_a[:, 0, j:j + 1]).then_inc(
                            decay_ready.sem, decay_ready.up())
                f(o_gate[:, bass.ds(h, 1), :], o_gate[:, bass.ds(h, 1), :], ACT.Sigmoid).then_inc(
                    gate_done.sem, gate_done.up())
                chunk_done.add(8)
                act.wait_ge(hm_ready.sem, hm_ready.next())
                f(h_mls[:, :, bass.ds(act.snap(h * MDH), MDH)],
                                    u_conv[:, :].rearrange("p (t d) -> p t d", d=MDH), ACT.Copy).then_inc(
                                        hm_taken.sem, hm_taken.up())

            ring.resize(4)

            x_v = x[0, :, :].rearrange("(t p) d -> p t d", p=P)
            act.wait_ge(chunk_done.sem, chunk_done.value())
            act.dma_start(x_half[0][:, :, :], x_v[:, 0:TT // 2, :]).then_inc(xh_loaded.sem, xh_loaded.up())
            ssq_ready.add(MH)
            act.wait_ge(ssq_ready.sem, ssq_ready.value())
            f(rstd[:, :, NH:NH + MH], ssq[:, :, NH:NH + MH], ACT.Sqrt, scale=1.0 / MDH, bias=EPS).then_inc(
                std_ready.sem, std_ready.up())
            for k in range(4):
                for c in range(2):
                    b = chunk()
                    f(h_hi[:, k, c * HALF:c * HALF + HALF], ps[:, b, :], ACT.Copy,
                                   scale=gains[:, G_HEAD, k:k + 1]).then_inc(hi_ready.sem, hi_ready.up())
            for k in range(4, 8):
                for c in range(2):
                    chunk_done.add(1)
                    freed_now()
                    f(h_hi[:, k, c * HALF:c * HALF + HALF], gated[2 * (k % 2) + c][:, :], ACT.Copy).then_inc(
                        hi_ready.sem, hi_ready.up())
            act.wait_ge(chunk_done.sem, chunk_done.value())
            act.dma_start(mem_tok[:, :, :], mem[0, :, :].rearrange("(t p) d -> p t d", p=P)).then_inc(
                mem_loaded.sem, mem_loaded.up())
            act.dma_start(x_half[1][:, :, :], x_v[:, TT // 2:TT, :]).then_inc(xh_loaded.sem, xh_loaded.up())


            def square(u, src):
                freed_now()
                act.wait_ge(sq_used.sem, sq_used.value(1))
                f(sq[u][:, :], src, ACT.Square).then_inc(sq_ready.sem, sq_ready.up())
                sq_used.add(1)

            def square_loop(turns=KT // 2):
                x_flat = x_t[:, :, :].rearrange("p k s -> p (k s)")
                with engine_loop(act, turns, [(chunk_done, 4), (sq_ready, 2), (sq_used, 2)]) as i:
                    for u in range(2):
                        chunk_done.add(2)
                        at_tile = act.snap(i * (2 * SEQ) + (KT - 2 * turns + u) * SEQ)
                        square(u, x_flat[:, bass.ds(at_tile, SEQ)])

            def norm_root():
                act.wait_ge(col_ready.sem, col_ready.next())
                f(col[:, 0, :], col[:, 0, :], ACT.Sqrt, scale=1.0 / D, bias=EPS).then_inc(
                    std_ready.sem, std_ready.up())

            def split_hi(src, n0, n1, gain=None):
                for n in range(n0, n1):
                    k, cs = n % KT, slice(n // KT * HALF, n // KT * HALF + HALF)
                    f(h_hi[:, k, cs], src[:, k, cs], ACT.Copy,
                      scale=1.0 if gain is None else gains[:, gain, k:k + 1]).then_inc(hi_ready.sem, hi_ready.up())

            act.wait_ge(mem_loaded.sem, mem_loaded.value())
            for i in range(MEMT):
                f(sq[0][:, :], mem_tok[:, i, :], ACT.Square, accum_out=ssq[:, i, 0:1]).then_inc(
                    junk_written.sem, junk_written.up())
                act.wait_ge(junk_written.sem, junk_written.value())
            f(rstd[:, 0:MEMT, 0:1], ssq[:, 0:MEMT, 0:1], ACT.Sqrt, scale=1.0 / D, bias=EPS).then_inc(
                std_ready.sem, std_ready.up())
            sq_used.add(2)
            chunk_done.add(2 + 2 * KT)
            square(0, x_t[:, 0, :])
            chunk_done.add(2)
            square(1, x_t[:, 1, :])
            square_loop(KT // 2 - 1)
            for k in range(KT):
                b = chunk()
                f(hm_hi[:, k, :], ps[:, b, 0:MEM], ACT.Copy, scale=gains[:, G_MKV, k:k + 1]).then_inc(
                    hi_ready.sem, hi_ready.up())
            w_loaded = [w_loaded0, w_loaded1]
            w_loaded0.add((FIRST_KV + 1) // 2)
            w_loaded1.add(FIRST_KV // 2)
            tile_started.add(FIRST_KV)
            for n in range(2 * KT):
                slot = (FIRST_KV + n) % 2
                act.wait_ge(w_loaded[slot].sem, w_loaded[slot].next())
                act.wait_ge(tile_started.sem, tile_started.value())
                f(w_hi[slot][:, :], w_raw[slot][:, :], ACT.Copy).then_inc(kv_hi_made.sem, kv_hi_made.up())
                tile_started.add(1)
                if n == 0:
                    norm_root()
                if n < 4:
                    split_hi(x_t, 4 * n, 4 * n + 4, G_MQ)
            chunk_done.add(2 * KT + 2 * MEMT)
            with engine_loop(act, XH, [(chunk_done, 20), (x_shift_ready, TT), (x_exp_ready, TT)]):
                chunk_done.add(4)
                for what, i in X_ORDER:
                    b = ring.bank()
                    chunk_done.add(1)
                    if what == "s":
                        act.wait_ge(x_shift_ready.sem, x_shift_ready.next())
                        f(xp[i % 4][:, :], ps[:, b, 0:MEM], ACT.Exp, bias=shift[:, i % 4:i % 4 + 1],
                                    accum_out=sums[:, i % 4:i % 4 + 1]).then_inc(x_exp_ready.sem, x_exp_ready.up())
            freed_now()
            split_hi(xo, 0, 2 * KT)
            sq_used.add(2)
            square_loop()
            split_hi(x_t, 0, KT, G_FFN)
            norm_root()
            split_hi(x_t, KT, 2 * KT, G_FFN)

            ring.resize(8)
            def first_tap(s):
                chunk_done.add(2)
                freed_now()
                f(fc[s][:, :], fu[s][:, 8:8 + SEQ], ACT.Copy, scale=fw[:, s, FTAPS - 1:FTAPS]).then_inc(
                    tap_ready.sem, tap_ready.up())

            def pair(b, downs):
                first_tap(0)
                act.wait_ge(conv_done.sem, conv_done.next())
                f(fg[:, :], fc[0][:, :], ACT.Gelu).then_inc(gelu_ready.sem, gelu_ready.up())
                if z_ready.past(0):
                    act.wait_ge(z_ready.sem, z_ready.value())
                first_tap(1)
                conv_done.add(1)
                chunk_done.add(16 * downs)
                act.wait_ge(z_made.sem, z_made.next())
                f(z_hi[b][:, :], fc[1][:, :], ACT.Copy).then_inc(hi_ready.sem, hi_ready.up())
                z_ready.add(1)

            pair(0, 0)
            with engine_loop(act, (FT - 2) // 2, [(conv_done, 4), (chunk_done, 40), (tap_ready, 4), (gelu_ready, 2),
                                                  (z_made, 2), (z_ready, 2), (hi_ready, 2)]):
                pair(1, 1)
                pair(0, 1)
            pair(1, 1)
            chunk_done.add(16)

            for i in range(TT):
                act.wait_ge(y_t_ready.sem, y_t_ready.next())
                f(sq[i % 2][:, :], ps_flat[:, 2 * (i % 4) * HALF:2 * (i % 4) * HALF + D], ACT.Square,
                  accum_out=ssq[:, i, 0:1]).then_inc(junk_written.sem, junk_written.up())
                act.wait_ge(junk_written.sem, junk_written.value())
                f(rstd[:, i, 0:1], ssq[:, i, 0:1], ACT.Sqrt, scale=1.0 / D, bias=EPS).then_inc(
                    std_ready.sem, std_ready.up())

        @block.vector
        def _(dve):
            t = View()
            chunk_done, chunk_freed, conv_done = t("chunk_done"), t("chunk_freed"), t("conv_done")
            conv_ready, decay_ready, diag_ready = t("conv_ready"), t("decay_ready"), t("diag_ready")
            f_abs_ready, gate_done, gates_ready = t("f_abs_ready"), t("gate_done"), t("gates_ready")
            gelu_ready, h_ready, hi_ready = t("gelu_ready"), t("h_ready"), t("hi_ready")
            hm_ready, hm_taken, khi_ready = t("hm_ready"), t("hm_taken"), t("khi_ready")
            ln_step, log_rows_ready, mem_scaled = t("ln_step"), t("log_rows_ready"), t("mem_scaled")
            mixed_ready, o_ready, o_stage_taken = t("mixed_ready"), t("o_ready"), t("o_stage_taken")
            o_taken, pick_ready, probs_ready = t("o_taken"), t("pick_ready"), t("probs_ready")
            pt_copied1, pt_made1, q_hi_ready = t("pt_copied1"), t("pt_made1"), t("q_hi_ready")
            q_ready, qk_ready, r_col_ready = t("q_ready"), t("qk_ready"), t("r_col_ready")
            scores_ready, shift_ready, split_ready = t("scores_ready"), t("shift_ready"), t("split_ready")
            sq_ready, sq_used, ssq_ready = t("sq_ready"), t("sq_used"), t("ssq_ready")
            std_ready, col_ready, sums_ready = t("std_ready"), t("col_ready"), t("sums_ready")
            spread_ready, tap_ready = t("spread_ready"), t("tap_ready")
            vector_chain, x_exp_ready, x_scaled = t("vector_chain"), t("x_exp_ready"), t("x_scaled")
            x_shift_ready, xv_ready, y_ready = t("x_shift_ready"), t("xv_ready"), t("y_ready")
            z_made, z_ready = t("z_made"), t("z_ready")
            params_loaded = t("params_loaded", 16)
            tt, ts, stt = dve.tensor_tensor, dve.tensor_scalar, dve.scalar_tensor_tensor
            ring = Ring(chunk_done)

            def chunk(k=1):
                assert chunk_freed.n == chunk_done.n
                b = ring.bank()
                chunk_done.add(k)
                dve.wait_ge(chunk_done.sem, chunk_done.value())
                return b

            def both(b):
                assert b % 2 == 0
                return ps_flat[:, b * HALF:b * HALF + SEQ]

            def wait_hi():
                dve.wait_ge(hi_ready.sem, hi_ready.next())

            def low(out_lo, src, hi, gain=None):
                if gain is None:
                    return tt(out_lo, src, hi.bitcast(FP32), ALU.subtract)
                return stt(out_lo, src, gain, hi.bitcast(FP32), ALU.mult, ALU.subtract)

            for n in range(0, 4, 2):
                b = chunk()
                width = PAR_TILES[n][0] + PAR_TILES[n + 1][0]
                dve.tensor_copy(par[:, PAR_TILES[n][1]:PAR_TILES[n][1] + width], ps[:, b, 0:width]).then_inc(
                    chunk_freed.sem, chunk_freed.up())
            dve.wait_ge(chunk_freed.sem, chunk_freed.value())
            for half in range(2):
                hs = slice(4 * half, 4 * half + 4)
                dve.wait_ge(std_ready.sem, std_ready.next())
                dve.reciprocal(rstd[:, hs, 0:1], rstd[:, hs, 0:1]).then_inc(vector_chain.sem, vector_chain.up())
                dve.wait_ge(vector_chain.sem, vector_chain.value())
                for i in range(4 * half, 4 * half + 4):
                    ts(x_tok[:, i, :], x_tok[:, i, :], rstd[:, i, 0:1], None, ALU.mult).then_inc(
                        x_scaled.sem, x_scaled.up())
            for half in range(2):
                for k in range(KT):
                    b = chunk()
                    wait_hi()
                    low(h_lo[:, k, half * HALF:half * HALF + HALF], ps[:, b, :],
                             h_hi[:, k, half * HALF:half * HALF + HALF], gains[:, G_MIX, k:k + 1]).then_inc(
                                 chunk_freed.sem, chunk_freed.up())

            for z in (kc_a, kc_b, vc):
                dve.memset(whole(z).bitcast(FP32), 0.0).then_inc(vector_chain.sem, vector_chain.up())
            params_loaded.add(PARAM_LOADS)
            dve.wait_ge(params_loaded.sem, params_loaded.value())
            for kv in range(2):
                for c in range(2):
                    b = chunk()
                    for part in range(2):
                        cs = slice(c * HALF, c * HALF + HALF)
                        ins = tt(kvp[:, kv, part, cs].rearrange("p (n l) -> p n l", l=CMP_STRIDE),
                                 ps[:, b, :].rearrange("p (n l) -> p n l", l=CMP_STRIDE),
                                 pos[:, kv, None, part * CMP_STRIDE:part * CMP_STRIDE + CMP_STRIDE].to_broadcast(
                                     [P, HALF // CMP_STRIDE, CMP_STRIDE]), ALU.add)
                    ins.then_inc(chunk_freed.sem, chunk_freed.up())
            for kv in range(2):
                for g in range(G):
                    b = chunk()
                    dve.tensor_copy(hid[:, kv, g, :], ps[0:CMP_HID, b, 0:NCMP]).then_inc(
                        chunk_freed.sem, chunk_freed.up())
            b = chunk()
            dve.wait_ge(vector_chain.sem, vector_chain.value())
            for g in range(G):
                src = ps[0:DH, b, DH * g:DH * g + NCMP]
                dve.tensor_copy(kc_b[rows(1), g, 0:NCMP], src).then_inc(vector_chain.sem, vector_chain.up())
                dve.tensor_copy(kc_a[rows(0), g, 0:NCMP], src).then_inc(vector_chain.sem, vector_chain.up())
                dve.wait_ge(vector_chain.sem, vector_chain.value())
                low(kc_a[rows(1), g, 0:NCMP], src, kc_a[rows(0), g, 0:NCMP]).then_inc(
                    vector_chain.sem, vector_chain.up())
                last = low(kc_b[rows(0), g, 0:NCMP], src, kc_a[rows(0), g, 0:NCMP])
                if g == 0:
                    last.then_inc(vector_chain.sem, vector_chain.up())
            last.then_inc(chunk_freed.sem, chunk_freed.up())
            b = chunk()
            dve.tensor_copy(vc[0:NCMP, :, :], ps[0:NCMP, b, 0:P].rearrange("n (g d) -> n g d", g=G)).then_inc(
                chunk_freed.sem, chunk_freed.up())
            for br in range(2):
                for c in range(2):
                    b = chunk()
                    cs = slice(c * HALF, c * HALF + HALF)
                    for g in range(G):
                        khi_ready.add(2)
                        dve.wait_ge(khi_ready.sem, khi_ready.value())
                        low(k_a[br][rows(1 - g), g, cs], ps[rows(g), b, :], k_a[br][rows(g), g, cs]).then_inc(
                            vector_chain.sem, vector_chain.up())
                        last = low(k_b[br][rows(g), g, cs], ps[rows(g), b, :], k_a[br][rows(g), g, cs])
                        if g == 0:
                            last.then_inc(vector_chain.sem, vector_chain.up())
                    last.then_inc(chunk_freed.sem, chunk_freed.up())
                b = chunk(2)
                dve.tensor_copy(v_feat[:, br, :], both(b)).then_inc(chunk_freed.sem, chunk_freed.up(2))
            b = chunk(2)
            dve.tensor_copy(g_rows[:, :], ps_flat[0:NH * 3, b * HALF:b * HALF + SEQ]).then_inc(
                vector_chain.sem, vector_chain.up())
            dve.tensor_copy(g_i[:, :], ps_flat[R_I:R_I + MH, b * HALF:b * HALF + SEQ]).then_inc(
                vector_chain.sem, vector_chain.up())
            dve.tensor_copy(g_f[:, :], ps_flat[R_F:R_F + MH, b * HALF:b * HALF + SEQ]).then_inc(
                chunk_freed.sem, chunk_freed.up(2))
            dve.wait_ge(vector_chain.sem, vector_chain.value())
            dve.wait_ge(chunk_freed.sem, chunk_freed.value())
            ts(g_i[:, :], g_i[:, :], bias_if[:, 0:1], None, ALU.add).then_inc(vector_chain.sem, vector_chain.up())
            dve.wait_ge(vector_chain.sem, vector_chain.value())
            ts(g_f[:, :], g_f[:, :], bias_if[:, 1:2], None, ALU.add).then_inc(vector_chain.sem, vector_chain.up())
            dve.wait_ge(vector_chain.sem, vector_chain.value())
            stt(g_t[:, :], g_f[:, :], -1.0, g_f[:, :], ALU.mult, ALU.min).then_inc(f_abs_ready.sem, f_abs_ready.up())
            for k in range(4):
                b = chunk(2)
                ts(nq[:, k, :], both(b), DH ** -0.5, None, ALU.mult).then_inc(chunk_freed.sem, chunk_freed.up(2))
            ln_step.add(2)
            dve.wait_ge(ln_step.sem, ln_step.value())
            stt(g_f[:, :], g_f[:, :], 0.0, g_t[:, :], ALU.min, ALU.subtract).then_inc(
                vector_chain.sem, vector_chain.up())
            dve.wait_ge(vector_chain.sem, vector_chain.value())
            dve.tensor_tensor_scan(g_t[:, :], g_f[:, :], g_f[:, :], 0.0, ALU.add, ALU.min).then_inc(
                vector_chain.sem, vector_chain.up())
            dve.wait_ge(vector_chain.sem, vector_chain.value())
            tt(g_i[:, :], g_i[:, :], g_t[:, :], ALU.subtract).then_inc(vector_chain.sem, vector_chain.up())
            dve.wait_ge(vector_chain.sem, vector_chain.value())
            dve.tensor_tensor_scan(m_rows[:, :], g_i[:, :], g_i[:, :], 0.0, ALU.max, ALU.max).then_inc(
                vector_chain.sem, vector_chain.up())
            dve.wait_ge(vector_chain.sem, vector_chain.value())
            tt(g_f[:, :], g_t[:, :], m_rows[:, :], ALU.add).then_inc(log_rows_ready.sem, log_rows_ready.up())
            for br in range(2):
                for q in range(2):
                    b = chunk()
                    dve.tensor_copy(v_tok[:, br, 4 * q:4 * q + 4, :],
                                         ps[:, b, :].rearrange("p (t d) -> p t d", d=P)).then_inc(
                                             chunk_freed.sem, chunk_freed.up())
            b = chunk()
            dve.tensor_copy(gate_sig[:, :, :],
                                 ps[:, b, 0:TT * 32].rearrange("p (t h) -> p t h", h=32)[:, :, 0:NH * 3]).then_inc(
                                     chunk_freed.sem, chunk_freed.up())
            b = chunk()
            dve.tensor_copy(log_in[:, :, :], ps[:, b, 0:TT * MH].rearrange("p (t h) -> p t h", h=MH)).then_inc(
                o_stage_taken.sem, o_stage_taken.up())
            dve.tensor_copy(den_floor[:, :, :], ps[:, b, 64:64 + TT * MH].rearrange("p (t h) -> p t h", h=MH)).then_inc(
                chunk_freed.sem, chunk_freed.up())
            dve.wait_ge(gates_ready.sem, gates_ready.next())
            tt(gate_sig[:, 0, 0:NH * 3:3], gate_sig[:, 0, 0:NH * 3:3], keep_cmp[:, :].to_broadcast([P, NH]), ALU.mult).then_inc(
                vector_chain.sem, vector_chain.up())
            dve.wait_ge(vector_chain.sem, vector_chain.value())

            CH_B = 2 + 2 * JOBS + 2 * (JOBS // 2)
            loop = lambda n, k: engine_loop(dve, n, [(q_hi_ready, 2 * k), (q_ready, 2 * k), (probs_ready, k * JOBS),
                                                     (scores_ready, k * JOBS), (shift_ready, k * JOBS), (pt_made1, k * JOBS_1),
                                                     (pt_copied1, k * JOBS_1), (o_ready, k * JOBS), (o_taken, k * JOBS),
                                                     (o_stage_taken, 2 * k), (vector_chain, k * CH_B)])
            dve.wait_ge(q_hi_ready.sem, q_hi_ready.next())
            low(q_st[0][rows(1), :], nq[rows(0), 0, :], q_st[0][rows(0), :]).then_inc(q_ready.sem, q_ready.up())
            with loop(G, 2) as g:
                with loop(2, 1) as hp:
                    at_q = dve.snap((g * 2 + hp) * SEQ)
                    at_h = dve.snap((g * 2 + hp) * 6)
                    nq_flat = nq[:, :, :].rearrange("p a s -> p (a s)")
                    at_next = dve.snap((g * 2 + hp + 1) % (NH // 2) * SEQ)
                    for u in range(2):
                        dve.tensor_copy(gate_h[:, u, :, :], gate_sig[:, :, bass.ds(at_h + 3 * u, 3)]).then_inc(
                            vector_chain.sem, vector_chain.up())
                    for st in range(JOBS + 4):
                        if st - 1 in Q_SPLITS:
                            u, at_head = (1, at_q) if st - 1 == Q_SPLITS[0] else (0, at_next)
                            dve.wait_ge(q_hi_ready.sem, q_hi_ready.next())
                            low(q_st[u][rows(1 - u), :], nq_flat[rows(u), bass.ds(at_head, SEQ)],
                                q_st[u][rows(u), :]).then_inc(q_ready.sem, q_ready.up())
                        if st < JOBS:
                            u, i, br = job_of(st)
                            n = (i + 1 if br == 0 else min(i, WT) + 1) * P
                            c0 = 2 * (st % 4)
                            flat = ps_flat[:, 2 * (st % 2) * HALF:2 * (st % 2) * HALF + 2 * HALF]
                            dve.wait_ge(scores_ready.sem, scores_ready.next())
                            if br == 0:
                                dve.tensor_reduce(shift[:, c0:c0 + 1], flat[:, 0:n], AX.X, ALU.max,
                                                                  negate=True).then_inc(
                                                                      shift_ready.sem, shift_ready.up())
                            else:
                                dve.tensor_reduce(shift[:, c0 + 1:c0 + 2], flat[:, 0:n], AX.X, ALU.max, negate=True).then_inc(
                                    vector_chain.sem, vector_chain.up())
                                dve.tensor_reduce(shift[:, c0:c0 + 1], flat[:, 5 * P:5 * P + DH], AX.X,
                                                                  ALU.max, negate=True).then_inc(
                                                                      shift_ready.sem, shift_ready.up())
                        z = st - 3
                        if 0 <= z < JOBS:
                            w = 1 + job_of(z)[2]
                            c0 = 2 * (z % 4)
                            dve.wait_ge(probs_ready.sem, probs_ready.next())
                            dve.reciprocal(coef[:, c0:c0 + w], sums[:, c0:c0 + w]).then_inc(
                                vector_chain.sem, vector_chain.up())
                        z = st - 2
                        if 0 <= z < JOBS:
                            u, i, br = job_of(z)
                            n = i + 1 if br == 0 else min(i, WT) + 1
                            if has_second(z):
                                dve.wait_ge(pt_made1.sem, pt_made1.next())
                                if n > 4:
                                    ins = dve.tensor_copy(probs_t[z % 2][:, 4:n, :],
                                                          ps[:, 5, 0:(n - 4) * P].rearrange("p (a k) -> p a k", k=P))
                                if br == 1:
                                    ins = dve.tensor_copy(probs_t[z % 2][0:DH, TT - 1, :], ps[0:DH, 5, 3 * P:4 * P])
                                ins.then_inc(pt_copied1.sem, pt_copied1.up())
                        z = st - 3
                        if 0 <= z < JOBS:
                            u, i, br = job_of(z)
                            c0 = 2 * (z % 4)
                            w = 1 + br
                            dve.wait_ge(vector_chain.sem, vector_chain.value())
                            tt(coef[:, c0:c0 + w], coef[:, c0:c0 + w],
                               gate_h[:, u, i, 1:2] if br == 0 else gate_h[:, u, i, 0:3:2], ALU.mult).then_inc(
                                   vector_chain.sem, vector_chain.up())
                        z = st - 4
                        if 0 <= z < JOBS:
                            u, i, br = job_of(z)
                            c0 = 2 * (z % 4)
                            o = ps[:, 6 + z % 2, :]
                            if z == 0:
                                dve.wait_ge(o_stage_taken.sem, o_stage_taken.value())
                            dve.wait_ge(vector_chain.sem, vector_chain.value(1 if st - 3 < JOBS else 0))
                            dve.wait_ge(o_ready.sem, o_ready.next())
                            parts = [(o[:, 0:DH], coef[:, c0 + br:c0 + br + 1])]
                            if br == 1:
                                parts.append((o[:, DH:2 * DH], coef[:, c0:c0 + 1]))
                            for a, (part, by) in enumerate(parts):
                                if a == 0 and comes_first(z):
                                    ins = ts(o_stage[:, u, i, :], part, by, None, ALU.mult)
                                else:
                                    if a == 0:
                                        dve.wait_ge(o_taken.sem, o_taken.value())
                                    ins = stt(o_stage[:, u, i, :], part, by, o_stage[:, u, i, :], ALU.mult, ALU.add)
                                if a < len(parts) - 1:
                                    ins.then_inc(vector_chain.sem, vector_chain.up())
                                    dve.wait_ge(vector_chain.sem, vector_chain.value())
                            ins.then_inc(o_taken.sem, o_taken.up())
                    o_stage_taken.add(2)

            dve.wait_ge(o_stage_taken.sem, o_stage_taken.value())
            nsa_sq = x_t[:, 0:4, :].rearrange("p k s -> p (k s)")
            nsa_v = o_nsa[:, :, :].rearrange("p t d -> p (t d)")
            tt(nsa_sq, nsa_v, nsa_v, ALU.mult).then_inc(vector_chain.sem, vector_chain.up())
            dve.wait_ge(vector_chain.sem, vector_chain.value())
            dve.tensor_reduce(ssq[:, :, 0:NH], nsa_sq.rearrange("p (t h d) -> p t h d", h=NH, d=DH),
                              AX.X, ALU.add).then_inc(ssq_ready.sem, ssq_ready.up())
            std_ready.add(1)
            dve.wait_ge(std_ready.sem, std_ready.value())
            dve.reciprocal(rstd[:, :, 0:NH], rstd[:, :, 0:NH]).then_inc(vector_chain.sem, vector_chain.up())
            dve.wait_ge(vector_chain.sem, vector_chain.value())
            for i in range(TT):
                tt(o_nsa[:, i, :].rearrange("p (h d) -> p h d", d=DH),
                   o_nsa[:, i, :].rearrange("p (h d) -> p h d", d=DH),
                   rstd[:, i, 0:NH, None].to_broadcast([P, NH, DH]), ALU.mult).then_inc(
                       vector_chain.sem, vector_chain.up())
            dve.memset(u_raw[:, 0:4], 0.0).then_inc(vector_chain.sem, vector_chain.up())
            dve.memset(mv_tok[:, :, MDH:MDH + 1], 1.0).then_inc(hm_taken.sem, hm_taken.up())
            CH_C = 38
            ring.resize(8)
            with engine_loop(dve, MH, [(chunk_done, 32), (chunk_freed, 32), (ssq_ready, 1), (vector_chain, CH_C), (conv_ready, 2), (hi_ready, 2),
                                       (qk_ready, 1), (pick_ready, 1), (diag_ready, 1),
                                       (decay_ready, 12), (hm_ready, 1), (hm_taken, 1)]) as h:
                dve.tensor_copy(head_w[:, 0, :], conv_m[:, :, bass.ds(h, 1)]).then_inc(
                    vector_chain.sem, vector_chain.up())
                dve.tensor_copy(head_w[:, 1, :], conv_m[:, :, bass.ds(dve.snap(h + MH), 1)]).then_inc(
                    vector_chain.sem, vector_chain.up())
                dve.tensor_copy(head_a[:, 0, :], log_in[:, :, bass.ds(h, 1)]).then_inc(
                    vector_chain.sem, vector_chain.up())
                dve.tensor_copy(head_a[:, 1, :], den_floor[:, :, bass.ds(h, 1)]).then_inc(
                    vector_chain.sem, vector_chain.up())
                ts(m_pick[:, :], ident[0:MH, bass.ds(h, 1)].to_broadcast([MH, P]), -1.0, None, ALU.mult).then_inc(
                    pick_ready.sem, pick_ready.up())
                dve.wait_ge(hm_taken.sem, hm_taken.value())
                for s, (hi, lo, scale) in enumerate(((mq_hi, mq_lo, MDH ** -0.5), (mk_hi, mk_lo, 1.0))):
                    b = chunk(2)
                    dve.tensor_copy(u_raw[:, 4:4 + SEQ], both(b)).then_inc(chunk_freed.sem, chunk_freed.up(2))
                    dve.wait_ge(chunk_freed.sem, chunk_freed.value())
                    dve.wait_ge(vector_chain.sem, vector_chain.value())
                    ts(u_conv[:, :], u_raw[:, 4:4 + SEQ], head_w[:, s, TAPS - 1:TAPS], None, ALU.mult).then_inc(
                        vector_chain.sem, vector_chain.up())
                    dve.wait_ge(vector_chain.sem, vector_chain.value())
                    for k in range(1, TAPS):
                        ins = stt(u_conv[:, :], u_raw[:, 4 - k:4 - k + SEQ], head_w[:, s, TAPS - 1 - k:TAPS - k],
                                  u_conv[:, :], ALU.mult, ALU.add)
                        if k < TAPS - 1:
                            ins.then_inc(vector_chain.sem, vector_chain.up())
                            dve.wait_ge(vector_chain.sem, vector_chain.value())
                    ins.then_inc(conv_ready.sem, conv_ready.up())
                    wait_hi()
                    ins = low(lo[:, :], u_conv[:, :], hi[:, :], scale)
                    if s == 0:
                        ins.then_inc(vector_chain.sem, vector_chain.up())
                    else:
                        ins.then_inc(qk_ready.sem, qk_ready.up())
                b = chunk(2)
                dve.tensor_copy(mv_feat[:, :], both(b)).then_inc(chunk_freed.sem, chunk_freed.up(2))
                b = chunk(2)
                dve.tensor_copy(m_bc[:, :], both(b)).then_inc(chunk_freed.sem, chunk_freed.up(2))
                dve.wait_ge(chunk_freed.sem, chunk_freed.value())
                dve.wait_ge(qk_ready.sem, qk_ready.value())
                for j in range(TT):
                    js = slice(j * P, j * P + P)
                    ins = stt(u_conv[:, js], m_bc[:, js], head_a[:, 0, j:j + 1], mmask[:, :], ALU.add, ALU.min)
                    if j < TT - 1:
                        ins.then_inc(vector_chain.sem, vector_chain.up())
                ins.then_inc(diag_ready.sem, diag_ready.up())
                b = chunk(2)
                dve.tensor_copy(o_gate[:, bass.ds(h, 1), :], both(b)).then_inc(chunk_freed.sem, chunk_freed.up(2))
                for q in range(2):
                    b = chunk()
                    dve.tensor_copy(mv_tok[:, 4 * q:4 * q + 4, 0:MDH],
                                         ps[:, b, :].rearrange("p (t d) -> p t d", d=P)).then_inc(
                                             chunk_freed.sem, chunk_freed.up())
                decay_ready.add(1)
                for n, (j, a, e) in enumerate(pieces):
                    b = chunk()
                    a2 = a + P if a == P * j else a
                    first = tri_at(j, a // P)
                    if a2 < e:
                        decay_ready.add(1)
                    dve.wait_ge(decay_ready.sem, decay_ready.value())
                    if a2 > a:
                        ins = tt(tri[:, first, :], ps[:, b, 0:P], u_conv[:, j * P:j * P + P], ALU.mult)
                        if a2 < e:
                            ins.then_inc(vector_chain.sem, vector_chain.up())
                    if a2 < e:
                        at_blk = first + (a2 - a) // P
                        ins = tt(tri[:, at_blk:at_blk + (e - a2) // P, :].rearrange("p b t -> p (b t)"),
                                 ps[:, b, a2 - a:e - a], decay[n % 2][:, 0:e - a2], ALU.mult)
                    ins.then_inc(chunk_freed.sem, chunk_freed.up())
                hv = u_raw[:, 4:4 + SEQ].rearrange("p (t d) -> p t d", d=MDH)
                for i in range(TT):
                    b = chunk()
                    dve.tensor_copy(hv[:, i, :], ps[:, b, 0:MDH]).then_inc(vector_chain.sem, vector_chain.up())
                    dve.tensor_copy(head_d[:, 0, i:i + 1], ps[:, b, MDH:MDH + 1]).then_inc(
                        chunk_freed.sem, chunk_freed.up())
                dve.wait_ge(chunk_freed.sem, chunk_freed.value())
                stt(head_d[:, 1, :], head_d[:, 0, :], -1.0, head_d[:, 0, :], ALU.mult, ALU.max).then_inc(
                    vector_chain.sem, vector_chain.up())
                dve.wait_ge(vector_chain.sem, vector_chain.value())
                tt(head_d[:, 1, :], head_d[:, 1, :], head_a[:, 1, :], ALU.max).then_inc(
                    vector_chain.sem, vector_chain.up())
                dve.wait_ge(vector_chain.sem, vector_chain.value())
                dve.reciprocal(head_d[:, 1, :], head_d[:, 1, :]).then_inc(vector_chain.sem, vector_chain.up())
                dve.wait_ge(vector_chain.sem, vector_chain.value())
                cv = u_conv[:, :].rearrange("p (t d) -> p t d", d=MDH)
                tt(cv, hv, head_d[:, 1, :, None].to_broadcast([P, TT, MDH]), ALU.mult).then_inc(
                    hm_ready.sem, hm_ready.up())
                dve.wait_ge(hm_ready.sem, hm_ready.value())
                tt(hv, cv, cv, ALU.mult).then_inc(vector_chain.sem, vector_chain.up())
                dve.wait_ge(vector_chain.sem, vector_chain.value())
                dve.tensor_reduce(head_d[:, 2, :], hv, AX.X, ALU.add).then_inc(vector_chain.sem, vector_chain.up())
                dve.wait_ge(vector_chain.sem, vector_chain.value())
                dve.tensor_copy(ssq[:, :, bass.ds(dve.snap(h + NH), 1)], head_d[:, 2, :, None]).then_inc(
                    ssq_ready.sem, ssq_ready.up())
                hm_taken.add(1)

            ring.resize(4)

            dve.wait_ge(hm_taken.sem, hm_taken.value())
            std_ready.add(1)
            dve.wait_ge(std_ready.sem, std_ready.value())
            dve.reciprocal(rstd[:, :, NH:NH + MH], rstd[:, :, NH:NH + MH]).then_inc(vector_chain.sem, vector_chain.up())
            dve.wait_ge(vector_chain.sem, vector_chain.value())
            for i in range(TT):
                ins = tt(h_mls[:, i, :].rearrange("p (h d) -> p h d", d=MDH),
                         h_mls[:, i, :].rearrange("p (h d) -> p h d", d=MDH),
                         rstd[:, i, NH:NH + MH, None].to_broadcast([P, MH, MDH]), ALU.mult)
            ins.then_inc(mixed_ready.sem, mixed_ready.up())

            for k in range(4):
                for c in range(2):
                    b = chunk()
                    wait_hi()
                    cs = slice(c * HALF, c * HALF + HALF)
                    low(h_lo[:, k, cs], ps[:, b, :], h_hi[:, k, cs], gains[:, G_HEAD, k:k + 1]).then_inc(
                        chunk_freed.sem, chunk_freed.up())
            gate_done.add(MH)
            dve.wait_ge(gate_done.sem, gate_done.value())

            def gated_piece(n):
                k, c = 4 + n // 2, n % 2
                b = chunk()
                if n >= 4:
                    dve.wait_ge(split_ready.sem, n - 3)
                stt(gated[n % 4][:, :], ps[:, b, :], gains[:, G_HEAD, k:k + 1], o_gate[:, k - 4, c * HALF:c * HALF + HALF],
                    ALU.mult, ALU.mult).then_inc(chunk_freed.sem, chunk_freed.up())

            gated_piece(0)
            for n in range(8):
                k, c = 4 + n // 2, n % 2
                if n < 7:
                    gated_piece(n + 1)
                dve.wait_ge(chunk_freed.sem, chunk_freed.value())
                wait_hi()
                low(h_lo[:, k, c * HALF:c * HALF + HALF], gated[n % 4][:, :], h_hi[:, k, c * HALF:c * HALF + HALF]).then_inc(
                    split_ready.sem, split_ready.up())

            def clear_sums():
                for c in range(2):
                    dve.memset(acc[:, c * HALF:c * HALF + HALF], 0.0).then_inc(sq_used.sem, sq_used.up())
                    dve.wait_ge(sq_used.sem, sq_used.value())

            def add_square(u):
                dve.wait_ge(sq_ready.sem, sq_ready.next())
                dve.wait_ge(sq_used.sem, sq_used.value())
                tt(acc[:, :], acc[:, :], sq[u][:, :], ALU.add).then_inc(sq_used.sem, sq_used.up())

            def residual_loop(turns=KT // 2):
                with engine_loop(dve, turns, [(chunk_done, 4), (chunk_freed, 4), (sq_ready, 2), (sq_used, 2)]) as i:
                    x_flat = x_t[:, :, :].rearrange("p k s -> p (k s)")
                    for u in range(2):
                        b = chunk(2)
                        dst = x_flat[:, bass.ds(dve.snap(i * (2 * SEQ) + (KT - 2 * turns + u) * SEQ), SEQ)]
                        tt(dst, both(b), dst, ALU.add).then_inc(chunk_freed.sem, chunk_freed.up(2))
                    for u in range(2):
                        add_square(u)
                dve.wait_ge(chunk_freed.sem, chunk_freed.value())

            def columns_start():
                dve.wait_ge(sums_ready.sem, sums_ready.next())
                dve.tensor_copy(col[:, 0, :], ps[:, 4, 0:TT]).then_inc(col_ready.sem, col_ready.up())

            def columns_end():
                dve.wait_ge(std_ready.sem, std_ready.next())
                dve.reciprocal(col[:, 0, :], col[:, 0, :]).then_inc(r_col_ready.sem, r_col_ready.up())

            def copy_spread(dst, bank):
                dve.wait_ge(spread_ready.sem, spread_ready.next())
                dve.tensor_copy(dst, ps_flat[:, bank * HALF:bank * HALF + SEQ]).then_inc(
                    vector_chain.sem, vector_chain.up())
                dve.wait_ge(vector_chain.sem, vector_chain.value())

            def split_low(src, gain=None):
                for n in range(2 * KT):
                    k, cs = n % KT, slice(n // KT * HALF, n // KT * HALF + HALF)
                    wait_hi()
                    low(h_lo[:, k, cs], src[:, k, cs], h_hi[:, k, cs],
                        None if gain is None else gains[:, gain, k:k + 1]).then_inc(h_ready.sem, h_ready.up())

            dve.wait_ge(std_ready.sem, std_ready.next())
            dve.reciprocal(rstd[:, 0:MEMT, 0:1], rstd[:, 0:MEMT, 0:1]).then_inc(vector_chain.sem, vector_chain.up())
            dve.wait_ge(vector_chain.sem, vector_chain.value())
            for i in range(MEMT):
                ins = ts(mem_tok[:, i, :], mem_tok[:, i, :], rstd[:, i, 0:1], None, ALU.mult)
                if i < MEMT - 1:
                    ins.then_inc(vector_chain.sem, vector_chain.up())
            ins.then_inc(mem_scaled.sem, mem_scaled.up())
            clear_sums()
            b = chunk(2)
            dve.tensor_copy(x_t[:, 0, :], both(b)).then_inc(chunk_freed.sem, chunk_freed.up(2))
            for k in range(KT):
                b = chunk(2)
                if k == 0:
                    dve.wait_ge(chunk_freed.sem, chunk_freed.value())
                    ins = tt(x_t[:, 0, :], both(b), x_t[:, 0, :], ALU.add)
                else:
                    ins = dve.tensor_copy(x_t[:, k, :], both(b))
                ins.then_inc(chunk_freed.sem, chunk_freed.up(2))
            add_square(0)
            b = chunk(2)
            dve.wait_ge(chunk_freed.sem, chunk_freed.value())
            tt(x_t[:, 1, :], both(b), x_t[:, 1, :], ALU.add).then_inc(chunk_freed.sem, chunk_freed.up(2))
            add_square(1)
            residual_loop(KT // 2 - 1)
            for k in range(KT):
                b = chunk()
                wait_hi()
                low(hm_lo[:, k, :], ps[:, b, 0:MEM], hm_hi[:, k, :], gains[:, G_MKV, k:k + 1]).then_inc(
                    chunk_freed.sem, chunk_freed.up())
            columns_start()
            split_low(x_t, G_MQ)
            columns_end()
            for dst in (xk, xv_feat):
                with engine_loop(dve, KT // 4, [(chunk_done, 4), (chunk_freed, 4)]) as i:
                    flat = dst[:, :, :].rearrange("p k m -> p (k m)")
                    for u in range(4):
                        b = chunk()
                        dve.tensor_copy(flat[:, bass.ds(dve.snap(i * (4 * MEM) + u * MEM), MEM)], ps[:, b, 0:MEM]).then_inc(
                            chunk_freed.sem, chunk_freed.up())
                if dst is xk:
                    copy_spread(r_bc[:, :], 6)
            for j in range(MEMT):
                for q in range(2):
                    b = chunk()
                    dve.tensor_copy(xv[:, j, q * HALF:q * HALF + HALF], ps[:, b, :]).then_inc(
                        chunk_freed.sem, chunk_freed.up())
            dve.wait_ge(chunk_freed.sem, chunk_freed.value())
            with engine_loop(dve, XH, [(chunk_done, 20), (chunk_freed, 20), (x_shift_ready, TT), (x_exp_ready, TT), (vector_chain, TT),
                                       (xv_ready, 1)]) as hd:
                dve.tensor_copy(xv_h[:, :, :], xv[:, :, bass.ds(dve.snap(hd * XDH), XDH)]).then_inc(
                    xv_ready.sem, xv_ready.up())
                for n in range(4):
                    z, cs = n // 2, slice(n % 2 * HALF, n % 2 * HALF + HALF)
                    b = chunk()
                    stt(xq[:, z, cs], ps[:, b, :], XDH ** -0.5, r_bc[:, cs], ALU.mult, ALU.mult).then_inc(
                        chunk_freed.sem, chunk_freed.up())
                waiting = []
                x_flat = xo[:, :, :].rearrange("p k s -> p (k s)")

                def finish():
                    i = waiting.pop(0)
                    dve.wait_ge(x_exp_ready.sem, x_exp_ready.next())
                    dve.reciprocal(sums[:, i % 4:i % 4 + 1], sums[:, i % 4:i % 4 + 1]).then_inc(
                        vector_chain.sem, vector_chain.up())
                    dve.wait_ge(vector_chain.sem, vector_chain.value())
                    ts(xp[i % 4][:, :], xp[i % 4][:, :], sums[:, i % 4:i % 4 + 1], None, ALU.mult).then_inc(
                        chunk_freed.sem, chunk_freed.up())

                for what, i in X_ORDER:
                    if what == "s":
                        b = ring.bank()
                        dve.wait_ge(chunk_done.sem, chunk_done.next())
                        dve.tensor_reduce(shift[:, i % 4:i % 4 + 1], ps[:, b, 0:MEM], AX.X, ALU.max,
                                                      negate=True).then_inc(x_shift_ready.sem, x_shift_ready.up())
                        waiting.append(i)
                        if len(waiting) > 1:
                            finish()
                    else:
                        while waiting:
                            finish()
                        b = chunk()
                        if what == "t":
                            ins = dve.tensor_copy(xp_t[:, :, i * P:i * P + 2 * P],
                                                  ps[:, b, :].rearrange("p (j q) -> p j q", j=MEMT))
                        else:
                            at_x = dve.snap(hd * (2 * SEQ) + (i % 2 * SEQ + i // 2 * HALF))
                            ins = dve.tensor_copy(x_flat[:, bass.ds(at_x, HALF)], ps[:, b, :])
                        ins.then_inc(chunk_freed.sem, chunk_freed.up())
            dve.wait_ge(chunk_freed.sem, chunk_freed.value())
            split_low(xo)
            clear_sums()
            residual_loop()
            columns_start()
            split_low(x_t, G_FFN)
            columns_end()

            ring.resize(8)
            for s in range(2):
                dve.memset(fu[s][:, 0:8], 0.0).then_inc(vector_chain.sem, vector_chain.up())
            dve.wait_ge(vector_chain.sem, vector_chain.value())

            def scaled(s):
                b = chunk(2)
                tt(fu[s][:, 8:8 + SEQ], both(b), r_bc[:, :], ALU.mult).then_inc(chunk_freed.sem, chunk_freed.up(2))

            def taps(s):
                dve.wait_ge(tap_ready.sem, tap_ready.next())
                for k in range(1, FTAPS):
                    ins = stt(fc[s][:, :], fu[s][:, 8 - k:8 - k + SEQ], fw[:, s, FTAPS - 1 - k:FTAPS - k], fc[s][:, :],
                              ALU.mult, ALU.add)
                    if k < FTAPS - 1:
                        ins.then_inc(vector_chain.sem, vector_chain.up())
                        dve.wait_ge(vector_chain.sem, vector_chain.value())
                ins.then_inc(conv_done.sem, conv_done.up())

            def down_tiles():
                for m in range(KT):
                    b = chunk(2)
                    tt(x_t[:, m, :], both(b), x_t[:, m, :], ALU.add).then_inc(chunk_freed.sem, chunk_freed.up(2))

            def pair(b, p, downs, last=False):
                at_p = [p + s * FT if isinstance(p, int) else dve.snap(p + s * FT) for s in range(2)]
                dve.tensor_copy(fw[:, 0, :], conv_f[:, :, bass.ds(at_p[0], 1)]).then_inc(
                    vector_chain.sem, vector_chain.up())
                dve.tensor_copy(fw[:, 1, :], conv_f[:, :, bass.ds(at_p[1], 1)]).then_inc(
                    vector_chain.sem, vector_chain.up())
                dve.wait_ge(vector_chain.sem, vector_chain.value())
                scaled(0)
                taps(0)
                scaled(1)
                if downs and not last:
                    down_tiles()
                taps(1)
                dve.wait_ge(conv_done.sem, conv_done.value())
                dve.wait_ge(gelu_ready.sem, gelu_ready.next())
                tt(fc[1][:, :], fg[:, :], fc[1][:, :], ALU.mult).then_inc(z_made.sem, z_made.up())
                dve.wait_ge(z_made.sem, z_made.value())
                wait_hi()
                low(z_lo[b][:, :], fc[1][:, :], z_hi[b][:, :]).then_inc(z_ready.sem, z_ready.up())

            copy_spread(r_bc[:, :], 6)
            copy_spread(gain_bc[:, :], 4)
            pair(0, 0, 0)
            with engine_loop(dve, (FT - 2) // 2, [(chunk_done, 40), (chunk_freed, 40), (vector_chain, 8), (conv_done, 4), (tap_ready, 4),
                                                  (gelu_ready, 2), (z_made, 2), (z_ready, 2),
                                                  (hi_ready, 2)]) as i:
                pair(1, i * 2 + 1, 1)
                pair(0, i * 2 + 2, 1)
            pair(1, FT - 1, 1, last=True)
            down_tiles()
            down_tiles()

            stored = [t(f"stored{b}", 16) for b in range(4)]
            for i in range(TT):
                dve.wait_ge(std_ready.sem, std_ready.next())
                dve.reciprocal(rstd[:, i, 0:1], rstd[:, i, 0:1]).then_inc(vector_chain.sem, vector_chain.up())
                dve.wait_ge(vector_chain.sem, vector_chain.value())
                if i >= 4:
                    dve.wait_ge(stored[i % 4].sem, stored[i % 4].next())
                stt(y_tok[i % 4][:, :], ps_flat[:, 2 * (i % 4) * HALF:2 * (i % 4) * HALF + D], rstd[:, i, 0:1],
                    gain_bc[:, :], ALU.mult, ALU.mult).then_inc(y_ready.sem, y_ready.up())


_INS = ["x", "mem", "g_mix", "w_in", "cmp_pos_k", "cmp_w1_k", "cmp_w2_k", "cmp_pos_v", "cmp_w1_v", "cmp_w2_v",
        "mlstm_conv_w", "mlstm_b_i", "mlstm_b_f", "g_head_nsa", "g_head_mlstm", "w_out", "g_mem_q", "g_mem_kv",
        "w_mem_q", "w_mem_k", "w_mem_v", "w_mem_o", "g_ffn", "w_up", "ffn_conv_w", "w_down", "g_final"]


def kernel(**inputs):
    import numpy as np
    import concourse.bacc as bacc
    from concourse.bass_utils import run_bass_kernel_spmd

    nc = bacc.Bacc("TRN2", target_bir_lowering=False, num_devices=1)
    arrays, args = {}, []
    for name in _INS:
        a = np.ascontiguousarray(inputs[name])
        arrays[f"in_{name}"] = a
        args.append(nc.dram_tensor(f"in_{name}", a.shape, mybir.dt.from_np(a.dtype), kind="ExternalInput").ap())
    args.append(nc.dram_tensor("out_y", (1, SEQ, D), FP32, kind="ExternalOutput").ap())
    build(nc, *args)
    r = run_bass_kernel_spmd(nc, [arrays], core_ids=[0])
    return r.results[0]["out_y"]
```
